# Optimizing a Trainium2 kernel written in Bass

```python
import math
import jax, jax.numpy as jnp
from jax import lax
import numpy as np

D_MODEL = 1024
BATCH = 1
SEQ = 256
DEPTH = 1

GRID_W = 64
CTX_LEN = 256

D_MIX = D_MODEL
D_FOURIER = D_MIX // 4
FOURIER_GROUPS = 4
D_FG = D_FOURIER // FOURIER_GROUPS
HEAD_DIM = 64
NA_HEADS = (D_MIX // 2) // HEAD_DIM
D_NA = NA_HEADS * HEAD_DIM
D_CONV = D_MIX - D_FOURIER - D_NA
CONV_WIDTH = 3
D_IN_PROJ = D_FOURIER + 3 * D_NA + 3 * D_CONV

NA_KH = 8
NA_KW = 16
NA_QB = 16
NA_KB = 32

N_GROUPS = 4
EXPERTS_PER_GROUP = 8
N_EXPERTS = N_GROUPS * EXPERTS_PER_GROUP
TOP_K = 2
D_EXPERT = 512

EPS = 1e-6
NEG_INF = -1e30


def rms_norm(x, gain):
    xf = x.astype(jnp.float32)
    y = xf * lax.rsqrt(jnp.mean(xf * xf, axis=-1, keepdims=True) + EPS)
    return (y * gain.astype(jnp.float32)).astype(x.dtype)

def split_in(u):
    o = [D_FOURIER, D_FOURIER + D_NA, D_FOURIER + 2 * D_NA, D_FOURIER + 3 * D_NA,
         D_FOURIER + 3 * D_NA + D_CONV, D_FOURIER + 3 * D_NA + 2 * D_CONV]
    f, q, k, v, gb, gc, h = jnp.split(u, o, axis=-1)
    heads = lambda t: t.reshape(*t.shape[:-1], NA_HEADS, HEAD_DIM)
    return f, heads(q), heads(k), heads(v), gb, gc, h

def fourier_mix(f):
    b, n, _ = f.shape
    fg = f.reshape(b, n, FOURIER_GROUPS, D_FG).astype(jnp.float32)
    out = jnp.fft.fft2(fg, axes=(1, 3), norm="ortho").real
    return out.reshape(b, n, D_FOURIER).astype(f.dtype)

def short_conv(h, w):
    return lax.conv_general_dilated(
        h, w[:, None, :].astype(h.dtype), window_strides=(1,), padding=((1, 1),),
        dimension_numbers=("NWC", "WIO", "NWC"), feature_group_count=h.shape[-1])

def na_latent(q, k, v, kc, vc, rpb):
    b, n, h, dh = q.shape
    rows = n // GRID_W
    kh = min(NA_KH, rows)
    ncb = GRID_W // NA_QB
    r = jnp.arange(rows)
    row_start = jnp.clip(r - kh // 2, 0, rows - kh)
    row_idx = row_start[:, None] + jnp.arange(kh)[None, :]
    cols = jnp.arange(GRID_W)
    col_start = jnp.clip(cols - NA_KW // 2, 0, GRID_W - NA_KW)
    band_start = jnp.clip(col_start[::NA_QB], 0, GRID_W - NA_KB)
    band_idx = band_start[:, None] + jnp.arange(NA_KB)[None, :]
    qcol = cols.reshape(ncb, NA_QB)
    qcs = col_start.reshape(ncb, NA_QB)
    kcol = band_idx[:, None, :]
    valid = (kcol >= qcs[..., None]) & (kcol < qcs[..., None] + NA_KW)
    roff = row_idx - r[:, None] + (NA_KH - 1)
    coff = jnp.clip(kcol - qcol[..., None] + (NA_KW - 1), 0, 2 * NA_KW - 2)
    bias = rpb[:, roff[:, None, None, :, None], coff[None, :, :, None, :]]

    qg = q.reshape(b, rows, ncb, NA_QB, h, dh)
    kg = k.reshape(b, rows, GRID_W, h, dh)
    vg = v.reshape(b, rows, GRID_W, h, dh)
    ri = row_idx[:, :, None, None]
    ci = band_idx[None, None]
    kb = kg[:, ri, ci]
    vb = vg[:, ri, ci]

    s_loc = jnp.einsum("brcqhd,brkcjhd->bhrcqkj", qg, kb).astype(jnp.float32)
    s_loc = jnp.where(valid[:, :, None, :], s_loc + bias.astype(jnp.float32), NEG_INF)
    s_ctx = jnp.einsum("brcqhd,blhd->bhrcql", qg, kc).astype(jnp.float32)
    kj = kh * NA_KB
    s = jnp.concatenate([s_loc.reshape(*s_loc.shape[:5], kj), s_ctx], axis=-1)
    p = jax.nn.softmax(s, axis=-1).astype(v.dtype)
    p_loc = p[..., :kj].reshape(s_loc.shape)
    p_ctx = p[..., kj:]
    o = (jnp.einsum("bhrcqkj,brkcjhd->brcqhd", p_loc, vb)
         + jnp.einsum("bhrcql,blhd->brcqhd", p_ctx, vc))
    return o.reshape(b, n, h * dh)

def na_context(qc, kc, vc):
    s = jnp.einsum("blhd,bmhd->bhlm", qc, kc).astype(jnp.float32)
    p = jax.nn.softmax(s, axis=-1).astype(vc.dtype)
    o = jnp.einsum("bhlm,bmhd->blhd", p, vc)
    return o.reshape(*o.shape[:2], D_NA)

def mix_out(f, attn, conv, w_fourier, w_out):
    return jnp.concatenate([fourier_mix(f) @ w_fourier, attn, conv], axis=-1) @ w_out

def hier_moe(t, w_rg, b_rg, w_re, b_re, w_gate, w_up, w_down):
    n_tok = t.shape[0]
    g_logits = (t @ w_rg + b_rg).astype(jnp.float32)
    g_prob = jax.nn.softmax(g_logits, axis=-1)
    g_idx = jnp.argmax(g_logits, axis=-1)
    g_w = jnp.take_along_axis(g_prob, g_idx[:, None], axis=-1)
    e_logits = (t @ w_re + b_re).astype(jnp.float32).reshape(n_tok, N_GROUPS, EXPERTS_PER_GROUP)
    e_sel = jnp.take_along_axis(e_logits, g_idx[:, None, None], axis=1)[:, 0]
    top_v, top_i = lax.top_k(e_sel, TOP_K)
    pair_w = g_w * jax.nn.softmax(top_v, axis=-1)
    expert_id = g_idx[:, None] * EXPERTS_PER_GROUP + top_i
    combine = jnp.sum(jax.nn.one_hot(expert_id, N_EXPERTS, dtype=jnp.float32)
                      * pair_w[..., None], axis=1).astype(t.dtype)
    y = jnp.zeros_like(t)
    for e in range(N_EXPERTS):
        he = jax.nn.silu(t @ w_gate[e]) * (t @ w_up[e])
        y = y + combine[:, e:e + 1] * (he @ w_down[e])
    return y

def trunk_layer(x, xc, mod_x, mod_c, norm1, norm2, w_in, w_fourier, w_conv, rpb, w_out,
                w_rg, b_rg, w_re, b_re, w_gate, w_up, w_down, last):
    b, n, d = x.shape
    l = xc.shape[1]
    sh1, sc1, g1, sh2, sc2, g2 = jnp.split(mod_x[:, None, :], 6, axis=-1)
    csh1, csc1, cg1, csh2, csc2, cg2 = jnp.split(mod_c, 6, axis=-1)
    scale = 1.0 / math.sqrt(HEAD_DIM)

    ux = (rms_norm(x, norm1) * (1 + sc1) + sh1) @ w_in
    uc = (rms_norm(xc, norm1) * (1 + csc1) + csh1) @ w_in
    fx, qx, kx, vx, bx, cx, hx = split_in(ux)
    fc, qc, kc, vc, bc, cc, hc = split_in(uc)
    attn_x = na_latent(qx * scale, kx, vx, kc, vc, rpb)
    conv_x = bx * short_conv(cx * hx, w_conv)
    x = x + g1 * mix_out(fx, attn_x, conv_x, w_fourier, w_out)
    if not last:
        attn_c = na_context(qc * scale, kc, vc)
        conv_c = bc * short_conv(cc * hc, w_conv)
        xc = xc + cg1 * mix_out(fc, attn_c, conv_c, w_fourier, w_out)

    hx2 = rms_norm(x, norm2) * (1 + sc2) + sh2
    if last:
        y = hier_moe(hx2.reshape(-1, d), w_rg, b_rg, w_re, b_re, w_gate, w_up, w_down)
        x = x + g2 * y.reshape(b, n, d)
    else:
        hc2 = rms_norm(xc, norm2) * (1 + csc2) + csh2
        tok = jnp.concatenate([hx2.reshape(-1, d), hc2.reshape(-1, d)], axis=0)
        y = hier_moe(tok, w_rg, b_rg, w_re, b_re, w_gate, w_up, w_down)
        x = x + g2 * y[:b * n].reshape(b, n, d)
        xc = xc + cg2 * y[b * n:].reshape(b, l, d)
    return x, xc

def first_inputs(seed: int = 0) -> dict:
    key = jax.random.key(seed)
    ks = jax.random.split(key, 24)
    d = D_MODEL
    nrm = lambda k, shape, s: jax.random.normal(k, shape, jnp.float32) * s
    return {
        "x": nrm(ks[0], (BATCH, SEQ, d), 1.0),
        "c": nrm(ks[1], (BATCH, d), 1.0),
        "ctx": nrm(ks[2], (BATCH, CTX_LEN, d), 1.0),
        "c_ctx": nrm(ks[3], (d,), 1.0),
        "w_ada": nrm(ks[4], (DEPTH, d, 6 * d), 0.5 * d ** -0.5),
        "b_ada": nrm(ks[5], (DEPTH, 6 * d), 0.02),
        "norm1": 1.0 + nrm(ks[6], (DEPTH, d), 0.05),
        "norm2": 1.0 + nrm(ks[7], (DEPTH, d), 0.05),
        "w_in": nrm(ks[8], (DEPTH, d, D_IN_PROJ), d ** -0.5),
        "w_fourier": nrm(ks[9], (DEPTH, D_FOURIER, D_FOURIER), D_FOURIER ** -0.5),
        "w_conv": nrm(ks[10], (DEPTH, CONV_WIDTH, D_CONV), CONV_WIDTH ** -0.5),
        "rpb": nrm(ks[11], (DEPTH, NA_HEADS, 2 * NA_KH - 1, 2 * NA_KW - 1), 0.1),
        "w_out": nrm(ks[12], (DEPTH, D_MIX, d), D_MIX ** -0.5),
        "w_rg": nrm(ks[13], (DEPTH, d, N_GROUPS), d ** -0.5),
        "b_rg": nrm(ks[14], (DEPTH, N_GROUPS), 0.01),
        "w_re": nrm(ks[15], (DEPTH, d, N_EXPERTS), d ** -0.5),
        "b_re": nrm(ks[16], (DEPTH, N_EXPERTS), 0.01),
        "w_gate": nrm(ks[17], (DEPTH, N_EXPERTS, d, D_EXPERT), d ** -0.5),
        "w_up": nrm(ks[18], (DEPTH, N_EXPERTS, d, D_EXPERT), d ** -0.5),
        "w_down": nrm(ks[19], (DEPTH, N_EXPERTS, D_EXPERT, d), D_EXPERT ** -0.5),
        "norm_final": 1.0 + nrm(ks[20], (d,), 0.05),
    }

def first_block(x, c, ctx, c_ctx, w_ada, b_ada, norm1, norm2, w_in, w_fourier, w_conv, rpb,
              w_out, w_rg, b_rg, w_re, b_re, w_gate, w_up, w_down, norm_final):
    xc = ctx
    sc = jax.nn.silu(c)
    scc = jax.nn.silu(c_ctx)
    for li in range(DEPTH):
        mod_x = sc @ w_ada[li] + b_ada[li]
        mod_c = scc @ w_ada[li] + b_ada[li]
        x, xc = trunk_layer(x, xc, mod_x, mod_c, norm1[li], norm2[li], w_in[li], w_fourier[li],
                            w_conv[li], rpb[li], w_out[li], w_rg[li], b_rg[li], w_re[li],
                            b_re[li], w_gate[li], w_up[li], w_down[li], li == DEPTH - 1)
    return rms_norm(x, norm_final)


DEPTH_2 = 2

N_MIXERS = 4
D_FF = 2816
NORM_EPS = 1e-6
GN_EPS = 1e-5
ROPE_THETA = 10000.0
Q_BLOCK = 128
NEG_INF_2 = -1e30

A_HEADS = 16
A_HEAD_DIM = 64
A_PATTERNS = ((128, 1), (512, 4), (2048, 16))
A_GROUPS = len(A_PATTERNS)
A_WIDTH = A_GROUPS * A_HEADS * A_HEAD_DIM

B_HEADS = 16
B_NOPE = 64
B_ROPE = 32
B_QK = B_NOPE + B_ROPE
B_VDIM = 64
B_Q_RANK = 384
B_KV_RANK = 256

C_HEADS = 8
C_KDIM = 128
C_VDIM = 256
C_CHUNK = 128

D_WIDTH = 1024
D_BLOCKS = 4
D_BLOCK = D_WIDTH // D_BLOCKS
D_CONV_2 = 4
LRU_C = 8.0


f32 = jnp.float32

def rmsnorm(x, g):
    xf = x.astype(f32)
    y = xf * lax.rsqrt(jnp.mean(xf * xf, axis=-1, keepdims=True) + NORM_EPS)
    return (y * g.astype(f32)).astype(x.dtype)

def rope(x, pos):
    d = x.shape[-1]
    half = d // 2
    inv = ROPE_THETA ** (-jnp.arange(half, dtype=f32) * 2.0 / d)
    ang = pos.astype(f32)[:, :, None, None] * inv
    cos, sin = jnp.cos(ang), jnp.sin(ang)
    xf = x.astype(f32)
    x1, x2 = xf[..., :half], xf[..., half:]
    return jnp.concatenate([x1 * cos - x2 * sin, x2 * cos + x1 * sin], axis=-1).astype(x.dtype)

def swiglu(x, w_in, w_out):
    gate, up = jnp.split(x @ w_in, 2, axis=-1)
    return (jax.nn.silu(gate) * up) @ w_out

def _dilated_band(q, k, v, window, dilation):
    B, S, H, dh = q.shape
    W = window // dilation
    L = S // dilation
    nb = -(-L // W)
    Lp = nb * W

    def by_residue(t):
        t = t.reshape(B, L, dilation, H, t.shape[-1]).transpose(0, 2, 3, 1, 4)
        return jnp.pad(t, ((0, 0), (0, 0), (0, 0), (0, Lp - L), (0, 0)))

    def band(t):
        t = jnp.pad(t, ((0, 0), (0, 0), (0, 0), (W, 0), (0, 0)))
        t = t.reshape(B, dilation, H, nb + 1, W, t.shape[-1])
        return jnp.concatenate([t[:, :, :, :-1], t[:, :, :, 1:]], axis=4)

    qb = by_residue(q).reshape(B, dilation, H, nb, W, dh)
    kb = band(by_residue(k))
    vb = band(by_residue(v))
    s = jnp.einsum('brhnqd,brhnkd->brhnqk', qb, kb).astype(f32) * (dh ** -0.5)
    u = jnp.arange(W)[None, :, None]
    c = jnp.arange(2 * W)[None, None, :]
    blk = jnp.arange(nb)[:, None, None]
    valid = (c >= u) & (c <= u + W) & (blk * W - W + c >= 0)
    s = jnp.where(valid, s, NEG_INF_2)
    lse = jax.nn.logsumexp(s, axis=-1)
    p = jnp.exp(s - lse[..., None]).astype(v.dtype)
    o = jnp.einsum('brhnqk,brhnkd->brhnqd', p, vb)
    o = o.reshape(B, dilation, H, Lp, dh)[:, :, :, :L].transpose(0, 3, 1, 2, 4).reshape(B, S, H, dh)
    lse = lse.reshape(B, dilation, H, Lp)[..., :L].transpose(0, 3, 1, 2).reshape(B, S, H)
    return o, lse

def dilated_window_attention(x, pos, w_in, q_gain, k_gain, w_out):
    B, S, _ = x.shape
    q, k, v = jnp.split(x @ w_in, 3, axis=-1)
    shp = (B, S, A_GROUPS * A_HEADS, A_HEAD_DIM)
    q = rope(rmsnorm(q.reshape(shp), q_gain), pos)
    k = rope(rmsnorm(k.reshape(shp), k_gain), pos)
    v = v.reshape(shp)
    outs, lses = [], []
    for g, (window, dilation) in enumerate(A_PATTERNS):
        sl = slice(g * A_HEADS, (g + 1) * A_HEADS)
        o, lse = _dilated_band(q[:, :, sl], k[:, :, sl], v[:, :, sl], window, dilation)
        outs.append(o)
        lses.append(lse)
    wts = jax.nn.softmax(jnp.stack(lses, axis=0), axis=0).astype(x.dtype)
    o = jnp.einsum('gbsh,gbshd->bshd', wts, jnp.stack(outs, axis=0))
    return o.reshape(B, S, A_HEADS * A_HEAD_DIM) @ w_out

def _causal_attention(q, k, v):
    B, S, H, dq = q.shape
    nb = S // Q_BLOCK
    scale = dq ** -0.5
    qb = q.reshape(B, nb, Q_BLOCK, H, dq).transpose(1, 0, 2, 3, 4)
    kpos = jnp.arange(S)

    def block(args):
        qblk, b = args
        s = jnp.einsum('bqhd,bkhd->bhqk', qblk, k).astype(f32) * scale
        qpos = b * Q_BLOCK + jnp.arange(Q_BLOCK)
        s = jnp.where(kpos[None, :] <= qpos[:, None], s, NEG_INF_2)
        p = jax.nn.softmax(s, axis=-1).astype(v.dtype)
        return jnp.einsum('bhqk,bkhd->bqhd', p, v)

    o = lax.map(block, (qb, jnp.arange(nb)))
    return o.transpose(1, 0, 2, 3, 4).reshape(B, S, H, v.shape[-1])

def latent_attention(x, pos, w_in, q_a_gain, w_q_up, kv_a_gain, w_kv_up, q_gain, k_gain, w_out):
    B, S, _ = x.shape
    h = x @ w_in
    c_q = h[..., :B_Q_RANK]
    c_kv = h[..., B_Q_RANK:B_Q_RANK + B_KV_RANK]
    k_rope = h[..., B_Q_RANK + B_KV_RANK:]
    q = (rmsnorm(c_q, q_a_gain) @ w_q_up).reshape(B, S, B_HEADS, B_QK)
    kv = (rmsnorm(c_kv, kv_a_gain) @ w_kv_up).reshape(B, S, B_HEADS, B_NOPE + B_VDIM)
    k_nope, v = kv[..., :B_NOPE], kv[..., B_NOPE:]
    k = jnp.concatenate([k_nope, jnp.broadcast_to(k_rope[:, :, None, :], (B, S, B_HEADS, B_ROPE))], axis=-1)
    q = rmsnorm(q, q_gain)
    k = rmsnorm(k, k_gain)
    q = jnp.concatenate([q[..., :B_NOPE], rope(q[..., B_NOPE:], pos)], axis=-1)
    k = jnp.concatenate([k[..., :B_NOPE], rope(k[..., B_NOPE:], pos)], axis=-1)
    o = _causal_attention(q, k, v)
    return o.reshape(B, S, B_HEADS * B_VDIM) @ w_out

def retention(x, pos, w_in, w_out):
    B, S, _ = x.shape
    h = x @ w_in
    qk_w = C_HEADS * C_KDIM
    v_w = C_HEADS * C_VDIM
    q = h[..., :qk_w].reshape(B, S, C_HEADS, C_KDIM)
    k = h[..., qk_w:2 * qk_w].reshape(B, S, C_HEADS, C_KDIM)
    v = h[..., 2 * qk_w:2 * qk_w + v_w].reshape(B, S, C_HEADS, C_VDIM)
    g = h[..., 2 * qk_w + v_w:]
    q = rope(q, pos).astype(f32)
    k = rope(k, pos).astype(f32) * (C_KDIM ** -0.5)
    v = v.astype(f32)
    log_g = jnp.log(1.0 - 2.0 ** (-5.0 - jnp.arange(C_HEADS, dtype=f32)))
    idx = jnp.arange(C_CHUNK, dtype=f32)
    diff = idx[:, None] - idx[None, :]
    causal = diff >= 0
    decay = jnp.where(causal[None], jnp.exp(jnp.where(causal, diff, 0.0)[None] * log_g[:, None, None]), 0.0)
    xi = jnp.exp((idx + 1.0)[None, :] * log_g[:, None])
    zeta = jnp.exp((C_CHUNK - 1.0 - idx)[None, :] * log_g[:, None])
    chunk_decay = jnp.exp(C_CHUNK * log_g)
    nc = S // C_CHUNK

    def to_chunks(t):
        return t.reshape(B, nc, C_CHUNK, C_HEADS, t.shape[-1]).transpose(1, 0, 3, 2, 4)

    def step(R, inp):
        qc, kc, vc = inp
        s = jnp.einsum('bhid,bhjd->bhij', qc, kc) * decay[None]
        inner = jnp.einsum('bhij,bhjv->bhiv', s, vc)
        cross = jnp.einsum('bhid,bhdv->bhiv', qc, R) * xi[None, :, :, None]
        R = chunk_decay[None, :, None, None] * R + jnp.einsum('bhjd,bhjv->bhdv', kc * zeta[None, :, :, None], vc)
        return R, inner + cross

    R0 = jnp.zeros((B, C_HEADS, C_KDIM, C_VDIM), f32)
    _, y = lax.scan(step, R0, (to_chunks(q), to_chunks(k), to_chunks(v)))
    y = y.transpose(1, 0, 3, 2, 4).reshape(B, S, C_HEADS, C_VDIM)
    mu = jnp.mean(y, axis=-1, keepdims=True)
    var = jnp.mean(jnp.square(y - mu), axis=-1, keepdims=True)
    y = ((y - mu) * lax.rsqrt(var + GN_EPS)).astype(x.dtype).reshape(B, S, v_w)
    return (jax.nn.silu(g) * y) @ w_out

def _linear_combine(c1, c2):
    a1, b1 = c1
    a2, b2 = c2
    return a1 * a2, a2 * b1 + b2

def recurrent_block(x, w_in, conv_w, conv_b, w_rg, b_rg, w_ig, b_ig, lru_param, w_out):
    B, S, _ = x.shape
    gate, u = jnp.split(x @ w_in, 2, axis=-1)
    u = lax.conv_general_dilated(u, conv_w[:, None, :], window_strides=(1,),
                                 padding=[(D_CONV_2 - 1, 0)],
                                 dimension_numbers=('NWC', 'WIO', 'NWC'),
                                 feature_group_count=D_WIDTH) + conv_b
    ub = u.reshape(B, S, D_BLOCKS, D_BLOCK)
    r = jax.nn.sigmoid(jnp.einsum('bsnc,ncd->bsnd', ub, w_rg).reshape(B, S, D_WIDTH) + b_rg)
    ig = jax.nn.sigmoid(jnp.einsum('bsnc,ncd->bsnd', ub, w_ig).reshape(B, S, D_WIDTH) + b_ig)
    log_a = -LRU_C * r.astype(f32) * jax.nn.softplus(-lru_param.astype(f32))
    a = jnp.exp(log_a)
    b = jnp.sqrt(jnp.maximum(-jnp.expm1(2.0 * log_a), 0.0)) * (ig * u).astype(f32)
    _, hs = lax.associative_scan(_linear_combine, (a, b), axis=1)
    return (jax.nn.gelu(gate) * hs.astype(x.dtype)) @ w_out

def _layers_of(m):
    return len(range(m, DEPTH_2, N_MIXERS))

def second_inputs(seed: int = 0) -> dict:
    key = jax.random.key(seed)
    kit = iter(jax.random.split(key, 40))

    def w(shape, fan_in):
        return jax.random.normal(next(kit), shape, f32) * (fan_in ** -0.5)

    def gain(shape):
        return 1.0 + 0.05 * jax.random.normal(next(kit), shape, f32)

    def bias(shape):
        return 0.01 * jax.random.normal(next(kit), shape, f32)

    nA, nB, nC, nD = (_layers_of(m) for m in range(N_MIXERS))
    x = jax.random.normal(next(kit), (BATCH, SEQ, D_MODEL), f32)
    offsets = jax.random.randint(next(kit), (BATCH, 1), 0, 1024)
    positions = (offsets + jnp.arange(SEQ)[None, :]).astype(jnp.int32)
    u = jax.random.uniform(next(kit), (nD, D_WIDTH), f32, minval=0.9, maxval=0.999)
    a0 = u ** (1.0 / LRU_C)
    lru_param = jnp.log(a0) - jnp.log1p(-a0)
    return {
        'x': x,
        'positions': positions,
        'norm_gains': gain((DEPTH_2, 3, D_MODEL)),
        'ffn_w_in': w((DEPTH_2, 2, D_MODEL, 2 * D_FF), D_MODEL),
        'ffn_w_out': w((DEPTH_2, 2, D_FF, D_MODEL), D_FF),
        'a_w_in': w((nA, D_MODEL, 3 * A_WIDTH), D_MODEL),
        'a_q_gain': gain((nA, A_HEAD_DIM)),
        'a_k_gain': gain((nA, A_HEAD_DIM)),
        'a_w_out': w((nA, A_HEADS * A_HEAD_DIM, D_MODEL), A_HEADS * A_HEAD_DIM),
        'b_w_in': w((nB, D_MODEL, B_Q_RANK + B_KV_RANK + B_ROPE), D_MODEL),
        'b_q_a_gain': gain((nB, B_Q_RANK)),
        'b_w_q_up': w((nB, B_Q_RANK, B_HEADS * B_QK), B_Q_RANK),
        'b_kv_a_gain': gain((nB, B_KV_RANK)),
        'b_w_kv_up': w((nB, B_KV_RANK, B_HEADS * (B_NOPE + B_VDIM)), B_KV_RANK),
        'b_q_gain': gain((nB, B_QK)),
        'b_k_gain': gain((nB, B_QK)),
        'b_w_out': w((nB, B_HEADS * B_VDIM, D_MODEL), B_HEADS * B_VDIM),
        'c_w_in': w((nC, D_MODEL, 2 * C_HEADS * C_KDIM + 2 * C_HEADS * C_VDIM), D_MODEL),
        'c_w_out': w((nC, C_HEADS * C_VDIM, D_MODEL), C_HEADS * C_VDIM),
        'd_w_in': w((nD, D_MODEL, 2 * D_WIDTH), D_MODEL),
        'd_conv_w': w((nD, D_CONV_2, D_WIDTH), D_CONV_2),
        'd_conv_b': bias((nD, D_WIDTH)),
        'd_w_rg': w((nD, D_BLOCKS, D_BLOCK, D_BLOCK), D_BLOCK),
        'd_b_rg': bias((nD, D_WIDTH)),
        'd_w_ig': w((nD, D_BLOCKS, D_BLOCK, D_BLOCK), D_BLOCK),
        'd_b_ig': bias((nD, D_WIDTH)),
        'd_lru_param': lru_param,
        'd_w_out': w((nD, D_WIDTH, D_MODEL), D_WIDTH),
    }

def second_block(x, positions, norm_gains, ffn_w_in, ffn_w_out,
              a_w_in, a_q_gain, a_k_gain, a_w_out,
              b_w_in, b_q_a_gain, b_w_q_up, b_kv_a_gain, b_w_kv_up, b_q_gain, b_k_gain, b_w_out,
              c_w_in, c_w_out,
              d_w_in, d_conv_w, d_conv_b, d_w_rg, d_b_rg, d_w_ig, d_b_ig, d_lru_param, d_w_out):
    for i in range(DEPTH_2):
        m, j = i % N_MIXERS, i // N_MIXERS
        x = x + 0.5 * swiglu(rmsnorm(x, norm_gains[i, 0]), ffn_w_in[i, 0], ffn_w_out[i, 0])
        h = rmsnorm(x, norm_gains[i, 1])
        if m == 0:
            y = dilated_window_attention(h, positions, a_w_in[j], a_q_gain[j], a_k_gain[j], a_w_out[j])
        elif m == 1:
            y = latent_attention(h, positions, b_w_in[j], b_q_a_gain[j], b_w_q_up[j], b_kv_a_gain[j],
                                 b_w_kv_up[j], b_q_gain[j], b_k_gain[j], b_w_out[j])
        elif m == 2:
            y = retention(h, positions, c_w_in[j], c_w_out[j])
        else:
            y = recurrent_block(h, d_w_in[j], d_conv_w[j], d_conv_b[j], d_w_rg[j], d_b_rg[j],
                                d_w_ig[j], d_b_ig[j], d_lru_param[j], d_w_out[j])
        x = x + y
        x = x + 0.5 * swiglu(rmsnorm(x, norm_gains[i, 2]), ffn_w_in[i, 1], ffn_w_out[i, 1])
    return x


def setup_inputs(seed=0):
    out = dict(first_inputs(seed))
    for name, value in second_inputs(seed + 1).items():
        if name != "x":
            out[name + "_2"] = value
    return out


def reference(
    x, c, ctx, c_ctx, w_ada, b_ada, norm1, norm2, w_in, w_fourier, w_conv, rpb, w_out, w_rg,
    b_rg, w_re, b_re, w_gate, w_up, w_down, norm_final, positions_2, norm_gains_2, ffn_w_in_2,
    ffn_w_out_2, a_w_in_2, a_q_gain_2, a_k_gain_2, a_w_out_2, b_w_in_2, b_q_a_gain_2,
    b_w_q_up_2, b_kv_a_gain_2, b_w_kv_up_2, b_q_gain_2, b_k_gain_2, b_w_out_2, c_w_in_2,
    c_w_out_2, d_w_in_2, d_conv_w_2, d_conv_b_2, d_w_rg_2, d_b_rg_2, d_w_ig_2, d_b_ig_2,
    d_lru_param_2, d_w_out_2,
):
    x = first_block(
        x, c, ctx, c_ctx, w_ada, b_ada, norm1, norm2, w_in, w_fourier, w_conv, rpb, w_out, w_rg,
        b_rg, w_re, b_re, w_gate, w_up, w_down, norm_final,
    )
    return second_block(
        x, positions_2, norm_gains_2, ffn_w_in_2, ffn_w_out_2, a_w_in_2, a_q_gain_2, a_k_gain_2,
        a_w_out_2, b_w_in_2, b_q_a_gain_2, b_w_q_up_2, b_kv_a_gain_2, b_w_kv_up_2, b_q_gain_2,
        b_k_gain_2, b_w_out_2, c_w_in_2, c_w_out_2, d_w_in_2, d_conv_w_2, d_conv_b_2, d_w_rg_2,
        d_b_rg_2, d_w_ig_2, d_b_ig_2, d_lru_param_2, d_w_out_2,
    )


_drawn_inputs = setup_inputs


def setup_inputs(seed=0):
    import zlib

    import numpy as np

    out = dict(_drawn_inputs(seed))
    spreads = {}
    factors = {'rpb': 8.0,
     'b_rg': 8.0,
     'b_re': 5.021,
     'a_q_gain_2': 6.367,
     'a_k_gain_2': 6.363,
     'b_q_a_gain_2': 7.284,
     'b_kv_a_gain_2': 4.251,
     'b_q_gain_2': 8.0,
     'b_k_gain_2': 7.244}
    for name, (base, spread) in spreads.items():
        noise = np.random.default_rng([zlib.crc32(name.encode()), seed]).standard_normal(out[name].shape)
        drawn = base * np.exp(spread * noise) if base else spread * noise
        out[name] = __import__('jax').numpy.asarray(drawn.astype(out[name].dtype))
    for name, factor in factors.items():
        out[name] = (out[name] * factor).astype(out[name].dtype)
    return out
```

```python
import math
from contextlib import ExitStack

import numpy as np
import concourse.bass as bass
from concourse import mybir

ALU = mybir.AluOpType
ACT = mybir.ActivationFunctionType
AX = mybir.AxisListType
f32 = mybir.dt.float32
f32r = mybir.dt.float32r
i32 = mybir.dt.int32

D = 1024
KT = D // 128
T = 256
NT = T // 128
EPS = 1e-6
FF = 2816
FF_TWICE = FF // 256
HEADS = 16
PAIRS = HEADS // 2
GROUPS = 3
AD = 64
AW = GROUPS * 128
B_NOPE, B_ROPE, B_QK, B_V = 64, 32, 96, 64
B_QR, B_KVR = 384, 256
B_IN = B_QR + B_KVR + B_ROPE
SLOT = 3072
MIX_LOADS = 5
MASK_A = [0, 384]
MASK_B = [1152, 1280]
N_MASK = 1536
GC_N1, GC_N2, GC_BA, GC_CONV = 48, 56, 64, 69
N_GC = 75
FAR = -1e30
SR = 2048
R_SLOTS = 5
EXPERTS, N_GROUPS = 32, 4
EPG = EXPERTS // N_GROUPS
CAP = 64
PAIR_STEPS = EXPERTS // 2
ROUNDS = T // CAP
KEYS = ROUNDS * EXPERTS
FH = D // 4


class Names:
    pass


def at_least(eng, sem, value):
    if not isinstance(value, int) or value > 0:
        eng.wait_ge(sem, value)


class Chain:

    def __init__(self, eng, sem, base=0):
        self.eng, self.sem, self.base, self.n = eng, sem, base, 0

    def add(self, ins):
        ins.then_inc(self.sem, 1)
        self.n += 1

    def wait(self):
        self.eng.wait_ge(self.sem, self.base + self.n)


def norm_and_transpose(nc, M, n, g0):
    X, XN, SS, RS, GC, XH, XL, TRB = M.X, M.XN, M.SS, M.RS, M.GC, M.XH, M.XL, M.TRB
    a, p, v, e = nc.scalar, nc.gpsimd, nc.vector, nc.tensor

    def act():
        a.wait_ge(M.x_ready, 4 * n + 4)
        for t in range(NT):
            at_least(a, M.squared, NT * n + t)
            a.activation(M.JUNK[:], X[:, t], ACT.Square, accum_out=SS[:, t:t + 1]).then_inc(M.squared, 1)
        for k in range(KT):
            a.wait_ge(M.turned, 4 * n + k // 2 + 1)
            a.activation(XH[:, k], TRB[k // 2 % 2][:, T * (k % 2):T * (k % 2) + T], ACT.Copy,
                         scale=GC[:, g0 + k:g0 + k + 1]).then_inc(M.xh_done, 1)

    def pool():
        p.wait_ge(M.squared, NT * (n + 1))
        p.tensor_scalar(RS[:], SS[:], 1 / D, EPS, ALU.mult, ALU.add).then_inc(M.rstd, 1)
        p.wait_ge(M.rstd, 2 * n + 1)
        p.tensor_tensor(RS[:], RS[:], M.HF[:, 0:NT], ALU.pow).then_inc(M.rstd, 1)

    def dve():
        v.wait_ge(M.rstd, 2 * n + 2)
        for t in range(NT):
            v.tensor_scalar(XN[:, t], X[:, t], RS[:, t:t + 1], None, ALU.mult).then_inc(M.xn_done, 1)
        for k in range(KT):
            v.wait_ge(M.xh_done, KT * n + 2 * (k // 2) + 2)
            v.scalar_tensor_tensor(XL[:, k], TRB[k // 2 % 2][:, T * (k % 2):T * (k % 2) + T],
                                   GC[:, g0 + k:g0 + k + 1], XH[:, k].bitcast(f32),
                                   ALU.mult, ALU.subtract).then_inc(M.xl_done, 1)

    def pe():
        e.wait_ge(M.xn_done, NT * (n + 1))
        for b in range(4):
            at_least(e, M.xl_done, KT * n + 2 * (b - 1))
            for kk in range(2):
                for t in range(NT):
                    k = 2 * b + kk
                    m = e.transpose(TRB[b % 2][:, T * kk + 128 * t:T * kk + 128 * t + 128],
                                    XN[:, t, 128 * k:128 * k + 128], M.ID[:])
            m.then_inc(M.turned, 1)
        e.wait_ge(M.xl_done, KT * (n + 1))

    return act, pool, dve, pe


def ffn(nc, M, f, w_in, w_out, raw_free):
    XH, XL, X, PS, s = M.XH, M.XL, M.X, M.PS, M.ffn
    Y = PS[:, 0:4, :]
    GU = [PS[:, 4, :], PS[:, 5, :]]
    w_in_v = w_in.rearrange("(k p) n -> p k n", p=128)
    w_out_v = w_out.rearrange("(c p) n -> c p n", p=128)
    u0 = FF_TWICE * f
    a, v, e, sp = nc.scalar, nc.vector, nc.tensor, nc.sync

    def gu(buf, j):
        return buf[:, j, 0:2048].rearrange("p (q k n) -> p q k n", q=2, k=KT)

    def dn(buf, j):
        return buf[:, j, 2048:3072]

    def sync():
        for j in range(2):
            raw_free(sp, j)
        with sp.Fori(0, FF_TWICE) as i:
            for j in range(2):
                sp.wait_ge(s.gu_lo[j], i + (u0 + 1))
                for q in range(2):
                    sp.dma_start(gu(M.RAW, j)[:, q], w_in_v[:, :, bass.ds(i * 256 + (j * 128 + q * FF), 128)]
                                 ).then_inc(s.gu_in[j], 16)
                sp.wait_ge(s.dn_lo[j], i + (u0 + 1))
                sp.dma_start(dn(M.RAW, j), w_out_v[bass.ds(i * 2 + j, 1)].rearrange("a p n -> p (a n)")
                             ).then_inc(s.dn_in[j], 16)

    def act():
        def high_parts(j, i):
            a.wait_ge(s.gu_in[j], i * 32 + (32 * u0 + 32))
            a.wait_ge(s.gu_used[j], i + (u0 + 1))
            a.activation(M.HI[:, j, 0:2048], M.RAW[:, j, 0:2048], ACT.Copy).then_inc(s.gu_hi[j], 1)
            a.wait_ge(s.dn_in[j], i * 16 + (16 * u0 + 16))
            a.wait_ge(s.dn_used[j], i + (u0 + 1))
            a.activation(dn(M.HI, j), dn(M.RAW, j), ACT.Copy).then_inc(s.dn_hi[j], 1)

        def silu(j, i):
            a.wait_ge(s.gu_used[j], i + (u0 + 2))
            a.wait_ge(s.h_done[j], i + (u0 + 1))
            a.activation(M.SG[:, j], GU[j][:, 0:T], ACT.Silu).then_inc(s.silu[j], 1)
            a.wait_ge(s.h_done[j], i + (u0 + 2))
            a.activation(M.HH[:, j], M.H[:, j], ACT.Copy).then_inc(s.hh_done[j], 1)

        high_parts(0, 0)
        high_parts(1, 0)
        silu(0, 0)
        with a.Fori(1, FF_TWICE) as i:
            high_parts(0, i)
            silu(1, i - 1)
            high_parts(1, i)
            silu(0, i)
        silu(1, FF_TWICE - 1)

    def dve():
        if f == 0:
            for j in range(2):
                v.sem_inc(s.h_done[j], 1)
                v.sem_inc(s.gu_lo[j], 1)
                v.sem_inc(s.dn_lo[j], 1)

        def low_parts(j, i):
            v.wait_ge(s.gu_hi[j], i + (u0 + 1))
            v.tensor_tensor(M.LO[:, j, 0:2048], M.RAW[:, j, 0:2048], M.HI[:, j, 0:2048].bitcast(f32),
                            ALU.subtract).then_inc(s.gu_lo[j], 1)
            v.wait_ge(s.dn_hi[j], i + (u0 + 1))
            v.tensor_tensor(dn(M.LO, j), dn(M.RAW, j), dn(M.HI, j).bitcast(f32),
                            ALU.subtract).then_inc(s.dn_lo[j], 1)

        def hidden(j, i):
            v.wait_ge(s.silu[j], i + (u0 + 1))
            v.wait_ge(s.dn_used[j], i + (u0 + 1))
            v.tensor_tensor(M.H[:, j], M.SG[:, j], GU[j][:, T:2 * T], ALU.mult).then_inc(s.h_done[j], 1)
            v.wait_ge(s.hh_done[j], i + (u0 + 1))
            v.tensor_tensor(M.HL[:, j], M.H[:, j], M.HH[:, j].bitcast(f32), ALU.subtract).then_inc(s.hl_done[j], 1)

        low_parts(0, 0)
        low_parts(1, 0)
        hidden(0, 0)
        with v.Fori(1, FF_TWICE) as i:
            low_parts(0, i)
            hidden(1, i - 1)
            low_parts(1, i)
            hidden(0, i)
        hidden(1, FF_TWICE - 1)
        for n in range(4):
            v.wait_ge(s.y_done, 4 * f + n + 1)
            xs = X[:, n // 2, 512 * (n % 2):512 * (n % 2) + 512]
            v.scalar_tensor_tensor(xs, Y[:, n], 0.5, xs, ALU.mult, ALU.add).then_inc(M.x_ready, 1)

    def pe():
        if f == 0:
            for j in range(2):
                e.sem_inc(s.gu_used[j], 1)
                e.sem_inc(s.dn_used[j], 1)

        def gate_up(j, i):
            e.wait_ge(s.gu_lo[j], i + (u0 + 2))
            e.wait_ge(s.h_done[j], i + (u0 + 1))
            for q in range(2):
                for k in range(KT):
                    for n, (w, x) in enumerate([(M.HI, XH), (M.HI, XL), (M.LO, XH)]):
                        m = e.matmul(GU[j][:, T * q:T * q + T], gu(w, j)[:, q, k, :], x[:, k, :],
                                     start=(k == 0 and n == 0), stop=(k == KT - 1 and n == 2))
            m.then_inc(s.gu_used[j], 1)

        def down(j, i, first=False, last=False):
            e.wait_ge(s.dn_lo[j], i + (u0 + 2))
            e.wait_ge(s.hl_done[j], i + (u0 + 1))
            for t in range(NT):
                for q in range(2):
                    for n, (h, w) in enumerate([(M.HH, M.HI), (M.HH, M.LO), (M.HL, M.HI)]):
                        m = e.matmul(Y[:, 2 * t + q], h[:, j, 128 * t:128 * t + 128],
                                     dn(w, j)[:, 512 * q:512 * q + 512],
                                     start=first and n == 0, stop=last and n == 2)
                        if last and (t, q, n) == (1, 1, 1):
                            m.then_inc(s.dn_used[j], 1)
                    if last:
                        m.then_inc(s.y_done, 1)
            if not last:
                m.then_inc(s.dn_used[j], 1)

        gate_up(0, 0)
        gate_up(1, 0)
        down(0, 0, first=True)
        with e.Fori(1, FF_TWICE) as i:
            gate_up(0, i)
            down(1, i - 1)
            gate_up(1, i)
            down(0, i)
        down(1, FF_TWICE - 1, last=True)

    return sync, act, dve, pe


class Attention:

    def __init__(self, nc, M, L, softmaxes=0, fills=0, pairs=0):
        self.nc, self.M, self.s, self.L = nc, M, M.att, L
        self.n0, self.f0, self.p0 = softmaxes, fills, pairs
        self.n_fills = 2 * sum(len(x) for x in L.fills)

    def softmax_of(self, i, j, h, t):
        return i * 8 + (self.n0 + 4 * j + 2 * h + t)

    def fill_of(self, i, j, h, t):
        half = self.n_fills // 2
        return i * (2 * self.n_fills) + (self.f0 + self.n_fills * j + half * h + (len(self.L.fills[0]) if t else 0))

    def scores(self, i, j, h, t):
        e, s, L = self.nc.tensor, self.s, self.L
        at_least(e, s.sc_read, self.softmax_of(i, j, h, t) - 1)
        for out, lhsT, rhs in L.products(i, j, h, t):
            m = e.matmul(out, lhsT, rhs, start=True, stop=True)
        m.then_inc(s.sc_full, 1)

    def shifted(self, i, j, h, t):
        v, s, L, M = self.nc.vector, self.s, self.L, self.M
        n = self.softmax_of(i, j, h, t)
        v.wait_ge(s.sc_full, n + 1)
        v.sem_inc(M.passed, 1)
        L.shift(v, i, j, h, t).then_inc(s.sc_read, 1)

    def exponent(self, i, j, h, t):
        a, s, L, M = self.nc.scalar, self.s, self.L, self.M
        w = L.width[t]
        a.wait_ge(s.sc_read, self.softmax_of(i, j, h, t) + 1)
        a.activation(L.SC[t][:, 0:w], L.SC[t][:, 0:w], ACT.Exp, bias=M.NM[t], scale=-1.0,
                     accum_out=M.SM[t]).then_inc(s.exp_done, 1)

    def divided(self, i, j, h, t):
        v, s, L, M = self.nc.vector, self.s, self.L, self.M
        n = self.softmax_of(i, j, h, t)
        w = L.width[t]
        v.wait_ge(s.exp_done, n + 1)
        v.reciprocal(M.RC[t], M.SM[t]).then_inc(s.recip, 1)
        v.wait_ge(s.recip, n + 1)
        v.tensor_scalar(L.SC[t][:, 0:w], L.SC[t][:, 0:w], M.RC[t], None, ALU.mult).then_inc(s.p_ready, 1)

    def weighted(self, i, j, h, t):
        e, s, L, M = self.nc.tensor, self.s, self.L, self.M
        e.wait_ge(s.p_ready, self.softmax_of(i, j, h, t) + 1)
        f0 = self.fill_of(i, j, h, t)
        if h == 0 and t == 0:
            at_least(e, s.o_free, i * 2 + (self.p0 + j))
        parity = (self.n_fills // 2 * h + (len(L.fills[0]) if t else 0)) % 2
        fills = L.fills[t]
        for c, fill in enumerate(fills):
            b = (parity + c) % 2
            at_least(e, s.pt_done, f0 + (c - 1))
            for at, (col, _) in enumerate(fill):
                m = e.transpose(M.PTB[b][:, 128 * at:128 * at + 128], L.SC[t][:, col:col + 128], M.ID[:])
            m.then_inc(s.pt_full, 1)
        n_blocks, at_block = sum(len(x) for x in fills), 0
        for c, fill in enumerate(fills):
            b = (parity + c) % 2
            e.wait_ge(s.pt_done, f0 + (c + 1))
            for at, (_, key) in enumerate(fill):
                m = e.matmul(M.OB[64 * h:64 * h + 64, 128 * t:128 * t + 128], L.value(i, j, key, h),
                             L.PT[b][:, 128 * at:128 * at + 128],
                             start=at_block == 0, stop=at_block == n_blocks - 1)
                at_block += 1
            m.then_inc(s.pv_done, 1)

    def turned_out(self, i, j, h, t):
        a, s, L, M = self.nc.scalar, self.s, self.L, self.M
        f0 = self.fill_of(i, j, h, t)
        parity = (self.n_fills // 2 * h + (len(L.fills[0]) if t else 0)) % 2
        for c, fill in enumerate(L.fills[t]):
            b = (parity + c) % 2
            a.wait_ge(s.pt_full, f0 + (c + 1))
            at_least(a, s.pv_done, f0 + (c - 1))
            w = 128 * len(fill)
            a.activation(L.PT[b][:, 0:w], M.PTB[b][:, 0:w], ACT.Copy).then_inc(s.pt_done, 1)

    def output(self, i, j):
        a, s, L, M = self.nc.scalar, self.s, self.L, self.M
        a.wait_ge(s.pv_done, self.fill_of(i, j, 0, 0) + self.n_fills)
        a.activation(L.out(i, j), M.OB, ACT.Copy).then_inc(s.o_free, 1)


def dilated(nc, M, w_in, w_out, raw_free):
    s = M.dil
    PS = M.PS
    FB = [PS[:, 0, :], PS[:, 1, :]]
    QK, SQ, QR, QT, KTT, V = M.a_QK, M.a_SQ, M.a_QR, M.a_QT, M.a_KT, M.a_V
    w_in_v = w_in.rearrange("(k p) (q g n) -> p k q g n", p=128, q=3, g=GROUPS)
    v, a, e, sp, p = nc.vector, nc.scalar, nc.tensor, nc.sync, nc.gpsimd

    class L:
        width = [GROUPS * 128, GROUPS * T]
        scores = [PS[:, 2, :], PS[:, 3:5, :].rearrange("p a b -> p (a b)")]
        fills = [[[(128 * g, (0, g)) for g in range(GROUPS)]],
                 [[(T * g + 128 * kt, (kt, g)) for g in range(GROUPS)] for kt in range(NT)]]
        SC, PT = M.SC, M.PT

        @staticmethod
        def out(i, j):
            return M.OT[:, bass.ds(i * 2 + j, 1)].rearrange("p a n -> p (a n)")

        @staticmethod
        def products(i, j, h, t):
            w = 128 * (t + 1)
            return [(L.scores[t][:, g * w:(g + 1) * w], QT[64 * h:64 * h + 64, j, g, 128 * t:128 * t + 128],
                     KTT[64 * h:64 * h + 64, j, g, 0:w]) for g in range(GROUPS)]

        @staticmethod
        def shift(v, i, j, h, t):
            w = L.width[t]
            return v.tensor_tensor_reduce(out=L.SC[t][:, 0:w], in0=L.scores[t][:, 0:w],
                                          in1=M.MASK[:, MASK_A[t]:MASK_A[t] + w], scale=-(AD ** -0.5),
                                          scalar=3.0e38, op0=ALU.add, op1=ALU.min, accum_out=M.NM[t])

        @staticmethod
        def value(i, j, key, h):
            kt, g = key
            return V[:, j, kt, 128 * g + 64 * h:128 * g + 64 * h + 64]

    at = Attention(nc, M, L, softmaxes=16, fills=16, pairs=4)

    def part(buf, slot):
        return buf[:, slot].rearrange("p (k g n) -> p k g n", k=KT, g=GROUPS)

    def chunk(i, j, q):
        c = 3 * j + q
        return c % 2, i * 3 + c // 2

    def load(i, j, q):
        slot, u = chunk(i, j, q)
        at_least(sp, s.w_lo[slot], u)
        for g in range(GROUPS):
            sp.dma_start(part(M.RAW, slot)[:, :, g], w_in_v[:, :, q, g, bass.ds(i * 256 + j * 128, 128)]
                         ).then_inc(s.w_in[slot], 16)

    def high(i, j, q):
        slot, u = chunk(i, j, q)
        a.wait_ge(s.w_in[slot], u * 48 + 48)
        a.activation(M.HI[:, slot], M.RAW[:, slot], ACT.Copy).then_inc(s.w_hi[slot], 1)

    def low(i, j, q):
        slot, u = chunk(i, j, q)
        v.wait_ge(s.w_hi[slot], u + 1)
        v.tensor_tensor(M.LO[:, slot], M.RAW[:, slot], M.HI[:, slot].bitcast(f32),
                        ALU.subtract).then_inc(s.w_lo[slot], 1)

    def project(i, j, q):
        slot, u = chunk(i, j, q)
        e.wait_ge(s.w_lo[slot], u + 1)
        for t in range(NT):
            at_least(e, s.fb_free, i * 20 + (10 * j + 2 * q + t - 1))
            for k in range(KT):
                for n, (x, w) in enumerate([(M.XL, M.HI), (M.XH, M.LO), (M.XH, M.HI)]):
                    m = e.matmul(FB[t][:, 0:AW], x[:, k, 128 * t:128 * t + 128],
                                 part(w, slot)[:, k].rearrange("p g n -> p (g n)"),
                                 start=(k == 0 and n == 0), stop=(k == KT - 1 and n == 2))
            m.then_inc(s.fb_full, 1)

    def project_out(i, j, q):
        slot, u = chunk(i, j, q)
        for t in range(NT):
            a.wait_ge(s.fb_full, i * 20 + (10 * j + 2 * q + t + 1))
            dst = QK[:, t, q] if q < 2 else V[:, j, t]
            a.activation(dst, FB[t][:, 0:AW], ACT.Copy).then_inc(s.fb_free, 1)

    def norm_rope(i, j, t):
        v.wait_ge(s.fb_free, i * 20 + (10 * j + 3 + t))
        n = Chain(v, s.nr, i * 28 + (14 * j + 7 * t))
        at_least(v, s.nr, i * 28 + (14 * j + 7 * t))
        x = QK[:, t].rearrange("p q (h d) -> p (q h) d", d=AD)
        n.add(v.tensor_tensor(SQ[:], QK[:, t], QK[:, t], ALU.mult))
        n.wait()
        n.add(v.tensor_reduce(M.SSH[:, 0:12], SQ[:].rearrange("p q (h d) -> p (q h) d", d=AD), axis=AX.X, op=ALU.add))
        v.wait_ge(s.rs, i * 8 + (4 * j + 2 * t + 2))
        n.add(v.tensor_tensor(x, x, M.RSH[:, 0:12].unsqueeze(2).broadcast_to([128, 12, AD]), ALU.mult))
        n.wait()
        heads = 2 * GROUPS
        n.add(v.tensor_tensor(QR[:, t].rearrange("p q (h d) -> p q h d", d=AD),
                              QK[:, t].rearrange("p q (h d) -> p q h d", d=AD),
                              M.ROPE_A[:, t, 0].unsqueeze(2).broadcast_to([128, 2, heads, AD]), ALU.mult))
        for q in range(2):
            n.add(v.tensor_tensor(SQ[:, q].rearrange("p (h s d) -> p h s d", s=2, d=AD // 2),
                                  QK[:, t, q].rearrange("p (h s d) -> p h s d", s=2, d=AD // 2)[:, :, ::-1, :],
                                  M.ROPE_A[:, t, 1, q].rearrange("p (s d) -> p s d", s=2).unsqueeze(1)
                                  .broadcast_to([128, heads, 2, AD // 2]), ALU.mult))
        n.wait()
        n.add(v.tensor_tensor(QR[:, t], QR[:, t], SQ[:], ALU.add))

    def inverse_rms(i, j, t):
        c = i * 8 + (4 * j + 2 * t)
        p.wait_ge(s.nr, i * 28 + (14 * j + 7 * t + 2))
        p.sem_inc(M.passed, 1)
        p.tensor_scalar(M.RSH[:, 0:12], M.SSH[:, 0:12], 1 / AD, EPS, ALU.mult, ALU.add).then_inc(s.rs, 1)
        p.wait_ge(s.rs, c + 1)
        p.tensor_tensor(M.RSH[:, 0:12], M.RSH[:, 0:12], M.HF[:, 0:12], ALU.pow).then_inc(s.rs, 1)

    def turn(i, j):
        for t in range(NT):
            e.wait_ge(s.nr, i * 28 + (14 * j + 7 * t + 7))
            for q in range(2):
                at_least(e, s.fb_free, i * 20 + (10 * j + 6 + 2 * t + q - 1))
                for g in range(GROUPS):
                    m = e.transpose(FB[q][:, 128 * g:128 * g + 128], QR[:, t, q, 128 * g:128 * g + 128], M.ID[:])
                m.then_inc(s.fb_full, 1)

    def turn_out(i, j):
        for t in range(NT):
            for q in range(2):
                a.wait_ge(s.fb_full, i * 20 + (10 * j + 6 + 2 * t + q + 1))
                a.activation((QT, KTT)[q][:, j, :, 128 * t:128 * t + 128],
                             FB[q][:, 0:AW].rearrange("p (g n) -> p g n", g=GROUPS), ACT.Copy).then_inc(s.fb_free, 1)

    def sync():
        for j in range(2):
            raw_free(sp, j)
        for q in range(3):
            load(0, 0, q)
        for q in range(3):
            load(0, 1, q)
        sp.wait_ge(M.x_ready, 4)
        for k in range(KT):
            sp.dma_start(M.R[:, D * k:D * k + D], w_out[128 * k:128 * k + 128, :]).then_inc(s.wo_in, 16)
        with sp.Fori(1, PAIRS // 2) as i:
            for j in range(2):
                for q in range(3):
                    load(i, j, q)

    def act():
        def body(i, j, bi, bj, first=False):
            high(i, j, 0)
            if not first:
                turn_out(bi, bj)
                at.exponent(bi, bj, 0, 0)
                at.exponent(bi, bj, 0, 1)
            high(i, j, 1)
            project_out(i, j, 0)
            if not first:
                at.turned_out(bi, bj, 0, 0)
                at.exponent(bi, bj, 1, 0)
            high(i, j, 2)
            project_out(i, j, 1)
            if not first:
                at.turned_out(bi, bj, 0, 1)
                at.exponent(bi, bj, 1, 1)
            project_out(i, j, 2)
            if not first:
                at.turned_out(bi, bj, 1, 0)
                at.turned_out(bi, bj, 1, 1)
                at.output(bi, bj)
        body(0, 0, 0, 0, first=True)
        body(0, 1, 0, 0)
        with a.Fori(1, PAIRS // 2) as i:
            body(i, 0, i - 1, 1)
            body(i, 1, i, 0)
        i, j = PAIRS // 2 - 1, 1
        turn_out(i, j)
        at.exponent(i, j, 0, 0)
        at.exponent(i, j, 0, 1)
        at.turned_out(i, j, 0, 0)
        at.exponent(i, j, 1, 0)
        at.turned_out(i, j, 0, 1)
        at.exponent(i, j, 1, 1)
        at.turned_out(i, j, 1, 0)
        at.turned_out(i, j, 1, 1)
        at.output(i, j)

    def pool():
        for j in range(2):
            for t in range(NT):
                inverse_rms(0, j, t)
        with p.Fori(1, PAIRS // 2) as i:
            for j in range(2):
                for t in range(NT):
                    inverse_rms(i, j, t)

    def dve():
        def body(i, j, bi, bj, first=False):
            low(i, j, 0)
            if not first:
                at.shifted(bi, bj, 0, 0)
                at.shifted(bi, bj, 0, 1)
                at.divided(bi, bj, 0, 0)
                at.divided(bi, bj, 0, 1)
            low(i, j, 1)
            if not first:
                at.shifted(bi, bj, 1, 0)
                at.divided(bi, bj, 1, 0)
            low(i, j, 2)
            norm_rope(i, j, 0)
            if not first:
                at.shifted(bi, bj, 1, 1)
                at.divided(bi, bj, 1, 1)
            norm_rope(i, j, 1)
        body(0, 0, 0, 0, first=True)
        body(0, 1, 0, 0)
        with v.Fori(1, PAIRS // 2) as i:
            body(i, 0, i - 1, 1)
            body(i, 1, i, 0)
        i, j = PAIRS // 2 - 1, 1
        at.shifted(i, j, 0, 0)
        at.shifted(i, j, 0, 1)
        at.divided(i, j, 0, 0)
        at.divided(i, j, 0, 1)
        for t in range(NT):
            at.shifted(i, j, 1, t)
            at.divided(i, j, 1, t)
        add_output(nc, M, s, v)

    def pe():
        def body(i, j, bi, bj, first=False):
            if not first:
                e.wait_ge(s.fb_free, bi * 20 + (10 * bj + 10))
                at.scores(bi, bj, 0, 0)
                at.scores(bi, bj, 0, 1)
            project(i, j, 0)
            if not first:
                at.weighted(bi, bj, 0, 0)
                at.scores(bi, bj, 1, 0)
            project(i, j, 1)
            if not first:
                at.weighted(bi, bj, 0, 1)
                at.scores(bi, bj, 1, 1)
            project(i, j, 2)
            if not first:
                at.weighted(bi, bj, 1, 0)
                at.weighted(bi, bj, 1, 1)
            turn(i, j)
        body(0, 0, 0, 0, first=True)
        body(0, 1, 0, 0)
        with e.Fori(1, PAIRS // 2) as i:
            body(i, 0, i - 1, 1)
            body(i, 1, i, 0)
        i, j = PAIRS // 2 - 1, 1
        e.wait_ge(s.fb_free, 20 * i + 20)
        at.scores(i, j, 0, 0)
        at.scores(i, j, 0, 1)
        at.weighted(i, j, 0, 0)
        at.scores(i, j, 1, 0)
        at.weighted(i, j, 0, 1)
        at.scores(i, j, 1, 1)
        at.weighted(i, j, 1, 0)
        at.weighted(i, j, 1, 1)
        output_product(nc, M, s, 12, lambda k: M.R[:, D * k:D * k + D], 16 * KT)

    return sync, act, pool, dve, pe


def output_product(nc, M, s, n_pairs, w, n_loaded):
    e = nc.tensor
    e.wait_ge(M.att.o_free, n_pairs)
    e.wait_ge(s.wo_in, n_loaded)
    for t in range(NT):
        for q in range(2):
            for k in range(KT):
                m = e.matmul(M.PS[:, 2 * t + q, :], M.OT[:, k, 128 * t:128 * t + 128],
                             w(k)[:, 512 * q:512 * q + 512], start=k == 0, stop=k == KT - 1)
            m.then_inc(s.y_done, 1)


def add_output(nc, M, s, v):
    for n in range(4):
        v.wait_ge(s.y_done, n + 1)
        xs = M.X[:, n // 2, 512 * (n % 2):512 * (n % 2) + 512]
        v.tensor_tensor(xs, M.PS[:, n, :], xs, ALU.add).then_inc(M.x_ready, 1)


def latent(nc, M, w_in, w_q_up, w_kv_up, w_out, raw_free):
    s = M.lat
    PS = M.PS
    FB = [PS[:, 0, :], PS[:, 1, :]]
    C, CT, QK, SQ, QR, QKT, V = M.b_C, M.b_CT, M.b_QK, M.b_SQ, M.b_QR, M.b_QKT, M.b_V
    v, a, e, sp, p = nc.vector, nc.scalar, nc.tensor, nc.sync, nc.gpsimd
    half = B_IN // 2
    KH = KT // 2
    RAWF = M.RAW[:].rearrange("p a n -> p (a n)")
    WQ = M.R[:, 0:3 * HEADS * B_QK].rearrange("p (k n) -> p k n", k=3)
    WKV = RAWF[:, 0:4096].rearrange("p (k n) -> p k n", k=2)
    wo_at = lambda k: (M.R[:, 4608 + D * k:4608 + D * k + D] if k < KT - 1 else RAWF[:, 4096:4096 + D])
    w_in_v = w_in.rearrange("(c k p) n -> p c k n", p=128, k=KH)

    class L:
        width = [128, T]
        scores = [PS[:, 2, :], PS[:, 3, :]]
        fills = [[[(0, 0)]], [[(0, 0), (128, 1)]]]
        SC, PT = M.SC, M.PT

        @staticmethod
        def out(i, j):
            return M.OT[:, bass.ds(i * 2 + j, 1)].rearrange("p a n -> p (a n)")

        @staticmethod
        def products(i, j, h, t):
            w = 128 * (t + 1)
            return [(L.scores[t][:, 0:w], QKT[:, j, h, 128 * t:128 * t + 128], QKT[:, j, 2 + h, 0:w])]

        @staticmethod
        def shift(v, i, j, h, t):
            w = L.width[t]
            return v.tensor_tensor_reduce(out=L.SC[t][:, 0:w], in0=L.scores[t][:, 0:w],
                                          in1=M.MASK[:, MASK_B[t]:MASK_B[t] + w], scale=-(B_QK ** -0.5),
                                          scalar=3.0e38, op0=ALU.add, op1=ALU.min, accum_out=M.NM[t])

        @staticmethod
        def value(i, j, key, h):
            return V[:, j, key, h]

    at = Attention(nc, M, L, softmaxes=48, fills=16 + 6 * PAIRS, pairs=12)

    def down_chunk(buf, c):
        return buf[:, c, 0:KH * B_IN].rearrange("p (k n) -> p k n", k=KH)

    def project(i, j):
        for t in range(NT):
            at_least(e, s.fb_free, i * 12 + (6 * j + t - 1))
            for k in range(3):
                m = e.matmul(FB[t][:, 0:2 * B_QK], CT[:, k, 128 * t:128 * t + 128],
                             WQ[:, k, bass.ds((i * 2 + j) * (2 * B_QK), 2 * B_QK)], start=k == 0, stop=k == 2)
            m.then_inc(s.fb_full, 1)
        for t in range(NT):
            at_least(e, s.fb_free, i * 12 + (6 * j + 2 + t - 1))
            for k in range(2):
                m = e.matmul(FB[t][:, 0:256], CT[:, 3 + k, 128 * t:128 * t + 128],
                             WKV[:, k, bass.ds((i * 2 + j) * 256, 256)], start=k == 0, stop=k == 1)
            m.then_inc(s.fb_full, 1)

    def project_out(i, j):
        for t in range(NT):
            a.wait_ge(s.fb_full, i * 12 + (6 * j + t + 1))
            a.activation(QK[:, t, 0:2].rearrange("p h d -> p (h d)"), FB[t][:, 0:2 * B_QK], ACT.Copy).then_inc(s.fb_free, 1)
        for t in range(NT):
            a.wait_ge(s.fb_full, i * 12 + (6 * j + 2 + t + 1))
            kv = FB[t][:, 0:256].rearrange("p (h d) -> p h d", h=2)
            a.activation(QK[:, t, 2:4, 0:B_NOPE], kv[:, :, 0:B_NOPE], ACT.Copy)
            a.activation(QK[:, t, 2:4, B_NOPE:], C[:, t, B_QR + B_KVR:].unsqueeze(1).broadcast_to([128, 2, B_ROPE]), ACT.Copy)
            a.activation(V[:, j, t], kv[:, :, B_NOPE:], ACT.Copy).then_inc(s.fb_free, 1)

    def norm_rope(i, j, t):
        v.wait_ge(s.fb_free, i * 12 + (6 * j + 3 + t))
        n = Chain(v, s.nr, i * 28 + (14 * j + 7 * t))
        at_least(v, s.nr, i * 28 + (14 * j + 7 * t))
        n.add(v.tensor_tensor(SQ[:], QK[:, t], QK[:, t], ALU.mult))
        n.wait()
        n.add(v.tensor_reduce(M.SSH[:, 0:4], SQ[:], axis=AX.X, op=ALU.add))
        v.wait_ge(s.rs, 2 + i * 8 + (4 * j + 2 * t + 2))
        n.add(v.tensor_tensor(QK[:, t], QK[:, t], M.RSH[:, 0:4].unsqueeze(2).broadcast_to([128, 4, B_QK]), ALU.mult))
        n.wait()
        n.add(v.tensor_tensor(QR[:, t].rearrange("p (q h) d -> p q h d", q=2),
                              QK[:, t].rearrange("p (q h) d -> p q h d", q=2),
                              M.ROPE_B[:, t, :, 0:B_QK].unsqueeze(2).broadcast_to([128, 2, 2, B_QK]), ALU.mult))
        for q in range(2):
            n.add(v.tensor_tensor(SQ[:, 2 * q:2 * q + 2, B_NOPE:].rearrange("p h (s d) -> p h s d", s=2),
                                  QK[:, t, 2 * q:2 * q + 2, B_NOPE:].rearrange("p h (s d) -> p h s d", s=2)[:, :, ::-1, :],
                                  M.ROPE_B[:, t, q, B_QK:].rearrange("p (s d) -> p s d", s=2).unsqueeze(1)
                                  .broadcast_to([128, 2, 2, B_ROPE // 2]), ALU.mult))
        n.wait()
        n.add(v.tensor_tensor(QR[:, t, :, B_NOPE:], QR[:, t, :, B_NOPE:], SQ[:, :, B_NOPE:], ALU.add))

    def inverse_rms(i, j, t):
        p.wait_ge(s.nr, i * 28 + (14 * j + 7 * t + 2))
        p.sem_inc(M.passed, 1)
        p.tensor_scalar(M.RSH[:, 0:4], M.SSH[:, 0:4], 1 / B_QK, EPS, ALU.mult, ALU.add).then_inc(s.rs, 1)
        p.wait_ge(s.rs, 2 + i * 8 + (4 * j + 2 * t + 1))
        p.tensor_tensor(M.RSH[:, 0:4], M.RSH[:, 0:4], M.HF[:, 0:4], ALU.pow).then_inc(s.rs, 1)

    def turn(i, j):
        for t in range(NT):
            e.wait_ge(s.nr, i * 28 + (14 * j + 7 * t + 7))
            at_least(e, s.fb_free, i * 12 + (6 * j + 4 + t - 1))
            for h in range(4):
                m = e.transpose(FB[t][0:B_QK, 128 * h:128 * h + 128], QR[:, t, h], M.ID[:])
            m.then_inc(s.fb_full, 1)

    def turn_out(i, j):
        for t in range(NT):
            a.wait_ge(s.fb_full, i * 12 + (6 * j + 4 + t + 1))
            a.activation(QKT[:, j, :, 128 * t:128 * t + 128],
                         FB[t][0:B_QK, :].rearrange("p (h n) -> p h n", h=4), ACT.Copy).then_inc(s.fb_free, 1)

    def sync():
        for c in range(2):
            raw_free(sp, c)
            sp.dma_start(down_chunk(M.RAW, c), w_in_v[:, c]).then_inc(s.w_in[c], 16)
        sp.wait_ge(M.x_ready, 12)
        sp.dma_start(WQ, w_q_up.rearrange("(k p) n -> p k n", p=128)).then_inc(s.wq_in, 16)
        for k in range(KT - 1):
            sp.dma_start(wo_at(k), w_out[128 * k:128 * k + 128, :]).then_inc(s.wo_in, 16)
        for c in range(2):
            sp.wait_ge(s.w_lo[c], MIX_LOADS + 1)
        sp.dma_start(WKV, w_kv_up.rearrange("(k p) n -> p k n", p=128)).then_inc(s.wq_in, 16)
        sp.dma_start(wo_at(KT - 1), w_out[D - 128:, :]).then_inc(s.wo_in, 16)

    def act():
        for c in range(2):
            a.wait_ge(s.w_in[c], 48 * 12 + 16)
            a.activation(down_chunk(M.HI, c), down_chunk(M.RAW, c), ACT.Copy).then_inc(s.w_hi[c], 1)
        for t in range(NT):
            a.wait_ge(s.c_full, t + 1)
            for q in range(2):
                a.activation(C[:, t, half * q:half * q + half], PS[:, 2 * t + q, 0:half], ACT.Copy).then_inc(s.c_out, 1)
            a.wait_ge(s.c_out, 4 * t + 2)
            for q, (lo, hi) in enumerate([(0, B_QR), (B_QR, B_QR + B_KVR)]):
                if q:
                    a.wait_ge(s.c_out, 4 * t + 3)
                a.activation(M.JUNK[:, 0:hi - lo], C[:, t, lo:hi], ACT.Square,
                             accum_out=M.SSB[:, 2 * q + t:2 * q + t + 1]).then_inc(s.c_out, 1)
        for k in range(5):
            a.wait_ge(s.ct_full, k // 2 + 1)
            a.activation(CT[:, k], M.TRB[k // 2 % 2][:, T * (k % 2):T * (k % 2) + T], ACT.Copy,
                         scale=M.GC[:, GC_BA + k:GC_BA + k + 1]).then_inc(s.ct_done, 1)

        def body(i, j, bi, bj):
            project_out(i, j)
            back(bi, bj)
            turn_out(i, j)

        def back(bi, bj):
            at.exponent(bi, bj, 0, 0)
            at.exponent(bi, bj, 0, 1)
            at.turned_out(bi, bj, 0, 0)
            at.exponent(bi, bj, 1, 0)
            at.turned_out(bi, bj, 0, 1)
            at.exponent(bi, bj, 1, 1)
            at.turned_out(bi, bj, 1, 0)
            at.turned_out(bi, bj, 1, 1)
            at.output(bi, bj)
        project_out(0, 0)
        turn_out(0, 0)
        body(0, 1, 0, 0)
        with a.Fori(1, PAIRS // 2) as i:
            body(i, 0, i - 1, 1)
            body(i, 1, i, 0)
        back(PAIRS // 2 - 1, 1)

    def pool():
        p.wait_ge(s.c_out, 8)
        RSB, SSB = M.RSB, M.SSB
        p.tensor_scalar(RSB[:, 0:2], SSB[:, 0:2], 1 / B_QR, EPS, ALU.mult, ALU.add).then_inc(s.rs, 1)
        p.tensor_scalar(RSB[:, 2:4], SSB[:, 2:4], 1 / B_KVR, EPS, ALU.mult, ALU.add).then_inc(s.rs, 1)
        p.wait_ge(s.rs, 2)
        p.tensor_tensor(RSB[:], RSB[:], M.HF[:, 0:4], ALU.pow).then_inc(s.c_rs, 1)
        for j in range(2):
            for t in range(NT):
                inverse_rms(0, j, t)
        with p.Fori(1, PAIRS // 2) as i:
            for j in range(2):
                for t in range(NT):
                    inverse_rms(i, j, t)

    def dve():
        for c in range(2):
            v.wait_ge(s.w_hi[c], MIX_LOADS + 1)
            v.tensor_tensor(down_chunk(M.LO, c), down_chunk(M.RAW, c), down_chunk(M.HI, c).bitcast(f32),
                            ALU.subtract).then_inc(s.w_lo[c], 1)
        v.wait_ge(s.c_rs, 1)
        for t in range(NT):
            for q, (lo, hi) in enumerate([(0, B_QR), (B_QR, B_QR + B_KVR)]):
                v.tensor_scalar(C[:, t, lo:hi], C[:, t, lo:hi], M.RSB[:, 2 * q + t:2 * q + t + 1], None,
                                ALU.mult).then_inc(s.cn, 1)

        def back(bi, bj):
            at.shifted(bi, bj, 0, 0)
            at.shifted(bi, bj, 0, 1)
            at.divided(bi, bj, 0, 0)
            at.divided(bi, bj, 0, 1)
            at.shifted(bi, bj, 1, 0)
            at.shifted(bi, bj, 1, 1)
            at.divided(bi, bj, 1, 0)
            at.divided(bi, bj, 1, 1)

        def body(i, j, bi, bj):
            back(bi, bj)
            norm_rope(i, j, 0)
            norm_rope(i, j, 1)
        norm_rope(0, 0, 0)
        norm_rope(0, 0, 1)
        body(0, 1, 0, 0)
        with v.Fori(1, PAIRS // 2) as i:
            body(i, 0, i - 1, 1)
            body(i, 1, i, 0)
        back(PAIRS // 2 - 1, 1)
        add_output(nc, M, s, v)

    def pe():
        for c in range(2):
            e.wait_ge(s.w_lo[c], MIX_LOADS + 1)
            for t in range(NT):
                for q in range(2):
                    for kk in range(KH):
                        k = KH * c + kk
                        for n, (x, w) in enumerate([(M.XL, M.HI), (M.XH, M.LO), (M.XH, M.HI)]):
                            m = e.matmul(PS[:, 2 * t + q, 0:half], x[:, k, 128 * t:128 * t + 128],
                                         down_chunk(w, c)[:, kk, half * q:half * q + half],
                                         start=(k == 0 and n == 0), stop=(k == KT - 1 and n == 2))
                if c == 1:
                    m.then_inc(s.c_full, 1)
        e.wait_ge(s.cn, 4)
        for b in range(3):
            if b == 2:
                e.wait_ge(s.ct_done, 2)
            for k in range(2 * b, min(2 * b + 2, 5)):
                for t in range(NT):
                    m = e.transpose(M.TRB[b % 2][:, T * (k % 2) + 128 * t:T * (k % 2) + 128 * t + 128],
                                    C[:, t, 128 * k:128 * k + 128], M.ID[:])
            m.then_inc(s.ct_full, 1)
        e.wait_ge(s.ct_done, 5)
        e.wait_ge(s.wq_in, 32)

        def back(bi, bj, between=lambda: None):
            e.wait_ge(s.fb_free, bi * 12 + (6 * bj + 6))
            at.scores(bi, bj, 0, 0)
            at.scores(bi, bj, 0, 1)
            between()
            at.weighted(bi, bj, 0, 0)
            at.scores(bi, bj, 1, 0)
            at.weighted(bi, bj, 0, 1)
            at.scores(bi, bj, 1, 1)
            at.weighted(bi, bj, 1, 0)
            at.weighted(bi, bj, 1, 1)

        def body(i, j, bi, bj):
            back(bi, bj, lambda: project(i, j))
            turn(i, j)
        project(0, 0)
        turn(0, 0)
        body(0, 1, 0, 0)
        with e.Fori(1, PAIRS // 2) as i:
            body(i, 0, i - 1, 1)
            body(i, 1, i, 0)
        back(PAIRS // 2 - 1, 1)
        output_product(nc, M, s, 20, wo_at, 16 * KT)

    return sync, act, pool, dve, pe


def rope_tables(nc, M):
    v, a, s = nc.vector, nc.scalar, M.rope
    two_pi = 2 * np.pi
    c1 = 6.28125
    c2 = float(two_pi - c1)
    magic = 1.5 * 2 ** 23
    ANG, TURNS, CS = M.r_ANG, M.r_TURNS, M.r_CS
    NF = 48

    def dve():
        n = Chain(v, s.ch)
        v.wait_ge(M.small_in, M.n_small)
        n.add(v.tensor_copy(M.POSF[:], M.POS[:]))
        n.wait()
        for t in range(NT):
            n.add(v.tensor_scalar(ANG[:, t], M.FREQ[:], M.POSF[:, t:t + 1], None, ALU.mult))
        n.wait()
        for which, quarter in enumerate((0.0, 0.25)):
            tr, cs = TURNS[:, which], CS[:, which]
            n.add(v.tensor_scalar(tr, ANG[:], 1 / two_pi, quarter, ALU.mult, ALU.add))
            n.wait()
            n.add(v.tensor_scalar(tr, tr, magic, None, ALU.add))
            n.wait()
            n.add(v.tensor_scalar(tr, tr, magic, None, ALU.subtract))
            n.wait()
            n.add(v.scalar_tensor_tensor(cs, tr, -c1, ANG[:], ALU.mult, ALU.add))
            n.wait()
            n.add(v.scalar_tensor_tensor(cs, tr, -c2, cs, ALU.mult, ALU.add))
            n.wait()
            n.add(v.tensor_scalar(cs, cs, quarter * two_pi, 3.1415925, ALU.add, ALU.min))
            n.wait()
            n.add(v.tensor_scalar(cs, cs, -3.1415925, None, ALU.max))
            n.wait()
        v.sem_inc(s.reduced, 1)
        v.wait_ge(s.sines, 1)
        n = Chain(v, s.ch, n.n)
        for t in range(NT):
            for q in range(2):
                for sin_lo, sin_hi, fl, g0, w, tab_c, tab_s in (
                        (0, 1, 0, 0, 32, M.ROPE_A[:, t, 0, q], M.ROPE_A[:, t, 1, q]),
                        (0, 1, 32, 64, 16, M.ROPE_B[:, t, q, B_NOPE:B_QK], M.ROPE_B[:, t, q, B_QK:])):
                    gains = M.HG[:, 160 * q:160 * q + 160]
                    g1 = gains[:, 0:32] if w == 32 else gains[:, 128:144]
                    g2 = gains[:, 32:64] if w == 32 else gains[:, 144:160]
                    cos, sin = CS[:, 1, t, fl:fl + w], CS[:, 0, t, fl:fl + w]
                    n.add(v.tensor_tensor(tab_c[:, 0:w], g1, cos, ALU.mult))
                    n.add(v.tensor_tensor(tab_c[:, w:2 * w], g2, cos, ALU.mult))
                    n.add(v.scalar_tensor_tensor(tab_s[:, 0:w], g2, -1.0, sin, ALU.mult, ALU.mult))
                    n.add(v.tensor_tensor(tab_s[:, w:2 * w], g1, sin, ALU.mult))
                n.add(v.tensor_copy(M.ROPE_B[:, t, q, 0:B_NOPE], M.HG[:, 160 * q + 64:160 * q + 128]))
        n.wait()

    def act():
        a.wait_ge(s.reduced, 1)
        a.activation(CS[:], CS[:], ACT.Sin).then_inc(s.sines, 1)

    return act, dve


def conditioning(nc, M, w_ada, b_ada):
    e, a, v, sp, s = nc.tensor, nc.scalar, nc.vector, nc.sync, M.ada
    AB, MTB = M.PS[:, 0, :], M.PS[:, 1, :]

    def load(n):
        g, m = divmod(n, 9)
        slot, u = n % R_SLOTS, n // R_SLOTS
        at_least(sp, s.r_used[slot], u)
        dst = M.R[:, SR * slot:SR * slot + SR]
        if m == 0:
            sp.dma_start(dst[0:1], b_ada[:, SR * g:SR * g + SR]).then_inc(s.r_in[slot], 16)
        else:
            sp.dma_start(dst, w_ada[128 * (m - 1):128 * m, SR * g:SR * g + SR]).then_inc(s.r_in[slot], 16)

    def product(n):
        g, m = divmod(n, 9)
        slot, u = n % R_SLOTS, n // R_SLOTS
        if n == 0:
            e.wait_ge(s.cs, 1)
            e.wait_ge(M.ones_set, 3)
        e.wait_ge(s.r_in[slot], 16 * u + 16)
        if m == 0:
            at_least(e, s.mr, 4 * g)
        for q in range(4):
            rhs = M.R[:, SR * slot + 512 * q:SR * slot + 512 * q + 512]
            lhsT = M.ONES[0:1, 0:2] if m == 0 else M.CS[:, m - 1, :]
            mm = e.matmul(AB[32 * q:32 * q + 2, :], lhsT, rhs[0:1] if m == 0 else rhs, start=m == 0, stop=m == 8)
        mm.then_inc(s.r_used[slot], 1)

    def rows_out(g):
        a.wait_ge(M.ones_set, 3)
        a.wait_ge(s.r_used[(9 * g + 8) % R_SLOTS], (9 * g + 8) // R_SLOTS + 1)
        for q in range(4):
            a.activation(M.MR[32 * q:32 * q + 2, g, :], AB[32 * q:32 * q + 2, :], ACT.Copy).then_inc(s.mr, 1)

    def turn(g):
        e.wait_ge(s.mr, 4 * g + 4)
        at_least(e, s.mc, g)
        for b in range(4):
            mm = e.transpose(MTB[:, 128 * b:128 * b + 128], M.MR[:, g, 128 * b:128 * b + 128], M.ID[:])
        mm.then_inc(s.mt, 1)

    def columns_out(g):
        v.wait_ge(s.mt, g + 1)
        v.tensor_copy(M.MC[:, 32 * g:32 * g + 32].rearrange("p (q b w) -> p q b w", q=4, b=4),
                      MTB.rearrange("p (b q r) -> p q b r", b=4, q=4)[:, :, :, 0:2]).then_inc(s.mc, 1)

    return load, product, rows_out, turn, columns_out


def first_mixer(nc, M, A):
    e, a, v, sp, p, s = nc.tensor, nc.scalar, nc.vector, nc.sync, nc.gpsimd, M.mix
    PS, TRB = M.PS, M.TRB
    FB = [PS[:, 4, :], PS[:, 5, :]]
    load, product, rows_out, turn_rows, columns_out = conditioning(nc, M, A["w_ada"], A["b_ada"])
    w_in_v = A["w_in"].rearrange("(k p) n -> p k n", p=128)
    Q0, K0, V0, B0 = FH, 3 * FH, 5 * FH, 7 * FH
    CHUNKS = [(K0, "k", 0), (K0 + 256, "k", 1), (V0, "v", 0), (V0 + 256, "v", 1), (Q0, "q", 0), (Q0 + 256, "q", 1),
              (0, "f", 0), (B0, "b", 0), (B0 + 256, "c", 0), (B0 + 512, "h", 0)]
    CH_PART = lambda buf, c: buf[:, c % 2, 0:SR].rearrange("p (k n) -> p k n", k=KT)
    CXP = lambda buf, k: buf[:, k // 4, SR + T * (k % 4):SR + T * (k % 4) + T]
    SIDES = [(lambda k: M.XH[:, k], lambda k: M.XL[:, k]), (lambda k: CXP(M.HI, k), lambda k: CXP(M.LO, k))]

    def uses():
        n = 0
        for c, (_, kind, at) in enumerate(CHUNKS):
            for side in range(2 if kind in "kv" else 1):
                yield n, c, kind, at, side
                n += 1
    USES = list(uses())

    class L:
        width = [512, 512]
        scores = [PS[:, 2, :], PS[:, 3, :]]
        fills = [[[(128 * kt, kt) for kt in range(4)]]] * 2
        SC, PT = M.n_SC, M.n_PT

        @staticmethod
        def products(i, j, h, t):
            return [(L.scores[t], M.QT0[64 * h:64 * h + 64, 2 * i + j, 128 * t:128 * t + 128],
                     M.KT0[64 * h:64 * h + 64, 2 * i + j, :])]

        @staticmethod
        def shift(v, i, j, h, t):
            v.wait_ge(s.bias_in[2 * h + t], 16 * (2 * i + j) + 16)
            return v.tensor_tensor_reduce(out=L.SC[t], in0=L.scores[t], in1=M.BIAS[2 * h + t], scale=-1.0,
                                          scalar=3.0e38, op0=ALU.add, op1=ALU.min, accum_out=M.NM[t])

        @staticmethod
        def value(i, j, key, h):
            return M.V0[:, key, 128 * (2 * i + j) + 64 * h:128 * (2 * i + j) + 64 * h + 64]

        @staticmethod
        def out(i, j):
            return M.mix_OT[:, 2 + 2 * i + j]

    NAP = 4
    at = Attention(nc, M, L)

    def bias_load(pr, h, t):
        at_least(sp, M.att.sc_read, 4 * (pr - 1) + 2 * h + t + 1)
        sp.dma_start(M.BIAS[2 * h + t][:, 0:T], A["bias"][2 * pr + h, 128 * t:128 * t + 128, :]).then_inc(s.bias_in[2 * h + t], 16)

    def sync():
        sp.dma_start(M.CRAW[:], A["conditions"]).then_inc(s.c_in, 16)
        for n in range(9):
            load(n)
        for h in range(2):
            for t in range(NT):
                bias_load(0, h, t)
        for n in range(9, 27):
            load(n)
        for k in range(4):
            n = 27 + k
            slot, u = n % R_SLOTS, n // R_SLOTS
            sp.wait_ge(M.ada.r_used[slot], u)
            sp.dma_start(M.R[:, SR * slot:SR * slot + SR].rearrange("p (a n) -> p a n", a=2),
                         A["w_out"][256 * k:256 * k + 256, :].rearrange("(a p) n -> p a n", p=128)).then_inc(M.ada.r_in[slot], 16)
        for pr in range(1, NAP):
            for h in range(2):
                for t in range(NT):
                    bias_load(pr, h, t)

    def pool():
        p.memset(M.BIASZ, 0.0).then_inc(s.zeroed, 1)
        for c in range(2):
            p.dma_start(CH_PART(M.RAW, c), w_in_v[:, :, CHUNKS[c][0]:CHUNKS[c][0] + 256]).then_inc(s.w_in[c], 16)
        p.wait_ge(s.sq, 4)
        p.tensor_scalar(M.RS4[:], M.SS4[:], 1 / D, EPS, ALU.mult, ALU.add).then_inc(s.rs, 1)
        p.wait_ge(s.rs, 1)
        p.tensor_tensor(M.RS4[:], M.RS4[:], M.HF[:, 0:4], ALU.pow).then_inc(s.rs, 1)
        for c in range(2, len(CHUNKS)):
            p.wait_ge(s.w_lo[c % 2], c // 2)
            p.dma_start(CH_PART(M.RAW, c), w_in_v[:, :, CHUNKS[c][0]:CHUNKS[c][0] + 256]).then_inc(s.w_in[c % 2], 16)

    def act():
        a.wait_ge(s.c_in, 16)
        a.activation(M.CS[:], M.CRAW[:], ACT.Silu).then_inc(M.ada.cs, 1)
        a.wait_ge(s.x_in, 32)
        for n in range(4):
            at_least(a, s.sq, n)
            src = (M.X, M.CX)[n // 2][:, n % 2]
            a.activation(M.JUNK1, src, ACT.Square, accum_out=M.SS4[:, n:n + 1]).then_inc(s.sq, 1)
        rows_out(0)
        for side in range(2):
            for k in range(KT):
                a.wait_ge(s.tm, KT * side + k + 1)
                a.activation(SIDES[side][0](k), M.TM[k % 4], ACT.Copy).then_inc(s.xh, 1)

        def high(c):
            a.wait_ge(s.w_in[c % 2], 16 * (c // 2) + 16)
            a.activation(M.HI[:, c % 2, 0:SR], M.RAW[:, c % 2, 0:SR], ACT.Copy).then_inc(s.w_hi[c % 2], 1)
        high(0)
        high(1)
        for n, c, kind, at_, side in USES:
            a.wait_ge(s.fb_full, n + 1)
            src = FB[n % 2]
            two = src.rearrange("p (m n) -> p m n", m=2)
            if kind == "v":
                dst = M.V0[:, 2 * side:2 * side + 2, 256 * at_:256 * at_ + 256]
            elif kind == "k":
                dst = M.KT0[:, 2 * at_:2 * at_ + 2, T * side:T * side + T]
            elif kind == "q":
                dst = M.QT0[:, 2 * at_:2 * at_ + 2]
            else:
                dst = {"f": M.FT, "b": M.BT, "c": M.CT0, "h": M.HT0}[kind]
            a.activation(dst, two, ACT.Copy, scale=AD ** -0.5 if kind == "q" else 1.0).then_inc(s.fb_free, 1)
            if c + 2 < len(CHUNKS) and (n + 1 == len(USES) or USES[n + 1][1] != c):
                high(c + 2)
            if c == 4:
                rows_out(1)
            if c == 9:
                rows_out(2)
        for t in range(NT):
            a.wait_ge(s.fo_full, t + 1)
            a.activation(M.FA[:, t], FB[t], ACT.Copy).then_inc(s.fo_done, 1)
        a.wait_ge(s.fo_full, 3)
        a.activation(M.FOT, FB[0], ACT.Copy).then_inc(s.fo_done, 1)
        a.wait_ge(s.fo_full, 4)
        a.activation(M.mix_OT[:, 0:2].rearrange("p a n -> p (a n)"), FB[1], ACT.Copy).then_inc(s.fo_done, 1)
        for pr in range(NAP):
            i, j = divmod(pr, 2)
            at.exponent(i, j, 0, 0)
            at.exponent(i, j, 0, 1)
            at.turned_out(i, j, 0, 0)
            at.exponent(i, j, 1, 0)
            at.turned_out(i, j, 0, 1)
            at.exponent(i, j, 1, 1)
            at.turned_out(i, j, 1, 0)
            at.turned_out(i, j, 1, 1)
            at.output(i, j)
        for g, q0, dst in ((1, 0, M.G1B), (2, 2, M.G2B)):
            for q in range(2):
                n = 2 * (g - 1) + q
                a.wait_ge(s.gb_full, n + 1)
                a.activation(dst[:, 512 * q:512 * q + 512], FB[n % 2], ACT.Copy).then_inc(s.gb_done, 1)

    def dve():
        columns_out(0)
        n = Chain(v, s.ch)
        v.wait_ge(M.ada.mc, 1)
        v.wait_ge(M.small_in, M.n_small)
        mc = M.MC[:].rearrange("p (f w) -> p f w", w=2)
        for who in range(2):
            n.add(v.scalar_tensor_tensor(M.MSC[:, who], mc[:, 8:16, who], 1.0, M.GC[:, GC_N1:GC_N1 + 8], ALU.add, ALU.mult))
        v.wait_ge(s.rs, 2)
        for side in range(2):
            src, dst = ((M.X, M.mix_XN), (M.CX, M.CX))[side]
            for t in range(NT):
                n.add(v.tensor_scalar(dst[:, t], src[:, t], M.RS4[:, 2 * side + t:2 * side + t + 1], None, ALU.mult))
        n.wait()
        for side in range(2):
            for k in range(KT):
                m = KT * side + k
                v.wait_ge(s.turned, m // 2 + 1)
                at_least(v, s.xl, m - 3)
                v.tensor_scalar(M.TM[k % 4], TRB[m // 2 % 2][:, T * (k % 2):T * (k % 2) + T],
                                M.MSC[:, side, k:k + 1], mc[:, k, side:side + 1], ALU.mult, ALU.add).then_inc(s.tm, 1)
                if k % 2:
                    for kk in (k - 1, k):
                        v.wait_ge(s.xh, KT * side + kk + 1)
                        v.tensor_tensor(SIDES[side][1](kk), M.TM[kk % 4], SIDES[side][0](kk).bitcast(f32),
                                        ALU.subtract).then_inc(s.xl, 1)
        for c in range(len(CHUNKS)):
            v.wait_ge(s.w_hi[c % 2], c // 2 + 1)
            v.tensor_tensor(M.LO[:, c % 2, 0:SR], M.RAW[:, c % 2, 0:SR], M.HI[:, c % 2, 0:SR].bitcast(f32),
                            ALU.subtract).then_inc(s.w_lo[c % 2], 1)
            if c == 7:
                columns_out(1)
        n = Chain(v, s.ch, 6)
        v.wait_ge(s.fb_free, len(USES))
        v.wait_ge(s.zeroed, 1)
        for col in (0, T + 1):
            n.add(v.memset(M.CHP[:, :, col:col + 1], 0.0))
        n.add(v.tensor_tensor(M.CHP[:, :, 1:T + 1], M.CT0, M.HT0, ALU.mult))
        n.wait()
        for m in range(2):
            w = lambda tap: M.GC[:, GC_CONV + 2 * tap + m:GC_CONV + 2 * tap + m + 1]
            dst = M.mix_OT[:, 6 + m]
            n.add(v.tensor_scalar(dst, M.CHP[:, m, 0:T], w(0), None, ALU.mult))
            n.wait()
            for tap in (1, 2):
                n.add(v.scalar_tensor_tensor(dst, M.CHP[:, m, tap:tap + T], w(tap), dst, ALU.mult, ALU.add))
                n.wait()
            n.add(v.tensor_tensor(dst, dst, M.BT[:, m], ALU.mult))
        n.wait()
        for pr in range(NAP):
            i, j = divmod(pr, 2)
            at.shifted(i, j, 0, 0)
            at.shifted(i, j, 0, 1)
            at.divided(i, j, 0, 0)
            at.divided(i, j, 0, 1)
            at.shifted(i, j, 1, 0)
            at.shifted(i, j, 1, 1)
            at.divided(i, j, 1, 0)
            at.divided(i, j, 1, 1)
        columns_out(2)
        for n4 in range(4):
            v.wait_ge(s.y_done, n4 + 1)
            v.wait_ge(s.gb_done, n4 % 2 + 1)
            at_least(v, s.xu, 2 * (n4 - 1))
            q = n4 % 2
            v.tensor_tensor(M.TMPX[n4 % 2], PS[:, n4, :], M.G1B[:, 512 * q:512 * q + 512], ALU.mult).then_inc(s.xu, 1)
            v.wait_ge(s.xu, 2 * n4 + 1)
            xs = M.X[:, n4 // 2, 512 * q:512 * q + 512]
            v.tensor_tensor(xs, M.TMPX[n4 % 2], xs, ALU.add).then_inc(s.xu, 1)

    def pe():
        for n in range(9):
            product(n)
        turn_rows(0)
        e.wait_ge(s.ch, 6)
        for m in range(KT):
            side, b = divmod(m, 4)
            at_least(e, s.tm, 2 * (m - 1))
            src = (M.mix_XN, M.CX)[side]
            for kk in range(2):
                for t in range(NT):
                    k = 2 * b + kk
                    mm = e.transpose(TRB[m % 2][:, T * kk + 128 * t:T * kk + 128 * t + 128],
                                     src[:, t, 128 * k:128 * k + 128], M.ID[:])
            mm.then_inc(s.turned, 1)
        e.wait_ge(s.xl, 2 * KT)
        ada = 9
        for n, c, kind, at_, side in USES:
            e.wait_ge(s.w_lo[c % 2], c // 2 + 1)
            at_least(e, s.fb_free, n - 1)
            xh, xl = SIDES[side]
            hi, lo = CH_PART(M.HI, c), CH_PART(M.LO, c)
            for m in range(2):
                for k in range(KT):
                    for q, (w, x) in enumerate([(hi, xh), (hi, xl), (lo, xh)]):
                        if kind == "v":
                            l, r = x(k)[:, 128 * m:128 * m + 128], w[:, k, :]
                        else:
                            l, r = w[:, k, 128 * m:128 * m + 128], x(k)
                        mm = e.matmul(FB[n % 2][:, 256 * m:256 * m + 256], l, r,
                                      start=(k == 0 and q == 0), stop=(k == KT - 1 and q == 2))
            mm.then_inc(s.fb_full, 1)
            if n + 1 == len(USES) or USES[n + 1][1] != c:
                if c < 9:
                    for _ in range(2):
                        product(ada)
                        ada += 1
                if c == 5:
                    turn_rows(1)
        e.wait_ge(M.small2, 64)
        e.wait_ge(s.fb_free, len(USES))
        for t in range(NT):
            for kc in range(2):
                mm = e.matmul(FB[t][:, 256 * kc:256 * kc + 256], M.FT[:, kc, 128 * t:128 * t + 128], M.DFT[:, 0:256],
                              start=True, stop=True)
            mm.then_inc(s.fo_full, 1)
        e.wait_ge(s.fo_done, 2)
        for kc in range(2):
            for n, (t, q) in enumerate([(0, 0), (0, 1), (1, 0), (1, 1)]):
                mm = e.matmul(FB[0][:, 256 * kc:256 * kc + 256], M.FA[:, t, 256 * kc + 128 * q:256 * kc + 128 * q + 128],
                              M.DFT[:, 256 + 512 * q + 256 * t:256 + 512 * q + 256 * t + 256], start=n == 0, stop=n == 3)
        mm.then_inc(s.fo_full, 1)
        e.wait_ge(s.fo_done, 3)
        for m in range(2):
            for kc in range(2):
                mm = e.matmul(FB[1][:, 256 * m:256 * m + 256], M.WF[:, kc, 128 * m:128 * m + 128], M.FOT[:, 256 * kc:256 * kc + 256],
                              start=kc == 0, stop=kc == 1)
        mm.then_inc(s.fo_full, 1)
        e.wait_ge(s.fo_done, 4)
        e.wait_ge(s.ch, 17)
        for pr in range(NAP):
            i, j = divmod(pr, 2)
            at.scores(i, j, 0, 0)
            at.scores(i, j, 0, 1)
            at.weighted(i, j, 0, 0)
            at.scores(i, j, 1, 0)
            at.weighted(i, j, 0, 1)
            at.scores(i, j, 1, 1)
            at.weighted(i, j, 1, 0)
            at.weighted(i, j, 1, 1)
        turn_rows(2)
        e.wait_ge(M.att.o_free, NAP)
        for g, q0 in ((1, 0), (2, 2)):
            for q in range(2):
                n = 2 * (g - 1) + q
                at_least(e, s.gb_done, n - 1)
                r = 32 * (q0 + q)
                e.matmul(FB[n % 2], M.ONES[r:r + 1, :], M.MR[r:r + 1, g, :], start=True, stop=True).then_inc(s.gb_full, 1)
        e.wait_ge(M.ada.mc, 3)
        for k in range(4):
            e.wait_ge(M.ada.r_in[(27 + k) % R_SLOTS], 16 * ((27 + k) // R_SLOTS) + 16)
        for n4 in range(4):
            t, q = divmod(n4, 2)
            for k in range(KT):
                slot = (27 + k // 2) % R_SLOTS
                w = M.R[:, SR * slot + D * (k % 2):SR * slot + D * (k % 2) + D]
                mm = e.matmul(PS[:, n4, :], M.mix_OT[:, k, 128 * t:128 * t + 128], w[:, 512 * q:512 * q + 512],
                              start=k == 0, stop=k == KT - 1)
            mm.then_inc(s.y_done, 1)

    return sync, act, pool, dve, pe


def experts(nc, M, A):
    e, a, v, sp, p, s = nc.tensor, nc.scalar, nc.vector, nc.sync, nc.gpsimd, M.moe
    PS, TRB, XN = M.PS, M.TRB, M.XN
    GB, UB = PS[:, 0, :], PS[:, 1, :]
    N_SLOTS = 6
    SLOTS = [M.R[:, SR * q:SR * q + SR] for q in range(R_SLOTS)] + [M.RAW[:, 0, 0:SR]]
    NL = N_GROUPS + EXPERTS
    lg = M.LG.rearrange("p (t n) -> p t n", t=NT)
    KEY, CW = M.KEY, M.CW
    gate, up = (w.rearrange("(g e) (c k p) n -> g c p e k n", e=2, k=2, p=128) for w in (A["w_gate"], A["w_up"]))
    down = A["w_down"].rearrange("(g e) (c p) n -> g c p e n", e=2, p=128)

    def passes(first, end):
        s = M.steps

        def load(g, m):
            slot = m % N_SLOTS
            for x in range(2):
                if m < 8:
                    dst = SLOTS[slot].rearrange("p (e k n) -> p e k n", e=2, k=2)[:, x]
                    src = (gate, up)[m // 4][bass.ds(g, 1), m % 4, :, x].rearrange("g p k n -> p (g k) n")
                else:
                    dst = SLOTS[slot].rearrange("p (e n) -> p e n", e=2)[:, x]
                    src = down[bass.ds(g, 1), m - 8, :, x].rearrange("g p n -> p (g n)")
                sp.dma_start(dst, src).then_inc(s.w_in[slot], 16)

        def step_loads(g, r):
            for m in range(12):
                sp.wait_ge(s.used[m % N_SLOTS], g * 2 + (2 * PAIR_STEPS * r + m // N_SLOTS))
                load(g, m)

        def sync():
            if first == 0:
                for m in range(12):
                    if m in (0, 2):
                        sp.wait_ge(M.mix.y_done, 4)
                    if m >= N_SLOTS:
                        sp.wait_ge(s.used[m % N_SLOTS], 1)
                    load(0, m)
                with sp.Fori(1, PAIR_STEPS) as g:
                    step_loads(g, 0)
            else:
                for r in range(1, ROUNDS):
                    with sp.Fori(0, PAIR_STEPS) as g:
                        step_loads(g, r)

        def gathered(it):
            for k in range(KT):
                if k % 4 == 0:
                    a.wait_ge(s.xg_full, it * 8 + (k + 4))
                a.activation(M.XG[:, k], PS[:, 4 + k // 4, 128 * (k % 4):128 * (k % 4) + 128], ACT.Identity,
                             scale=M.MSC[:, 2, k:k + 1], bias=M.SH2[:, k:k + 1]).then_inc(s.xg_done, 1)

        def silu(it):
            a.wait_ge(s.used[7 % N_SLOTS], it * 2 + 2)
            a.activation(M.SGM, GB, ACT.Silu).then_inc(s.silu, 1)

        def turned(it):
            a.wait_ge(s.ht_full, it + 1)
            a.activation(M.HT, PS[:, 6, :], ACT.Copy).then_inc(s.ht_done, 1)
            a.wait_ge(s.cm_full, it + 1)
            a.activation(M.CM, PS[:, 7, 0:T], ACT.Copy).then_inc(s.cm_done, 1)

        def y_out(it):
            a.wait_ge(s.used[11 % N_SLOTS], it * 2 + 2)
            a.activation(M.YS, PS[:, 2:4, :].rearrange("p a n -> p (a n)"), ACT.Copy).then_inc(s.y_done, 1)

        def act():
            gathered(first)
            silu(first)
            gathered(first + 1)
            turned(first)
            y_out(first)
            with a.Fori(first + 1, end - 1) as it:
                silu(it)
                gathered(it + 1)
                turned(it)
                y_out(it)
            silu(end - 1)
            turned(end - 1)
            y_out(end - 1)

        def hot(it, weighted):
            sem, dst = (s.ohc, M.OHC) if weighted else (s.oh, M.OH)
            for t in range(NT):
                for x in range(2):
                    col = bass.ds(it * 2 + x, 1)
                    out = dst[:, t, CAP * x:CAP * x + CAP]
                    if weighted:
                        m = v.tensor_scalar(out, M.IOTA, KEY[:, t, col], CW[:, t, col], ALU.is_equal, ALU.mult)
                    else:
                        m = v.tensor_scalar(out, M.IOTA, KEY[:, t, col], None, ALU.is_equal)
                    m.then_inc(sem, 1)

        def hidden(it):
            v.wait_ge(s.silu, it + 1)
            v.tensor_tensor(M.HM, M.SGM, UB, ALU.mult).then_inc(s.h_done, 1)

        def accumulate(it):
            for c in range(4):
                v.wait_ge(s.sc_full, it * 4 + (c + 1))
                ys = M.YACC[:, c // 2, 512 * (c % 2):512 * (c % 2) + 512]
                v.tensor_tensor(ys, PS[:, 6 + c % 2, :], ys, ALU.add).then_inc(s.acc, 1)

        def dve():
            hot(first, False)
            v.wait_ge(s.xg_full, 8 * first + 8)
            hot(first + 1, False)
            hot(first, True)
            hidden(first)
            with v.Fori(first + 1, end - 1) as it:
                v.wait_ge(s.xg_full, it * 8 + 8)
                hot(it + 1, False)
                v.wait_ge(s.cm_full, it)
                hot(it, True)
                accumulate(it - 1)
                hidden(it)
            it = end - 1
            v.wait_ge(s.cm_full, it)
            hot(it, True)
            accumulate(it - 1)
            hidden(it)
            accumulate(it)
            v.wait_ge(s.acc, 4 * end)

        def gather(it):
            e.wait_ge(s.oh, it * 4 + 4)
            at_least(e, s.xg_done, it * 8)
            for k in range(KT):
                for t in range(NT):
                    m = e.matmul(PS[:, 4 + k // 4, 128 * (k % 4):128 * (k % 4) + 128], XN[:, t, 128 * k:128 * k + 128],
                                 M.OH[:, t], start=t == 0, stop=t == 1)
                m.then_inc(s.xg_full, 1)

        def gate_up(it):
            e.wait_ge(s.xg_done, it * 8 + 8)
            at_least(e, s.h_done, it)
            for m in range(8):
                slot = m % N_SLOTS
                e.wait_ge(s.w_in[slot], it * 64 + (32 * (m // N_SLOTS) + 32))
                w = SLOTS[slot].rearrange("p (e k n) -> p e k n", e=2, k=2)
                for kk in range(2):
                    k = 2 * (m % 4) + kk
                    for x in range(2):
                        mm = e.matmul((GB, UB)[m // 4][CAP * x:CAP * x + CAP], M.XG[:, k, CAP * x:CAP * x + CAP],
                                      w[:, x, kk, :], start=k == 0, stop=k == KT - 1)
                mm.then_inc(s.used[slot], 1)

        def scatter(it):
            e.wait_ge(s.y_done, it + 1)
            e.wait_ge(s.cm_done, it + 1)
            for c in range(4):
                if c >= 2:
                    e.wait_ge(s.acc, it * 4 + (c - 1))
                e.matmul(PS[:, 6 + c % 2, :], M.CM[:, 128 * (c // 2):128 * (c // 2) + 128],
                         M.YS[:, 512 * (c % 2):512 * (c % 2) + 512], start=True, stop=True).then_inc(s.sc_full, 1)

        def turn(it):
            e.wait_ge(s.h_done, it + 1)
            at_least(e, s.acc, it * 4)
            for f in range(4):
                m = e.transpose(PS[:, 6, 128 * f:128 * f + 128], M.HM[:, 128 * f:128 * f + 128], M.ID[:])
            m.then_inc(s.ht_full, 1)
            e.wait_ge(s.ohc, it * 4 + 4)
            for t in range(NT):
                m = e.transpose(PS[:, 7, 128 * t:128 * t + 128], M.OHC[:, t], M.ID[:])
            m.then_inc(s.cm_full, 1)

        def down_product(it):
            e.wait_ge(s.ht_done, it + 1)
            at_least(e, s.y_done, it)
            for f in range(4):
                slot = (8 + f) % N_SLOTS
                e.wait_ge(s.w_in[slot], it * 64 + 64)
                w = SLOTS[slot].rearrange("p (e n) -> p e n", e=2)
                for q in range(2):
                    for x in range(2):
                        mm = e.matmul(PS[CAP * x:CAP * x + CAP, 2 + q, :],
                                      M.HT[:, 128 * f + CAP * x:128 * f + CAP * x + CAP],
                                      w[:, x, 512 * q:512 * q + 512], start=f == 0, stop=f == 3)
                mm.then_inc(s.used[slot], 1)

        def pe():
            gather(first)
            gate_up(first)
            gather(first + 1)
            turn(first)
            down_product(first)
            with e.Fori(first + 1, end - 1) as it:
                gate_up(it)
                scatter(it - 1)
                gather(it + 1)
                turn(it)
                down_product(it)
            it = end - 1
            gate_up(it)
            scatter(it - 1)
            turn(it)
            down_product(it)
            scatter(it)

        return sync, act, dve, pe

    sync1, act1, dve1, pe1 = passes(0, PAIR_STEPS)
    sync2, act2, dve2, pe2 = passes(PAIR_STEPS, ROUNDS * PAIR_STEPS)

    def other_rounds(eng, steps):
        eng.wait_ge(M.steps.acc, 4 * PAIR_STEPS)
        eng.wait_ge(s.counted, 1)
        left = eng.value_load(M.FLAG[0:1, 0:1], min_val=0, max_val=1)
        with eng.If(left > 0):
            steps()

    def sync():
        sync1()

        def steps():
            sync2()
            for q in range(N_SLOTS):
                sp.wait_ge(M.steps.used[q], 2 * ROUNDS * PAIR_STEPS)
        other_rounds(sp, steps)
        sp.dma_start(M.NFR, A["norm_final"]).then_inc(s.nf_in, 16)

    def act():
        a.wait_ge(M.mix.xu, 8)
        for t in range(NT):
            a.wait_ge(M.mix.sq, 4 + t)
            a.activation(M.m_JUNK, M.X[:, t], ACT.Square, accum_out=M.SS[:, t:t + 1]).then_inc(M.mix.sq, 1)
        a.wait_ge(s.ge, 1)
        a.activation(M.GE, M.GE, ACT.Exp).then_inc(s.ex, 1)
        a.wait_ge(s.ed, 1)
        a.activation(M.ED, M.ED, ACT.Exp).then_inc(s.ex, 1)
        act1()
        other_rounds(a, act2)
        a.wait_ge(s.fin, 4)
        for t in range(NT):
            a.wait_ge(M.mix.sq, 4 + NT + t)
            a.activation(M.m_JUNK, M.X[:, t], ACT.Square, accum_out=M.SS[:, t:t + 1]).then_inc(M.mix.sq, 1)

    def pool():
        for n in range(2):
            p.wait_ge(M.mix.sq, 4 + NT * (n + 1))
            p.tensor_scalar(M.RS[:], M.SS[:], 1 / D, EPS, ALU.mult, ALU.add).then_inc(M.mix.rs, 1)
            p.wait_ge(M.mix.rs, 2 * n + 3)
            p.tensor_tensor(M.RS[:], M.RS[:], M.HF[:, 0:NT], ALU.pow).then_inc(M.mix.rs, 1)

    def dve():
        n = Chain(v, s.rt)
        mc = M.MC[:].rearrange("p (f w) -> p f w", w=2)
        v.wait_ge(M.mix.xu, 8)
        v.wait_ge(M.ada.mc, 3)
        n.add(v.scalar_tensor_tensor(M.MSC[:, 2], mc[:, 32:40, 0], 1.0, M.GC[:, GC_N2:GC_N2 + 8], ALU.add, ALU.mult))
        n.add(v.tensor_copy(M.SH2[:], mc[:, 24:32, 0]))
        v.wait_ge(M.mix.rs, 4)
        for t in range(NT):
            n.add(v.tensor_scalar(XN[:, t], M.X[:, t], M.RS[:, t:t + 1], None, ALU.mult))
        n.wait()
        for k in range(KT):
            v.wait_ge(M.mix.turned, KT + k // 2 + 1)
            v.tensor_scalar(M.XT2[:, k], TRB[k // 2 % 2][:, T * (k % 2):T * (k % 2) + T], M.MSC[:, 2, k:k + 1],
                            M.SH2[:, k:k + 1], ALU.mult, ALU.add).then_inc(M.mix.tm, 1)
        v.wait_ge(s.lg_full, 1)
        n.add(v.tensor_copy(M.LG, PS[:, 0, 0:NT * NL]))
        n.wait()
        gl, el = lg[:, :, 0:N_GROUPS], lg[:, :, N_GROUPS:]
        MX = M.MX
        by_tile = lambda ap: ap.rearrange("p (t n) -> p t n", t=NT)
        GE, OHG, T4 = by_tile(M.GE), by_tile(M.OHG), by_tile(M.T4)
        EM, T32, OH1, OH2, ED = by_tile(M.EM), by_tile(M.T32), by_tile(M.OH1), by_tile(M.OH2), M.ED
        over = lambda col, w: col.unsqueeze(2).broadcast_to([128, NT, w])
        row = lambda r, w: r.unsqueeze(1).broadcast_to([128, NT, w])

        def step(ins):
            n.add(ins)
            n.wait()

        def first_largest(x, mx, hot, tmp, w):
            step(v.tensor_reduce(mx, x, axis=AX.X, op=ALU.max))
            step(v.tensor_tensor(tmp, x, over(mx, w), ALU.is_equal))
            step(v.tensor_tensor(tmp, tmp, row(M.DESC[:, EXPERTS - w:EXPERTS], w), ALU.mult))
            step(v.tensor_reduce(M.PK, tmp, axis=AX.X, op=ALU.max))
            step(v.tensor_tensor(hot, tmp, over(M.PK, w), ALU.is_equal))

        first_largest(gl, MX[:, 0:2], OHG, T4, N_GROUPS)
        v.tensor_tensor(GE, gl, over(MX[:, 0:2], N_GROUPS), ALU.subtract).then_inc(s.ge, 1)
        step(v.tensor_scalar(T4, OHG, -FAR, FAR, ALU.mult, ALU.add))
        for t in range(NT):
            group = lambda ap: ap[:, t].unsqueeze(2).broadcast_to([128, N_GROUPS, EPG])
            expert = lambda ap: ap[:, t].rearrange("p (g e) -> p g e", e=EPG)
            step(v.tensor_tensor(expert(EM), expert(el), group(OHG), ALU.mult))
            step(v.tensor_tensor(expert(EM), expert(EM), group(T4), ALU.add))
        first_largest(EM, MX[:, 2:4], OH1, T32, EXPERTS)
        step(v.scalar_tensor_tensor(EM, OH1, 2 * FAR, EM, ALU.mult, ALU.add))
        first_largest(EM, MX[:, 4:6], OH2, T32, EXPERTS)
        v.tensor_tensor(ED, MX[:, 4:6], MX[:, 2:4], ALU.subtract).then_inc(s.ed, 1)
        v.tensor_tensor(EM, OH1, OH2, ALU.add).then_inc(s.sel, 1)
        v.wait_ge(s.ex, 1)
        step(v.tensor_reduce(M.GW, GE, axis=AX.X, op=ALU.add))
        step(v.reciprocal(M.GW, M.GW))
        v.wait_ge(s.ex, 2)
        step(v.tensor_scalar(M.P1, ED, 1.0, None, ALU.add))
        step(v.reciprocal(M.P1, M.P1))
        step(v.tensor_tensor(M.P1, M.P1, M.GW, ALU.mult))
        step(v.tensor_tensor(M.P2, M.P1, ED, ALU.mult))
        n.add(v.tensor_tensor(OH1, OH1, over(M.P1, EXPERTS), ALU.mult))
        n.add(v.tensor_tensor(OH2, OH2, over(M.P2, EXPERTS), ALU.mult))
        n.wait()
        step(v.tensor_tensor(OH1, OH1, OH2, ALU.add))
        v.wait_ge(s.rk_full, 1)
        step(v.tensor_reduce(M.CNT, PS[0:1, 1, 64:96], axis=AX.X, op=ALU.max))
        v.tensor_scalar(M.FLAG[0:1, 0:1], M.CNT, float(CAP), None, ALU.is_gt).then_inc(s.counted, 1)
        v.wait_ge(s.sel, 1)
        step(v.tensor_scalar(T32, by_tile(PS[:, 1, 0:64]), 1.0, None, ALU.add))
        step(v.tensor_tensor(T32, T32, EM, ALU.mult))
        for r in range(ROUNDS):
            n.add(v.tensor_scalar(KEY[:, :, 32 * r:32 * r + 32], T32, -(1.0 + CAP * r), None, ALU.add))
            n.add(v.tensor_copy(CW[:, :, 32 * r:32 * r + 32], OH1))
        n.add(v.memset(M.YACC[:], 0.0))
        n.wait()
        dve1()
        other_rounds(v, dve2)
        v.wait_ge(M.mix.gb_done, 4)
        for t in range(NT):
            v.tensor_tensor(M.YACC[:, t], M.YACC[:, t], M.G2B, ALU.mult).then_inc(s.fin, 1)
        v.wait_ge(s.fin, 2)
        for t in range(NT):
            v.tensor_tensor(M.X[:, t], M.YACC[:, t], M.X[:, t], ALU.add).then_inc(s.fin, 1)
        v.wait_ge(M.mix.rs, 6)
        v.wait_ge(s.nf_in, 16)
        for t in range(NT):
            v.scalar_tensor_tensor(M.X[:, t], M.X[:, t], M.RS[:, t:t + 1], M.NFR, ALU.mult, ALU.mult).then_inc(M.x_ready, 2)

    def pe():
        e.wait_ge(s.rt, 4)
        for b in range(4):
            if b > 1:
                e.wait_ge(M.mix.tm, 2 * KT + 2 * (b - 1))
            for kk in range(2):
                for t in range(NT):
                    k = 2 * b + kk
                    m = e.transpose(TRB[b % 2][:, T * kk + 128 * t:T * kk + 128 * t + 128],
                                    XN[:, t, 128 * k:128 * k + 128], M.ID[:])
            m.then_inc(M.mix.turned, 1)
        e.wait_ge(M.mix.tm, 3 * KT)
        e.wait_ge(M.small2, 64)
        for t in range(NT):
            for k in range(KT):
                e.matmul(PS[:, 0, NL * t:NL * t + NL], M.XT2[:, k, 128 * t:128 * t + 128], M.WR[:, k, :],
                         start=k == 0, stop=False)
            m = e.matmul(PS[:, 0, NL * t:NL * t + NL], M.ONES[0:1, :], M.BR[0:1, :], start=False, stop=True)
        m.then_inc(s.lg_full, 1)
        e.wait_ge(s.sel, 1)
        EM = M.EM.rearrange("p (t n) -> p t n", t=NT)
        for t in range(NT):
            out = PS[:, 1, 32 * t:32 * t + 32]
            e.matmul(out, M.UPPER[:], EM[:, t], start=True, stop=t == 0)
            if t:
                e.matmul(out, M.ONES[:], EM[:, 0], start=False, stop=True)
        for t in range(NT):
            m = e.matmul(PS[0:1, 1, 64:96], M.ONES[:, 0:1], EM[:, t], start=t == 0, stop=t == 1)
        m.then_inc(s.rk_full, 1)
        e.wait_ge(M.mix.gb_done, 4)
        pe1()
        other_rounds(e, pe2)

    return sync, act, pool, dve, pe


def program(nc, A, out):
    with ExitStack() as c:
        M = Names()

        def sb(name, shape, dtype=f32):
            return c.enter_context(nc.sbuf_tensor(name, shape, dtype))

        def sem(name):
            return c.enter_context(nc.semaphore(name))

        def sems(prefix, names):
            return [sem(prefix + n) for n in names.split()]

        def for_each(n_buffers, prefix, names):
            return [[sem(f"{prefix}{n}{b}") for b in range(n_buffers)] for n in names.split()]

        M.X = sb("X", [128, NT, D])
        M.ID = sb("ID", [128, 128])
        M.GC = sb("GC", [128, N_GC])
        M.XH, M.XL = sb("XH", [128, KT, T], f32r), sb("XL", [128, KT, T], f32r)
        M.RAW = sb("RAW", [128, 2, SLOT])
        M.HI, M.LO = sb("HI", [128, 2, SLOT], f32r), sb("LO", [128, 2, SLOT], f32r)
        M.R = sb("R", [128, 11776])
        M.MASK = sb("MASK", [128, N_MASK])
        M.ROPE_A, M.ROPE_B = sb("ROPE_A", [128, NT, 2, 2, AD]), sb("ROPE_B", [128, NT, 2, B_QK + B_ROPE])
        M.SS, M.RS, M.HF = sb("SS", [128, NT]), sb("RS", [128, NT]), sb("HF", [128, 12])
        M.HG, M.FREQ = sb("HG", [128, 320]), sb("FREQ", [128, 48])
        M.POS, M.POSF = sb("POS", [128, NT], i32), sb("POSF", [128, NT])
        M.SSH, M.RSH, M.SSB, M.RSB = sb("SSH", [128, 12]), sb("RSH", [128, 12]), sb("SSB", [128, 4]), sb("RSB", [128, 4])
        M.SS4, M.RS4 = M.SSB, M.RSB
        stats = sb("STATS", [128, 6])
        M.NM, M.SM, M.RC = ([stats[:, 2 * n + t:2 * n + t + 1] for t in range(NT)] for n in range(3))
        M.HH, M.HL = sb("HH", [128, 2, T], f32r), sb("HL", [128, 2, T], f32r)
        M.FLAG = sb("FLAG", [1, 1], i32)

        ARENA = 12544
        arena = sb("ARENA", [128, ARENA])
        end = [0]

        def carve(*shape, at=None):
            n = math.prod(shape)
            start = end[0] if at is None else at
            end[0] = start + n
            assert end[0] <= ARENA
            ap = arena[:, start:start + n]
            if len(shape) == 2:
                return ap.rearrange("p (a b) -> p a b", a=shape[0])
            if len(shape) == 3:
                return ap.rearrange("p (a b c) -> p a b c", a=shape[0], b=shape[1])
            if len(shape) == 4:
                return ap.rearrange("p (a b c d) -> p a b c d", a=shape[0], b=shape[1], c=shape[2])
            return ap

        M.WF = carve(2, FH, at=11268)
        M.MC, M.CRAW, M.CS = carve(96), carve(KT, 2), carve(KT, 2)
        M.MSC, M.SH2, M.ONES = carve(3, KT), carve(KT), carve(128)
        M.WR, M.BR = carve(KT, N_GROUPS + EXPERTS), carve(N_GROUPS + EXPERTS)
        M.DFT = M.MASK[:, 0:1280]
        M.UPPER, M.IOTA, M.DESC = M.MASK[:, 1280:1408], M.MASK[:, 1408:1472], M.MASK[:, 1472:1504]
        M.MR = M.R[:, R_SLOTS * SR:R_SLOTS * SR + 1536].rearrange("p (g n) -> p g n", g=3)
        tm = carve(4, T, at=0)
        M.TM = [tm[:, k] for k in range(4)]
        M.JUNK1 = carve(D)
        M.r_ANG, M.r_TURNS, M.r_CS = carve(NT, 48), carve(2, NT, 48), carve(2, NT, 48)
        M.QT0, M.KT0, M.V0 = carve(4, T, at=0), carve(4, 2 * T), carve(4, 512)
        M.FT, M.BT, M.CT0, M.HT0 = carve(2, T), carve(2, T), carve(2, T), carve(2, T)
        M.XN, M.CX = carve(NT, D), carve(NT, D)
        M.mix_XN = M.XN
        M.mix_OT = carve(KT, T, at=7168)
        M.n_SC = [carve(512), carve(512)]
        M.n_PT = [carve(512), carve(512)]
        M.FA, M.FOT, M.CHP = carve(2, 512, at=9216), carve(512), carve(2, T + 2)
        M.G2B, M.G1B = carve(D, at=0), carve(D)
        M.TMPX = [carve(512), carve(512)]
        beside = [M.RAW[:, n // 2, SR + 512 * (n % 2):SR + 512 * (n % 2) + 512] for n in range(4)]
        M.BIAS = beside
        M.BIASZ = M.RAW[:, :, SR:].rearrange("p a (b n) -> p a b n", b=2)[:, :, :, T:]
        M.moe_XN = carve(NT, D, at=1024)
        M.XT2 = carve(KT, T)
        M.YACC = carve(NT, D, at=3072)
        M.XG, M.SGM, M.HM, M.HT, M.CM, M.YS = carve(KT, 128), carve(512), carve(512), carve(512), carve(T), carve(D)
        M.m_JUNK = M.YS
        M.OH, M.OHC = carve(NT, 128), carve(NT, 128)
        M.NFR = carve(D)
        M.KEY, M.CW = carve(NT, KEYS), carve(NT, KEYS)
        M.LG = carve(NT * (N_GROUPS + EXPERTS), at=5120)
        M.GE, M.OHG, M.T4 = carve(8), carve(8), carve(8)
        M.EM, M.T32, M.OH1, M.OH2 = carve(64), carve(64), carve(64), carve(64)
        M.MX, M.PK, M.ED, M.GW, M.P1, M.P2 = carve(6), carve(2), carve(2), carve(2), carve(2), carve(2)
        M.CNT = carve(1)[0:1]
        xn = carve(NT, D, at=0)
        ot = carve(KT, T, at=0)
        base = end[0]
        junk, M.SG, M.H = carve(D), carve(2, T), carve(2, T)
        M.SC, M.PT = [carve(384, at=base), carve(768)], [carve(384), carve(384)]
        base = end[0]
        M.a_QK, M.a_SQ, M.a_QR = carve(NT, 2, AW), carve(2, AW), carve(NT, 2, AW)
        M.a_QT, M.a_KT, M.a_V = carve(2, GROUPS, T), carve(2, GROUPS, T), carve(2, NT, AW)
        M.b_C, M.b_CT = carve(NT, B_IN, at=base), carve(5, T)
        M.b_QK, M.b_SQ, M.b_QR = carve(NT, 4, B_QK), carve(4, B_QK), carve(NT, 4, B_QK)
        M.b_QKT, M.b_V = carve(2, 4, T)[0:B_QK], carve(2, NT, 2, B_V)
        M.PS = c.enter_context(nc.psum_tensor("PS", [128, 8, 512], f32))
        M.TRB = M.PTB = [M.PS[:, 6, :], M.PS[:, 7, :]]
        M.OB = M.PS[:, 5, 0:T]

        (M.x_ready, M.squared, M.turned, M.xh_done, M.xl_done, M.rstd, M.xn_done, M.small_in) = \
            sems("", "x_ready squared turned xh_done xl_done rstd xn_done small_in")
        M.small2, M.ones_set, M.mask_in, M.out_written = sems("", "small2 ones_set mask_in out_written")
        M.att = Names()
        (M.att.sc_full, M.att.sc_read, M.att.exp_done, M.att.recip, M.att.p_ready, M.att.pt_full, M.att.pt_done, M.att.pv_done) = \
            sems("t_", "sc_full sc_read exp_done recip p_ready pt_full pt_done pv_done")
        M.att.o_free, = sems("t_", "o_free")
        M.ffn = Names()
        M.ffn.y_done, = sems("f_", "y_done")
        (M.ffn.gu_in, M.ffn.dn_in, M.ffn.gu_hi, M.ffn.gu_lo, M.ffn.dn_hi, M.ffn.dn_lo, M.ffn.gu_used, M.ffn.dn_used) = \
            for_each(2, "f_", "gu_in dn_in gu_hi gu_lo dn_hi dn_lo gu_used dn_used")
        M.ffn.silu, M.ffn.h_done, M.ffn.hh_done, M.ffn.hl_done = for_each(2, "f_", "silu h_done hh_done hl_done")
        M.dil = Names()
        (M.dil.y_done, M.dil.wo_in, M.dil.fb_full, M.dil.fb_free, M.dil.nr, M.dil.rs) = \
            sems("a_", "y_done wo_in fb_full fb_free nr rs")
        M.dil.w_in, M.dil.w_hi, M.dil.w_lo = for_each(2, "a_", "w_in w_hi w_lo")
        M.lat = Names()
        (M.lat.y_done, M.lat.wo_in, M.lat.fb_full, M.lat.fb_free, M.lat.nr, M.lat.rs, M.lat.c_full, M.lat.c_out) = \
            sems("b_", "y_done wo_in fb_full fb_free nr rs c_full c_out")
        M.lat.ct_full, M.lat.ct_done, M.lat.c_rs, M.lat.cn, M.lat.wq_in = sems("b_", "ct_full ct_done c_rs cn wq_in")
        M.rope = Names()
        M.rope.ch, M.rope.reduced, M.rope.sines = sems("r_", "ch reduced sines")
        M.ada = Names()
        M.ada.cs, M.ada.mr, M.ada.mt, M.ada.mc = sems("d_", "cs mr mt mc")
        M.ada.r_in, M.ada.r_used = for_each(R_SLOTS, "d_", "r_in r_used")
        M.mix = Names()
        (M.mix.c_in, M.mix.x_in, M.mix.sq, M.mix.rs, M.mix.ch, M.mix.turned, M.mix.tm, M.mix.xh) = \
            sems("m_", "c_in x_in sq rs ch turned tm xh")
        (M.mix.xl, M.mix.fb_full, M.mix.fb_free, M.mix.fo_full, M.mix.fo_done, M.mix.zeroed, M.mix.y_done, M.mix.xu) = \
            sems("m_", "xl fb_full fb_free fo_full fo_done zeroed y_done xu")
        M.mix.gb_full, M.mix.gb_done = sems("m_", "gb_full gb_done")
        M.mix.w_in, M.mix.w_hi, M.mix.w_lo = for_each(2, "m_", "w_in w_hi w_lo")
        M.lat.w_in, M.lat.w_hi, M.lat.w_lo = M.dil.w_in, M.mix.w_hi, M.mix.w_lo
        M.mix.bias_in, = for_each(4, "m_", "bias_in")
        M.moe = Names()
        (M.moe.ge, M.moe.ed, M.moe.ex, M.moe.sel, M.moe.counted, M.moe.rt, M.moe.lg_full, M.moe.rk_full) = \
            sems("e_", "ge ed ex sel counted rt lg_full rk_full")
        M.moe.nf_in, M.moe.fin = sems("e_", "nf_in fin")
        M.steps = Names()
        (M.steps.oh, M.steps.xg_full, M.steps.xg_done, M.steps.silu, M.steps.h_done, M.steps.ht_full, M.steps.ht_done, M.steps.cm_full) = \
            sems("s_", "oh xg_full xg_done silu h_done ht_full ht_done cm_full")
        (M.steps.cm_done, M.steps.ohc, M.steps.y_done, M.steps.sc_full, M.steps.acc) = \
            sems("s_", "cm_done ohc y_done sc_full acc")
        M.steps.w_in, M.steps.used = for_each(6, "s_", "w_in used")
        M.passed = sem("passed")
        M.n_small = 16 * 5

        def after_experts(sp, j):
            if j == 0:
                sp.wait_ge(M.steps.used[5], 2 * PAIR_STEPS)
            else:
                sp.wait_ge(M.mix.w_lo[1], 5)
                for n in range(2, 4):
                    sp.wait_ge(M.att.sc_read, 16)

        def after_ffn(f):
            def wait(sp, j):
                sp.wait_ge(M.ffn.gu_lo[j], 1 + FF_TWICE * (f + 1))
                sp.wait_ge(M.ffn.dn_lo[j], 1 + FF_TWICE * (f + 1))
            return wait

        def after_dilated(sp, j):
            sp.wait_ge(M.dil.w_lo[j], 12)

        def after_latent(sp, j):
            sp.wait_ge(M.lat.y_done, 4)

        def nothing():
            pass

        M.XN, M.OT, M.JUNK = M.mix_XN, M.mix_OT, M.JUNK1
        mixer = first_mixer(nc, M, A)
        M.XN = M.moe_XN
        moe = experts(nc, M, A)
        M.XN, M.OT, M.JUNK = xn, ot, junk
        rope_act, rope_dve = rope_tables(nc, M)
        phases = []
        n_ffn = 0
        before = after_experts
        for n, kind in enumerate(("ffn", "dilated", "ffn", "ffn", "latent", "ffn")):
            n_act, n_pool, n_dve, n_pe = norm_and_transpose(nc, M, n, KT * n)
            if kind == "ffn":
                sync, act, dve, pe = ffn(nc, M, n_ffn, A["ffn_w_in"][n_ffn // 2, n_ffn % 2], A["ffn_w_out"][n_ffn // 2, n_ffn % 2],
                                         before)
                pool = nothing
                before = after_ffn(n_ffn)
                n_ffn += 1
            elif kind == "dilated":
                sync, act, pool, dve, pe = dilated(nc, M, A["a_w_in"], A["a_w_out"], before)
                before = after_dilated
            else:
                sync, act, pool, dve, pe = latent(nc, M, A["b_w_in"], A["b_w_q_up"], A["b_w_kv_up"], A["b_w_out"], before)
                before = after_latent
            phases.append((sync, n_act, act, n_pool, pool, n_dve, dve, n_pe, pe))

        block = c.enter_context(nc.Block())

        @block.sync
        def _(sp):
            mixer[0]()
            moe[0]()
            for n, (sync, *_) in enumerate(phases):
                sync()
                if n == 0:
                    sp.wait_ge(M.x_ready, 4)
                    sp.dma_start(M.MASK[:], A["mask"]).then_inc(M.mask_in, 16)
            sp.wait_ge(M.x_ready, 28)
            sp.dma_start(out.rearrange("(t p) n -> p t n", p=128), M.X[:]).then_inc(M.out_written, 16)
            sp.wait_ge(M.out_written, 16)

        @block.scalar
        def _(a):
            for to, what in ((M.POS, A["positions"]), (M.FREQ, A["freq"]), (M.HG, A["head_gains"]), (M.ID, A["identity"]), (M.GC, A["gains"])):
                a.dma_start(to[:], what).then_inc(M.small_in, 16)
            a.dma_start(M.X[:], A["x"].rearrange("(t p) n -> p t n", p=128)).then_inc(M.mix.x_in, 16)
            a.dma_start(M.CX, A["ctx"].rearrange("(t p) n -> p t n", p=128)).then_inc(M.mix.x_in, 16)
            a.dma_start(M.MASK[:, 0:1504], A["constants"]).then_inc(M.small2, 16)
            a.dma_start(M.WF, A["w_fourier"].rearrange("(k p) n -> p k n", p=128)).then_inc(M.small2, 16)
            a.dma_start(M.WR, A["w_router"].rearrange("(k p) n -> p k n", p=128)).then_inc(M.small2, 16)
            a.dma_start(M.BR[0:1], A["b_router"]).then_inc(M.small2, 16)
            rope_act()
            mixer[1]()
            moe[1]()
            for _, norm, act, *_ in phases:
                norm()
                act()

        @block.gpsimd
        def _(p):
            p.memset(M.HF[:], -0.5).then_inc(M.ones_set, 1)
            p.memset(M.ONES, 1.0).then_inc(M.ones_set, 1)
            p.memset(M.MR, 0.0).then_inc(M.ones_set, 1)
            p.wait_ge(M.ones_set, 3)
            mixer[2]()
            moe[2]()
            for _, _, _, norm, pool, *_ in phases:
                norm()
                pool()

        @block.vector
        def _(v):
            rope_dve()
            mixer[3]()
            moe[3]()
            for n, (_, _, _, _, _, norm, dve, _, _) in enumerate(phases):
                norm()
                if n == 1:
                    v.wait_ge(M.mask_in, 16)
                dve()

        @block.tensor
        def _(e):
            e.wait_ge(M.small_in, M.n_small)
            mixer[4]()
            moe[4]()
            for *_, norm, pe in phases:
                norm()
                pe()


def kernel(**inputs):
    import concourse.bacc as bacc
    from concourse.bass_utils import run_bass_kernel_spmd

    given = {name: np.asarray(value) for name, value in inputs.items()}

    def columns(vector):
        return vector.reshape(-1, 128).T

    def on_all(row):
        return np.broadcast_to(row, (128, row.shape[-1]))

    def two(name):
        return given[name].reshape(given[name].shape[1:])

    zero_or_far = lambda ok: np.where(ok, 0.0, FAR).astype(np.float32)
    q, k = np.arange(T)[:, None], np.arange(T)[None, :]
    gap = q - k
    bands = [zero_or_far((gap >= 0) & (gap % dilation == 0) & (gap <= window)) for window, dilation in ((128, 1), (512, 4), (2048, 16))]
    causal = zero_or_far(gap >= 0)
    mask = np.concatenate([b[:128, :128] for b in bands] + [b[128:] for b in bands] + [causal[:128, :128], causal[128:]], axis=1)
    freq = np.concatenate([10000.0 ** (-np.arange(32) * 2.0 / 64), 10000.0 ** (-np.arange(16) * 2.0 / 32)])
    n64, n256 = np.arange(64), np.arange(T)
    angle64 = 2 * np.pi * ((n64[:, None] * n64[None, :]) % 64) / 64
    angle256 = 2 * np.pi * ((n256[:, None] * n256[None, :]) % T) / T
    both = lambda m: np.kron(np.eye(2), m)
    tiles = lambda m: m.reshape(NT, 128, T).transpose(1, 0, 2).reshape(128, NT * T)
    norm = 1 / math.sqrt(64 * T)
    constants = np.concatenate([both(np.cos(angle64)), both(np.sin(angle64)), tiles(np.cos(angle256) * norm),
                                tiles(-np.sin(angle256) * norm), np.triu(np.ones((128, 128)), 1),
                                on_all(np.arange(64.0)[None]), on_all(np.arange(32.0, 0.0, -1.0)[None])], axis=1)
    row, col = n256 // 64, n256 % 64
    start = np.clip(col - 8, 0, 64 - 16)[:, None]
    inside = (col[None, :] >= start) & (col[None, :] < start + 16)
    bias = two("rpb")[:, row[None, :] - row[:, None] + 7, np.clip(col[None, :] - col[:, None] + 15, 0, 30)]
    bias = np.where(inside[None], bias, np.float32(FAR))

    A = dict(
        x=given["x"][0], ctx=given["ctx"][0],
        conditions=np.stack([given["c"][0], given["c_ctx"]], axis=-1).reshape(KT, 128, 2).transpose(1, 0, 2),
        w_ada=two("w_ada"), b_ada=given["b_ada"], w_in=two("w_in"), w_fourier=two("w_fourier"), w_out=two("w_out"),
        w_router=np.concatenate([two("w_rg"), two("w_re")], axis=1),
        b_router=np.concatenate([given["b_rg"], given["b_re"]], axis=1),
        w_gate=two("w_gate"), w_up=two("w_up"), w_down=two("w_down"), norm_final=on_all(given["norm_final"][None]),
        bias=bias, positions=given["positions_2"].reshape(NT, 128).T, freq=on_all(freq.astype(np.float32)[None]),
        head_gains=on_all(np.concatenate([given[n][0] for n in ("a_q_gain_2", "b_q_gain_2", "a_k_gain_2", "b_k_gain_2")])[None]),
        gains=np.concatenate([columns(given[n]) for n in ("norm_gains_2", "norm1", "norm2", "b_q_a_gain_2", "b_kv_a_gain_2",
                                                          "w_conv")], axis=1),
        identity=np.eye(128, dtype=np.float32), constants=constants.astype(np.float32), mask=mask,
        ffn_w_in=given["ffn_w_in_2"], ffn_w_out=given["ffn_w_out_2"], a_w_in=two("a_w_in_2"), a_w_out=two("a_w_out_2"),
        b_w_in=two("b_w_in_2"), b_w_q_up=two("b_w_q_up_2"), b_w_kv_up=two("b_w_kv_up_2"), b_w_out=two("b_w_out_2"),
    )
    nc = bacc.Bacc("TRN2", target_bir_lowering=False, num_devices=1)
    arrays = {name: np.ascontiguousarray(value) for name, value in A.items()}
    handles = {name: nc.dram_tensor(name, value.shape, mybir.dt.from_np(value.dtype), kind="ExternalInput").ap()
               for name, value in arrays.items()}
    out = nc.dram_tensor("out_0_dram", (T, D), f32, kind="ExternalOutput").ap()
    program(nc, handles, out)
    result = run_bass_kernel_spmd(nc, [arrays], core_ids=[0])
    return result.results[0]["out_0_dram"].reshape(1, T, D)
```

```python
import math
from contextlib import ExitStack

import numpy as np
import concourse.bass as bass
from concourse import mybir

ALU = mybir.AluOpType
ACT = mybir.ActivationFunctionType
AX = mybir.AxisListType
f32 = mybir.dt.float32
f32r = mybir.dt.float32r
i32 = mybir.dt.int32

D = 1024
KT = D // 128
T = 256
NT = T // 128
EPS = 1e-6
FF = 2816
FF_TWICE = FF // 256
HEADS = 16
PAIRS = HEADS // 2
GROUPS = 3
AD = 64
AW = GROUPS * 128
B_NOPE, B_ROPE, B_QK, B_V = 64, 32, 96, 64
B_QR, B_KVR = 384, 256
B_IN = B_QR + B_KVR + B_ROPE
SLOT = 3072
MIX_LOADS = 5
MASK_A = [0, 384]
MASK_B = [1152, 1280]
N_MASK = 1536
GC_N1, GC_N2, GC_BA, GC_CONV = 48, 56, 64, 69
N_GC = 75
FAR = -1e30
SR = 2048
R_SLOTS = 5
EXPERTS, N_GROUPS = 32, 4
EPG = EXPERTS // N_GROUPS
CAP = 64
PAIR_STEPS = EXPERTS // 2
ROUNDS = T // CAP
KEYS = ROUNDS * EXPERTS
FH = D // 4


class Names:
    pass


def at_least(eng, sem, value):
    if not isinstance(value, int) or value > 0:
        eng.wait_ge(sem, value)


class Chain:

    def __init__(self, eng, sem, base=0):
        self.eng, self.sem, self.base, self.n = eng, sem, base, 0

    def add(self, ins):
        ins.then_inc(self.sem, 1)
        self.n += 1

    def wait(self):
        self.eng.wait_ge(self.sem, self.base + self.n)


def norm_and_transpose(nc, M, n, g0, first_high, first_low):
    X, XN, SS, RS, GC, XH, XL = M.X, M.XN, M.SS, M.RS, M.GC, M.XH, M.XL
    TRB = [M.PS[:, b, :] for b in (6, 7, 2, 3)]
    a, p, v, e = nc.scalar, nc.gpsimd, nc.vector, nc.tensor

    def act():
        first_high()
        for t in range(NT):
            a.wait_ge(M.x_ready, 4 * n + 2 * t + 2)
            at_least(a, M.squared, NT * n + t)
            a.activation(M.JUNK[:], X[:, t], ACT.Square, accum_out=SS[:, t:t + 1]).then_inc(M.squared, 1)
        for k in range(KT):
            a.wait_ge(M.turned, 4 * n + k // 2 + 1)
            a.activation(XH[:, k], TRB[k // 2][:, T * (k % 2):T * (k % 2) + T], ACT.Copy,
                         scale=GC[:, g0 + k:g0 + k + 1]).then_inc(M.xh_done, 1)

    def pool():
        p.wait_ge(M.squared, NT * (n + 1))
        p.tensor_scalar(RS[:], SS[:], 1 / D, EPS, ALU.mult, ALU.add).then_inc(M.rstd, 1)
        p.wait_ge(M.rstd, 2 * n + 1)
        p.tensor_tensor(RS[:], RS[:], M.HF[:, 0:NT], ALU.pow).then_inc(M.rstd, 1)

    def dve():
        first_low()
        v.wait_ge(M.rstd, 2 * n + 2)
        for t in range(NT):
            v.tensor_scalar(XN[:, t], X[:, t], RS[:, t:t + 1], None, ALU.mult).then_inc(M.xn_done, 1)
        for k in range(KT):
            v.wait_ge(M.xh_done, KT * n + 2 * (k // 2) + 2)
            v.scalar_tensor_tensor(XL[:, k], TRB[k // 2][:, T * (k % 2):T * (k % 2) + T],
                                   GC[:, g0 + k:g0 + k + 1], XH[:, k].bitcast(f32),
                                   ALU.mult, ALU.subtract).then_inc(M.xl_done, 1)

    def pe():
        e.wait_ge(M.xn_done, NT * (n + 1))
        for b in range(4):
            for kk in range(2):
                for t in range(NT):
                    k = 2 * b + kk
                    m = e.transpose(TRB[b][:, T * kk + 128 * t:T * kk + 128 * t + 128],
                                    XN[:, t, 128 * k:128 * k + 128], M.ID[:])
            m.then_inc(M.turned, 1)
    return act, pool, dve, pe


def ffn(nc, M, n_norm, f, w_in, w_out, raw_free):
    XH, XL, X, PS, s = M.XH, M.XL, M.X, M.PS, M.ffn
    Y = PS[:, 0:4, :]
    GU = [PS[:, 4, :], PS[:, 5, :]]
    w_in_v = w_in.rearrange("(k p) n -> p k n", p=128)
    w_out_v = w_out.rearrange("(c p) n -> c p n", p=128)
    u0 = FF_TWICE * f
    a, v, e, sp = nc.scalar, nc.vector, nc.tensor, nc.sync

    def gu(buf, j):
        return buf[:, j, 0:2048].rearrange("p (q k n) -> p q k n", q=2, k=KT)

    def dn(buf, j):
        return buf[:, j, 2048:3072]

    def sync():
        for j in range(2):
            raw_free(sp, j)
        with sp.Fori(0, FF_TWICE) as i:
            for j in range(2):
                sp.wait_ge(s.gu_lo[j], i + (u0 + 1))
                for q in range(2):
                    sp.dma_start(gu(M.RAW, j)[:, q], w_in_v[:, :, bass.ds(i * 256 + (j * 128 + q * FF), 128)]
                                 ).then_inc(s.gu_in[j], 16)
                sp.wait_ge(s.dn_lo[j], i + (u0 + 1))
                sp.dma_start(dn(M.RAW, j), w_out_v[bass.ds(i * 2 + j, 1)].rearrange("a p n -> p (a n)")
                             ).then_inc(s.dn_in[j], 16)

    def gu_high(j, i):
        a.wait_ge(s.gu_in[j], i * 32 + (32 * u0 + 32))
        a.wait_ge(s.gu_used[j], i + (u0 + 1))
        a.activation(M.HI[:, j, 0:2048], M.RAW[:, j, 0:2048], ACT.Copy).then_inc(s.gu_hi[j], 1)

    def gu_low(j, i):
        v.wait_ge(s.gu_hi[j], i + (u0 + 1))
        v.tensor_tensor(M.LO[:, j, 0:2048], M.RAW[:, j, 0:2048], M.HI[:, j, 0:2048].bitcast(f32),
                        ALU.subtract).then_inc(s.gu_lo[j], 1)

    def act():
        def high_parts(j, i, first=False):
            if not first:
                gu_high(j, i)
            a.wait_ge(s.dn_in[j], i * 16 + (16 * u0 + 16))
            a.wait_ge(s.dn_used[j], i + (u0 + 1))
            a.activation(dn(M.HI, j), dn(M.RAW, j), ACT.Copy).then_inc(s.dn_hi[j], 1)

        def silu(j, i):
            a.wait_ge(s.gu_used[j], i + (u0 + 2))
            a.wait_ge(s.h_done[j], i + (u0 + 1))
            a.activation(M.SG[:, j], GU[j][:, 0:T], ACT.Silu).then_inc(s.silu[j], 1)
            a.wait_ge(s.h_done[j], i + (u0 + 2))
            a.activation(M.HH[:, j], M.H[:, j], ACT.Copy).then_inc(s.hh_done[j], 1)

        high_parts(0, 0, first=True)
        high_parts(1, 0)
        silu(0, 0)
        with a.Fori(1, FF_TWICE) as i:
            high_parts(0, i)
            silu(1, i - 1)
            high_parts(1, i)
            silu(0, i)
        silu(1, FF_TWICE - 1)

    def dve():
        def low_parts(j, i, first=False):
            if not first:
                gu_low(j, i)
            v.wait_ge(s.dn_hi[j], i + (u0 + 1))
            v.tensor_tensor(dn(M.LO, j), dn(M.RAW, j), dn(M.HI, j).bitcast(f32),
                            ALU.subtract).then_inc(s.dn_lo[j], 1)

        def hidden(j, i):
            v.wait_ge(s.silu[j], i + (u0 + 1))
            v.wait_ge(s.dn_used[j], i + (u0 + 1))
            v.tensor_tensor(M.H[:, j], M.SG[:, j], GU[j][:, T:2 * T], ALU.mult).then_inc(s.h_done[j], 1)
            v.wait_ge(s.hh_done[j], i + (u0 + 1))
            v.tensor_tensor(M.HL[:, j], M.H[:, j], M.HH[:, j].bitcast(f32), ALU.subtract).then_inc(s.hl_done[j], 1)

        low_parts(0, 0, first=True)
        low_parts(1, 0)
        hidden(0, 0)
        with v.Fori(1, FF_TWICE) as i:
            low_parts(0, i)
            hidden(1, i - 1)
            low_parts(1, i)
            hidden(0, i)
        hidden(1, FF_TWICE - 1)
        for n in range(4):
            v.wait_ge(s.y_done, 4 * f + n + 1)
            xs = X[:, n // 2, 512 * (n % 2):512 * (n % 2) + 512]
            v.scalar_tensor_tensor(xs, Y[:, n], 0.5, xs, ALU.mult, ALU.add).then_inc(M.x_ready, 1)

    def pe():
        def gate_up(j, i, first=False):
            e.wait_ge(s.gu_lo[j], i + (u0 + 2))
            e.wait_ge(s.h_done[j], i + (u0 + 1))
            for q in range(2):
                for k in range(KT):
                    if first and q == 0:
                        e.wait_ge(M.xl_done, KT * n_norm + k + 1)
                    for n, (w, x) in enumerate([(M.HI, XH), (M.HI, XL), (M.LO, XH)]):
                        m = e.matmul(GU[j][:, T * q:T * q + T], gu(w, j)[:, q, k, :], x[:, k, :],
                                     start=(k == 0 and n == 0), stop=(k == KT - 1 and n == 2))
            m.then_inc(s.gu_used[j], 1)

        def down(j, i, first=False, last=False):
            e.wait_ge(s.dn_lo[j], i + (u0 + 2))
            e.wait_ge(s.hl_done[j], i + (u0 + 1))
            for t in range(NT):
                for q in range(2):
                    for n, (h, w) in enumerate([(M.HH, M.HI), (M.HH, M.LO), (M.HL, M.HI)]):
                        m = e.matmul(Y[:, 2 * t + q], h[:, j, 128 * t:128 * t + 128],
                                     dn(w, j)[:, 512 * q:512 * q + 512],
                                     start=first and n == 0, stop=last and n == 2)
                        if last and (t, q, n) == (1, 1, 1):
                            m.then_inc(s.dn_used[j], 1)
                    if last:
                        m.then_inc(s.y_done, 1)
            if not last:
                m.then_inc(s.dn_used[j], 1)

        gate_up(0, 0, first=True)
        gate_up(1, 0)
        down(0, 0, first=True)
        with e.Fori(1, FF_TWICE) as i:
            gate_up(0, i)
            down(1, i - 1)
            gate_up(1, i)
            down(0, i)
        down(1, FF_TWICE - 1, last=True)

    return sync, act, dve, pe, lambda: gu_high(0, 0), lambda: gu_low(0, 0)


class Attention:

    def __init__(self, nc, M, L, softmaxes=0, fills=0, pairs=0):
        self.nc, self.M, self.s, self.L = nc, M, M.att, L
        self.n0, self.f0, self.p0 = softmaxes, fills, pairs
        self.n_fills = 2 * sum(len(x) for x in L.fills)

    def buf(self, h, t):
        return 2 * h + t if self.L.depth == 4 else t

    def softmax_of(self, i, j, h, t):
        return i * 8 + (self.n0 + 4 * j + 2 * h + t)

    def fill_of(self, i, j, h, t):
        half = self.n_fills // 2
        return i * (2 * self.n_fills) + (self.f0 + self.n_fills * j + half * h + (len(self.L.fills[0]) if t else 0))

    def scores(self, i, j, h, t):
        e, s, L = self.nc.tensor, self.s, self.L
        shared = L.shared_bank and (h, t) == (1, 0)
        n = self.softmax_of(i, j, h, t) + shared
        at_least(e, s.sc_read, n + (1 - L.depth))
        for out, lhsT, rhs in L.products(i, j, h, t):
            m = e.matmul(out, lhsT, rhs, start=True, stop=True)
        m.then_inc(s.sc_full, 1)

    def shifted(self, i, j, h, t):
        v, s, L, M = self.nc.vector, self.s, self.L, self.M
        n = self.softmax_of(i, j, h, t)
        v.wait_ge(s.sc_full, n + (2 if L.shared_bank and (h, t) == (1, 0) else 1))
        v.sem_inc(M.passed, 1)
        L.shift(v, i, j, h, t).then_inc(s.sc_read, 1)

    def exponent(self, i, j, h, t):
        a, s, L, M = self.nc.scalar, self.s, self.L, self.M
        w = L.width[t]
        a.wait_ge(s.sc_read, self.softmax_of(i, j, h, t) + 1)
        a.activation(L.SC[self.buf(h, t)][:, 0:w], L.SC[self.buf(h, t)][:, 0:w], ACT.Exp, bias=M.NM[self.buf(h, t)], scale=-1.0,
                     accum_out=M.SM[self.buf(h, t)]).then_inc(s.exp_done, 1)

    def divided(self, i, j, h, t):
        v, s, L, M = self.nc.vector, self.s, self.L, self.M
        n = self.softmax_of(i, j, h, t)
        w = L.width[t]
        v.wait_ge(s.exp_done, n + 1)
        v.reciprocal(M.RC[self.buf(h, t)], M.SM[self.buf(h, t)]).then_inc(s.recip, 1)
        v.wait_ge(s.recip, n + 1)
        v.tensor_scalar(L.SC[self.buf(h, t)][:, 0:w], L.SC[self.buf(h, t)][:, 0:w], M.RC[self.buf(h, t)], None, ALU.mult).then_inc(s.p_ready, 1)

    def weighted(self, i, j, h, t):
        e, s, L, M = self.nc.tensor, self.s, self.L, self.M
        e.wait_ge(s.p_ready, self.softmax_of(i, j, h, t) + 1)
        f0 = self.fill_of(i, j, h, t)
        if h == 0 and t == 0:
            at_least(e, s.o_free, i * 2 + (self.p0 + j))
        parity = (self.n_fills // 2 * h + (len(L.fills[0]) if t else 0)) % 2
        fills = L.fills[t]
        for c, fill in enumerate(fills):
            b = (parity + c) % 2
            at_least(e, s.pt_done, f0 + (c - 1))
            for at, (col, _) in enumerate(fill):
                m = e.transpose(M.PTB[b][:, 128 * at:128 * at + 128], L.SC[self.buf(h, t)][:, col:col + 128], M.ID[:])
            m.then_inc(s.pt_full, 1)
        n_blocks, at_block = sum(len(x) for x in fills), 0
        for c, fill in enumerate(fills):
            b = (parity + c) % 2
            e.wait_ge(s.pt_done, f0 + (c + 1))
            for at, (_, key) in enumerate(fill):
                m = e.matmul(M.OB[64 * h:64 * h + 64, 128 * t:128 * t + 128], L.value(i, j, key, h),
                             L.PT[b][:, 128 * at:128 * at + 128],
                             start=at_block == 0, stop=at_block == n_blocks - 1)
                at_block += 1
            m.then_inc(s.pv_done, 1)

    def turned_out(self, i, j, h, t):
        a, s, L, M = self.nc.scalar, self.s, self.L, self.M
        f0 = self.fill_of(i, j, h, t)
        parity = (self.n_fills // 2 * h + (len(L.fills[0]) if t else 0)) % 2
        for c, fill in enumerate(L.fills[t]):
            b = (parity + c) % 2
            a.wait_ge(s.pt_full, f0 + (c + 1))
            at_least(a, s.pv_done, f0 + (c - 1))
            w = 128 * len(fill)
            a.activation(L.PT[b][:, 0:w], M.PTB[b][:, 0:w], ACT.Copy).then_inc(s.pt_done, 1)

    def output(self, i, j):
        a, s, L, M = self.nc.scalar, self.s, self.L, self.M
        a.wait_ge(s.pv_done, self.fill_of(i, j, 0, 0) + self.n_fills)
        a.activation(L.out(i, j), M.OB, ACT.Copy).then_inc(s.o_free, 1)


def dilated(nc, M, n_norm, w_in, w_out, raw_free):
    s = M.dil
    PS = M.PS
    FB = [PS[:, 0, :], PS[:, 1, :]]
    QK, SQ, QR, QT, KTT, V = M.a_QK, M.a_SQ, M.a_QR, M.a_QT, M.a_KT, M.a_V
    w_in_v = w_in.rearrange("(k p) (q g n) -> p k q g n", p=128, q=3, g=GROUPS)
    v, a, e, sp, p = nc.vector, nc.scalar, nc.tensor, nc.sync, nc.gpsimd

    class L:
        depth, shared_bank = 2, False
        width = [GROUPS * 128, GROUPS * T]
        scores = [PS[:, 2, :], PS[:, 3:5, :].rearrange("p a b -> p (a b)")]
        fills = [[[(128 * g, (0, g)) for g in range(GROUPS)]],
                 [[(T * g + 128 * kt, (kt, g)) for g in range(GROUPS)] for kt in range(NT)]]
        SC, PT = M.SC, M.PT

        @staticmethod
        def out(i, j):
            return M.OT[:, bass.ds(i * 2 + j, 1)].rearrange("p a n -> p (a n)")

        @staticmethod
        def products(i, j, h, t):
            w = 128 * (t + 1)
            return [(L.scores[t][:, g * w:(g + 1) * w], QT[64 * h:64 * h + 64, j, g, 128 * t:128 * t + 128],
                     KTT[64 * h:64 * h + 64, j, g, 0:w]) for g in range(GROUPS)]

        @staticmethod
        def shift(v, i, j, h, t):
            w = L.width[t]
            return v.tensor_tensor_reduce(out=L.SC[t][:, 0:w], in0=L.scores[t][:, 0:w],
                                          in1=M.MASK[:, MASK_A[t]:MASK_A[t] + w], scale=-(AD ** -0.5),
                                          scalar=3.0e38, op0=ALU.add, op1=ALU.min, accum_out=M.NM[t])

        @staticmethod
        def value(i, j, key, h):
            kt, g = key
            return V[:, j, kt, 128 * g + 64 * h:128 * g + 64 * h + 64]

    at = Attention(nc, M, L, softmaxes=16, fills=16, pairs=4)

    def part(buf, slot):
        return buf[:, slot].rearrange("p (k g n) -> p k g n", k=KT, g=GROUPS)

    def chunk(i, j, q):
        c = 3 * j + q
        return c % 2, i * 3 + c // 2

    def load(i, j, q):
        slot, u = chunk(i, j, q)
        at_least(sp, s.w_lo[slot], u)
        for g in range(GROUPS):
            sp.dma_start(part(M.RAW, slot)[:, :, g], w_in_v[:, :, q, g, bass.ds(i * 256 + j * 128, 128)]
                         ).then_inc(s.w_in[slot], 16)

    def high(i, j, q):
        slot, u = chunk(i, j, q)
        a.wait_ge(s.w_in[slot], u * 48 + 48)
        a.activation(M.HI[:, slot], M.RAW[:, slot], ACT.Copy).then_inc(s.w_hi[slot], 1)

    def low(i, j, q):
        slot, u = chunk(i, j, q)
        v.wait_ge(s.w_hi[slot], u + 1)
        v.tensor_tensor(M.LO[:, slot], M.RAW[:, slot], M.HI[:, slot].bitcast(f32),
                        ALU.subtract).then_inc(s.w_lo[slot], 1)

    def project(i, j, q, first=False):
        slot, u = chunk(i, j, q)
        e.wait_ge(s.w_lo[slot], u + 1)
        for t in range(NT):
            at_least(e, s.fb_free, i * 20 + (10 * j + 2 * q + t - 1))
            for k in range(KT):
                if first and t == 0:
                    e.wait_ge(M.xl_done, KT * n_norm + k + 1)
                for n, (x, w) in enumerate([(M.XL, M.HI), (M.XH, M.LO), (M.XH, M.HI)]):
                    m = e.matmul(FB[t][:, 0:AW], x[:, k, 128 * t:128 * t + 128],
                                 part(w, slot)[:, k].rearrange("p g n -> p (g n)"),
                                 start=(k == 0 and n == 0), stop=(k == KT - 1 and n == 2))
            m.then_inc(s.fb_full, 1)

    def project_out(i, j, q):
        slot, u = chunk(i, j, q)
        for t in range(NT):
            a.wait_ge(s.fb_full, i * 20 + (10 * j + 2 * q + t + 1))
            dst = QK[:, t, q] if q < 2 else V[:, j, t]
            a.activation(dst, FB[t][:, 0:AW], ACT.Copy).then_inc(s.fb_free, 1)

    def square_sums(i, j):
        v.wait_ge(s.fb_free, i * 20 + (10 * j + 4))
        n = Chain(v, s.nr, i * 26 + 13 * j)
        at_least(v, s.nr, i * 26 + 13 * j)
        for t in range(NT):
            n.add(v.tensor_tensor(SQ[:], QK[:, t], QK[:, t], ALU.mult))
            n.wait()
            n.add(v.tensor_reduce(M.SSH[:, 12 * t:12 * t + 12], SQ[:].rearrange("p q (h d) -> p (q h) d", d=AD),
                                  axis=AX.X, op=ALU.add))
            if t == 0:
                n.wait()

    def norm_rope(i, j):
        n = Chain(v, s.nr, i * 26 + (13 * j + 4))
        v.wait_ge(s.rs, i * 4 + (2 * j + 2))
        x = QK[:].rearrange("p t q (h d) -> p (t q h) d", d=AD)
        n.add(v.tensor_tensor(x, x, M.RSH[:, 0:24].unsqueeze(2).broadcast_to([128, 24, AD]), ALU.mult))
        n.wait()
        heads = 2 * GROUPS
        for t in range(NT):
            n.add(v.tensor_tensor(QR[:, t].rearrange("p q (h d) -> p q h d", d=AD),
                                  QK[:, t].rearrange("p q (h d) -> p q h d", d=AD),
                                  M.ROPE_A[:, t, 0].unsqueeze(2).broadcast_to([128, 2, heads, AD]), ALU.mult))
            for q in range(2):
                n.add(v.tensor_tensor(SQ[:, q].rearrange("p (h s d) -> p h s d", s=2, d=AD // 2),
                                      QK[:, t, q].rearrange("p (h s d) -> p h s d", s=2, d=AD // 2)[:, :, ::-1, :],
                                      M.ROPE_A[:, t, 1, q].rearrange("p (s d) -> p s d", s=2).unsqueeze(1)
                                      .broadcast_to([128, heads, 2, AD // 2]), ALU.mult))
            n.wait()
            n.add(v.tensor_tensor(QR[:, t], QR[:, t], SQ[:], ALU.add))
            if t == 0:
                n.wait()

    def inverse_rms(i, j):
        p.wait_ge(s.nr, i * 26 + (13 * j + 4))
        p.sem_inc(M.passed, 1)
        p.tensor_scalar(M.RSH[:, 0:24], M.SSH[:, 0:24], 1 / AD, EPS, ALU.mult, ALU.add).then_inc(s.rs, 1)
        p.wait_ge(s.rs, i * 4 + (2 * j + 1))
        p.tensor_tensor(M.RSH[:, 0:24], M.RSH[:, 0:24], M.HF[:, 0:24], ALU.pow).then_inc(s.rs, 1)

    def turn(i, j):
        for t in range(NT):
            e.wait_ge(s.nr, i * 26 + (13 * j + 4 * t + 9))
            for q in range(2):
                at_least(e, s.fb_free, i * 20 + (10 * j + 6 + 2 * t + q - 1))
                for g in range(GROUPS):
                    m = e.transpose(FB[q][:, 128 * g:128 * g + 128], QR[:, t, q, 128 * g:128 * g + 128], M.ID[:])
                m.then_inc(s.fb_full, 1)

    def turn_out(i, j):
        for t in range(NT):
            for q in range(2):
                a.wait_ge(s.fb_full, i * 20 + (10 * j + 6 + 2 * t + q + 1))
                a.activation((QT, KTT)[q][:, j, :, 128 * t:128 * t + 128],
                             FB[q][:, 0:AW].rearrange("p (g n) -> p g n", g=GROUPS), ACT.Copy).then_inc(s.fb_free, 1)

    def sync():
        for j in range(2):
            raw_free(sp, j)
        for q in range(3):
            load(0, 0, q)
        for q in range(3):
            load(0, 1, q)
        sp.wait_ge(M.x_ready, 4)
        for k in range(KT):
            sp.dma_start(M.R[:, D * k:D * k + D], w_out[128 * k:128 * k + 128, :]).then_inc(s.wo_in, 16)
        with sp.Fori(1, PAIRS // 2) as i:
            for j in range(2):
                for q in range(3):
                    load(i, j, q)

    def act():
        def body(i, j, bi, bj, following, first=False):
            if not first:
                turn_out(bi, bj)
                at.exponent(bi, bj, 0, 0)
                at.exponent(bi, bj, 0, 1)
            high(i, j, 1)
            project_out(i, j, 0)
            if not first:
                at.turned_out(bi, bj, 0, 0)
                at.exponent(bi, bj, 1, 0)
            high(i, j, 2)
            project_out(i, j, 1)
            if following:
                high(*following, 0)
            if not first:
                at.turned_out(bi, bj, 0, 1)
                at.exponent(bi, bj, 1, 1)
            project_out(i, j, 2)
            if not first:
                at.turned_out(bi, bj, 1, 0)
                at.turned_out(bi, bj, 1, 1)
                at.output(bi, bj)
        body(0, 0, 0, 0, (0, 1), first=True)
        body(0, 1, 0, 0, (1, 0))
        with a.Fori(1, PAIRS // 2 - 1) as i:
            body(i, 0, i - 1, 1, (i, 1))
            body(i, 1, i, 0, (i + 1, 0))
        i, j = PAIRS // 2 - 1, 1
        body(i, 0, i - 1, 1, (i, 1))
        body(i, 1, i, 0, None)
        turn_out(i, j)
        at.exponent(i, j, 0, 0)
        at.exponent(i, j, 0, 1)
        at.turned_out(i, j, 0, 0)
        at.exponent(i, j, 1, 0)
        at.turned_out(i, j, 0, 1)
        at.exponent(i, j, 1, 1)
        at.turned_out(i, j, 1, 0)
        at.turned_out(i, j, 1, 1)
        at.output(i, j)

    def pool():
        for j in range(2):
            inverse_rms(0, j)
        with p.Fori(1, PAIRS // 2) as i:
            for j in range(2):
                inverse_rms(i, j)

    def dve():
        def body(i, j, bi, bj, following, first=False):
            if not first:
                at.shifted(bi, bj, 0, 0)
                at.shifted(bi, bj, 0, 1)
                at.divided(bi, bj, 0, 0)
                at.divided(bi, bj, 0, 1)
            low(i, j, 1)
            if not first:
                at.shifted(bi, bj, 1, 0)
                at.divided(bi, bj, 1, 0)
            low(i, j, 2)
            square_sums(i, j)
            if not first:
                at.shifted(bi, bj, 1, 1)
            if following:
                low(*following, 0)
            if not first:
                at.divided(bi, bj, 1, 1)
            norm_rope(i, j)
        body(0, 0, 0, 0, (0, 1), first=True)
        body(0, 1, 0, 0, (1, 0))
        with v.Fori(1, PAIRS // 2 - 1) as i:
            body(i, 0, i - 1, 1, (i, 1))
            body(i, 1, i, 0, (i + 1, 0))
        i, j = PAIRS // 2 - 1, 1
        body(i, 0, i - 1, 1, (i, 1))
        body(i, 1, i, 0, None)
        at.shifted(i, j, 0, 0)
        at.shifted(i, j, 0, 1)
        at.divided(i, j, 0, 0)
        at.divided(i, j, 0, 1)
        for t in range(NT):
            at.shifted(i, j, 1, t)
            at.divided(i, j, 1, t)
        add_output(nc, M, s, v)

    def pe():
        def body(i, j, bi, bj, first=False):
            if not first:
                e.wait_ge(s.fb_free, bi * 20 + (10 * bj + 10))
                at.scores(bi, bj, 0, 0)
                at.scores(bi, bj, 0, 1)
            project(i, j, 0, first)
            if not first:
                at.weighted(bi, bj, 0, 0)
                at.scores(bi, bj, 1, 0)
            project(i, j, 1)
            if not first:
                at.weighted(bi, bj, 0, 1)
                at.scores(bi, bj, 1, 1)
            project(i, j, 2)
            if not first:
                at.weighted(bi, bj, 1, 0)
                at.weighted(bi, bj, 1, 1)
            turn(i, j)
        body(0, 0, 0, 0, first=True)
        body(0, 1, 0, 0)
        with e.Fori(1, PAIRS // 2) as i:
            body(i, 0, i - 1, 1)
            body(i, 1, i, 0)
        i, j = PAIRS // 2 - 1, 1
        e.wait_ge(s.fb_free, 20 * i + 20)
        at.scores(i, j, 0, 0)
        at.scores(i, j, 0, 1)
        at.weighted(i, j, 0, 0)
        at.scores(i, j, 1, 0)
        at.weighted(i, j, 0, 1)
        at.scores(i, j, 1, 1)
        at.weighted(i, j, 1, 0)
        at.weighted(i, j, 1, 1)
        output_product(nc, M, s, 12, lambda k: M.R[:, D * k:D * k + D], 16 * KT)

    def first_high():
        a.wait_ge(M.ffn.dn_used[0], FF_TWICE + 1)
        high(0, 0, 0)

    return sync, act, pool, dve, pe, first_high, lambda: low(0, 0, 0)


def output_product(nc, M, s, n_pairs, w, n_loaded):
    e = nc.tensor
    e.wait_ge(M.att.o_free, n_pairs)
    e.wait_ge(s.wo_in, n_loaded)
    for t in range(NT):
        for q in range(2):
            for k in range(KT):
                m = e.matmul(M.PS[:, 2 * t + q, :], M.OT[:, k, 128 * t:128 * t + 128],
                             w(k)[:, 512 * q:512 * q + 512], start=k == 0, stop=k == KT - 1)
            m.then_inc(s.y_done, 1)


def add_output(nc, M, s, v):
    for n in range(4):
        v.wait_ge(s.y_done, n + 1)
        xs = M.X[:, n // 2, 512 * (n % 2):512 * (n % 2) + 512]
        v.tensor_tensor(xs, M.PS[:, n, :], xs, ALU.add).then_inc(M.x_ready, 1)


def latent(nc, M, n_norm, w_in, w_q_up, w_kv_up, w_out, raw_free):
    s = M.lat
    PS = M.PS
    FB = [PS[:, 0, :], PS[:, 1, :]]
    C, CT, QK, SQ, QR, QKT, V = M.b_C, M.b_CT, M.b_QK, M.b_SQ, M.b_QR, M.b_QKT, M.b_V
    v, a, e, sp, p = nc.vector, nc.scalar, nc.tensor, nc.sync, nc.gpsimd
    half = B_IN // 2
    KH = KT // 2
    RAWF = M.RAW[:].rearrange("p a n -> p (a n)")
    WQ = M.R[:, 0:3 * HEADS * B_QK].rearrange("p (k n) -> p k n", k=3)
    WKV = RAWF[:, 0:4096].rearrange("p (k n) -> p k n", k=2)
    wo_at = lambda k: (M.R[:, 4608 + D * k:4608 + D * k + D] if k < KT - 1 else M.b_WO)
    w_in_v = w_in.rearrange("(c k p) n -> p c k n", p=128, k=KH)

    class L:
        depth, shared_bank = 4, True
        width = [128, T]
        scores = [PS[:, 2, :], PS[:, 3, :], PS[:, 4, 0:128], PS[:, 4, 128:384]]
        fills = [[[(0, 0)]], [[(0, 0), (128, 1)]]]
        SC, PT = M.b_SC, M.b_PT

        @staticmethod
        def out(i, j):
            return M.OT[:, bass.ds(i * 2 + j, 1)].rearrange("p a n -> p (a n)")

        @staticmethod
        def products(i, j, h, t):
            w = 128 * (t + 1)
            return [(L.scores[2 * h + t][:, 0:w], QKT[:, j, h, 128 * t:128 * t + 128], QKT[:, j, 2 + h, 0:w])]

        @staticmethod
        def shift(v, i, j, h, t):
            w = L.width[t]
            return v.tensor_tensor_reduce(out=L.SC[2 * h + t][:, 0:w], in0=L.scores[2 * h + t][:, 0:w],
                                          in1=M.MASK[:, MASK_B[t]:MASK_B[t] + w], scale=-(B_QK ** -0.5),
                                          scalar=3.0e38, op0=ALU.add, op1=ALU.min, accum_out=M.NM[2 * h + t])

        @staticmethod
        def value(i, j, key, h):
            return V[:, j, key, h]

    at = Attention(nc, M, L, softmaxes=48, fills=16 + 6 * PAIRS, pairs=12)

    def down_chunk(buf, c):
        return buf[:, c, 0:KH * B_IN].rearrange("p (k n) -> p k n", k=KH)

    def first_pair(i, j):
        return isinstance(i, int) and i == 0 and j == 0

    def projected(i, j):
        return 0 if first_pair(i, j) else i * 12 + (6 * j - 2)

    def turned(i, j, last=False):
        return i * 12 + (6 * j + (4 if last else 8))

    def project(i, j):
        u = projected(i, j)
        for t in range(NT):
            at_least(e, s.fb_free, u + (t - 1))
            for k in range(3):
                m = e.matmul(FB[t][:, 0:2 * B_QK], CT[:, k, 128 * t:128 * t + 128],
                             WQ[:, k, bass.ds((i * 2 + j) * (2 * B_QK), 2 * B_QK)], start=k == 0, stop=k == 2)
            m.then_inc(s.fb_full, 1)
        for t in range(NT):
            at_least(e, s.fb_free, u + (2 + t - 1))
            for k in range(2):
                m = e.matmul(FB[t][:, 0:256], CT[:, 3 + k, 128 * t:128 * t + 128],
                             WKV[:, k, bass.ds((i * 2 + j) * 256, 256)], start=k == 0, stop=k == 1)
            m.then_inc(s.fb_full, 1)

    def project_out(i, j):
        u = projected(i, j)
        qk = QK[j]
        for t in range(NT):
            a.wait_ge(s.fb_full, u + (t + 1))
            a.activation(qk[:, t, 0:2].rearrange("p h d -> p (h d)"), FB[t][:, 0:2 * B_QK], ACT.Copy).then_inc(s.fb_free, 1)
        at_least(a, s.v_moved, i * 2 + j)
        for t in range(NT):
            a.wait_ge(s.fb_full, u + (2 + t + 1))
            kv = FB[t][:, 0:256].rearrange("p (h d) -> p h d", h=2)
            a.activation(qk[:, t, 2:4, 0:B_NOPE], kv[:, :, 0:B_NOPE], ACT.Copy)
            a.activation(qk[:, t, 2:4, B_NOPE:], C[:, t, B_QR + B_KVR:].unsqueeze(1).broadcast_to([128, 2, B_ROPE]), ACT.Copy)
            a.activation(M.b_VN[:, t], kv[:, :, B_NOPE:], ACT.Copy).then_inc(s.fb_free, 1)

    def move_values(i, j):
        a.wait_ge(s.fb_free, projected(i, j) + 4)
        a.activation(V[:, j], M.b_VN, ACT.Copy).then_inc(s.v_moved, 1)

    def square_sums(i, j):
        v.wait_ge(s.fb_free, projected(i, j) + 4)
        n = Chain(v, s.nr, i * 26 + 13 * j)
        at_least(v, s.nr, i * 26 + 13 * j)
        for t in range(NT):
            n.add(v.tensor_tensor(SQ[:], QK[j][:, t], QK[j][:, t], ALU.mult))
            n.wait()
            n.add(v.tensor_reduce(M.SSH[:, 4 * t:4 * t + 4], SQ[:], axis=AX.X, op=ALU.add))
            if t == 0:
                n.wait()

    def norm_rope(i, j):
        n = Chain(v, s.nr, i * 26 + (13 * j + 4))
        v.wait_ge(s.rs, 2 + i * 4 + (2 * j + 2))
        if not first_pair(i, j):
            v.wait_ge(s.fb_free, i * 12 + (6 * j + 4))
        n.add(v.tensor_tensor(QK[j], QK[j], M.RSH[:, 0:8].rearrange("p (t h) -> p t h", t=NT).unsqueeze(3)
                              .broadcast_to([128, NT, 4, B_QK]), ALU.mult))
        n.wait()
        for t in range(NT):
            n.add(v.tensor_tensor(QR[:, t].rearrange("p (q h) d -> p q h d", q=2),
                                  QK[j][:, t].rearrange("p (q h) d -> p q h d", q=2),
                                  M.ROPE_B[:, t, :, 0:B_QK].unsqueeze(2).broadcast_to([128, 2, 2, B_QK]), ALU.mult))
            for q in range(2):
                n.add(v.tensor_tensor(SQ[:, 2 * q:2 * q + 2, B_NOPE:].rearrange("p h (s d) -> p h s d", s=2),
                                      QK[j][:, t, 2 * q:2 * q + 2, B_NOPE:].rearrange("p h (s d) -> p h s d", s=2)[:, :, ::-1, :],
                                      M.ROPE_B[:, t, q, B_QK:].rearrange("p (s d) -> p s d", s=2).unsqueeze(1)
                                      .broadcast_to([128, 2, 2, B_ROPE // 2]), ALU.mult))
            n.wait()
            n.add(v.tensor_tensor(QR[:, t, :, B_NOPE:], QR[:, t, :, B_NOPE:], SQ[:, :, B_NOPE:], ALU.add))
            if t == 0:
                n.wait()

    def inverse_rms(i, j):
        p.wait_ge(s.nr, i * 26 + (13 * j + 4))
        p.sem_inc(M.passed, 1)
        p.tensor_scalar(M.RSH[:, 0:8], M.SSH[:, 0:8], 1 / B_QK, EPS, ALU.mult, ALU.add).then_inc(s.rs, 1)
        p.wait_ge(s.rs, 2 + i * 4 + (2 * j + 1))
        p.tensor_tensor(M.RSH[:, 0:8], M.RSH[:, 0:8], M.HF[:, 0:8], ALU.pow).then_inc(s.rs, 1)

    def turn(i, j, last=False):
        for t in range(NT):
            e.wait_ge(s.nr, i * 26 + (13 * j + 4 * t + 9))
            e.wait_ge(s.fb_free, turned(i, j, last) + (t - 1))
            for h in range(4):
                m = e.transpose(FB[t][0:B_QK, 128 * h:128 * h + 128], QR[:, t, h], M.ID[:])
            m.then_inc(s.fb_full, 1)

    def turn_out(i, j, last=False):
        for t in range(NT):
            a.wait_ge(s.fb_full, turned(i, j, last) + (t + 1))
            a.activation(QKT[:, j, :, 128 * t:128 * t + 128],
                         FB[t][0:B_QK, :].rearrange("p (h n) -> p h n", h=4), ACT.Copy).then_inc(s.fb_free, 1)

    def after(i, j):
        return (i, 1) if j == 0 else (i + 1, 0)

    LAST = PAIRS // 2 - 1

    def high(c):
        a.wait_ge(s.w_in[c], 48 * 12 + 16)
        a.activation(down_chunk(M.HI, c), down_chunk(M.RAW, c), ACT.Copy).then_inc(s.w_hi[c], 1)

    def low(c):
        v.wait_ge(s.w_hi[c], MIX_LOADS + 1)
        v.tensor_tensor(down_chunk(M.LO, c), down_chunk(M.RAW, c), down_chunk(M.HI, c).bitcast(f32),
                        ALU.subtract).then_inc(s.w_lo[c], 1)

    def sync():
        for c in range(2):
            raw_free(sp, c)
            sp.dma_start(down_chunk(M.RAW, c), w_in_v[:, c]).then_inc(s.w_in[c], 16)
        sp.wait_ge(M.x_ready, 12)
        sp.dma_start(WQ, w_q_up.rearrange("(k p) n -> p k n", p=128)).then_inc(s.wq_in, 16)
        for k in range(KT - 1):
            sp.dma_start(wo_at(k), w_out[128 * k:128 * k + 128, :]).then_inc(s.wo_in, 16)
        for c in range(2):
            sp.wait_ge(s.w_lo[c], MIX_LOADS + 1)
        sp.dma_start(WKV, w_kv_up.rearrange("(k p) n -> p k n", p=128)).then_inc(s.wq_in, 16)
        sp.dma_start(wo_at(KT - 1), w_out[D - 128:, :]).then_inc(s.wo_in, 16)

    def act():
        high(1)
        for t in range(NT):
            a.wait_ge(s.c_full, t + 1)
            for q in range(2):
                a.activation(C[:, t, half * q:half * q + half], PS[:, 2 * t + q, 0:half], ACT.Copy).then_inc(s.c_out, 1)
            a.wait_ge(s.c_out, 4 * t + 2)
            for q, (lo, hi) in enumerate([(0, B_QR), (B_QR, B_QR + B_KVR)]):
                if q:
                    a.wait_ge(s.c_out, 4 * t + 3)
                a.activation(M.JUNK[:, 0:hi - lo], C[:, t, lo:hi], ACT.Square,
                             accum_out=M.SSB[:, 2 * q + t:2 * q + t + 1]).then_inc(s.c_out, 1)
        for k in range(5):
            a.wait_ge(s.ct_full, k // 2 + 1)
            a.activation(CT[:, k], M.TRB[k // 2 % 2][:, T * (k % 2):T * (k % 2) + T], ACT.Copy,
                         scale=M.GC[:, GC_BA + k:GC_BA + k + 1]).then_inc(s.ct_done, 1)

        def body(i, j, further=True, following=True):
            ni, nj = after(i, j)
            if further:
                project_out(i + 1, j)
            if following:
                turn_out(ni, nj, last=not further)
            at.turned_out(i, j, 0, 0)
            at.turned_out(i, j, 0, 1)
            if following:
                at.exponent(ni, nj, 0, 0)
                at.exponent(ni, nj, 0, 1)
            at.turned_out(i, j, 1, 0)
            at.turned_out(i, j, 1, 1)
            at.output(i, j)
            if further:
                move_values(i + 1, j)
            if following:
                at.exponent(ni, nj, 1, 0)
                at.exponent(ni, nj, 1, 1)
        for j in range(2):
            project_out(0, j)
            move_values(0, j)
        turn_out(0, 0)
        for h in range(2):
            for t in range(NT):
                at.exponent(0, 0, h, t)
        body(0, 0)
        body(0, 1)
        with a.Fori(1, LAST) as i:
            body(i, 0)
            body(i, 1)
        body(LAST, 0, further=False)
        body(LAST, 1, further=False, following=False)

    def pool():
        p.wait_ge(s.c_out, 8)
        RSB, SSB = M.RSB, M.SSB
        p.tensor_scalar(RSB[:, 0:2], SSB[:, 0:2], 1 / B_QR, EPS, ALU.mult, ALU.add).then_inc(s.rs, 1)
        p.tensor_scalar(RSB[:, 2:4], SSB[:, 2:4], 1 / B_KVR, EPS, ALU.mult, ALU.add).then_inc(s.rs, 1)
        p.wait_ge(s.rs, 2)
        p.tensor_tensor(RSB[:], RSB[:], M.HF[:, 0:4], ALU.pow).then_inc(s.c_rs, 1)
        for j in range(2):
            inverse_rms(0, j)
        with p.Fori(1, PAIRS // 2) as i:
            for j in range(2):
                inverse_rms(i, j)

    def dve():
        low(1)
        v.wait_ge(s.c_rs, 1)
        for t in range(NT):
            for q, (lo, hi) in enumerate([(0, B_QR), (B_QR, B_QR + B_KVR)]):
                v.tensor_scalar(C[:, t, lo:hi], C[:, t, lo:hi], M.RSB[:, 2 * q + t:2 * q + t + 1], None,
                                ALU.mult).then_inc(s.cn, 1)

        def body(i, j, further=True, following=True):
            ni, nj = after(i, j)
            if following:
                norm_rope(ni, nj)
            for h in range(2):
                for t in range(NT):
                    at.divided(i, j, h, t)
            if following:
                at.shifted(ni, nj, 0, 0)
                at.shifted(ni, nj, 0, 1)
            if further:
                square_sums(i + 1, j)
            if following:
                at.shifted(ni, nj, 1, 0)
                at.shifted(ni, nj, 1, 1)
        square_sums(0, 0)
        norm_rope(0, 0)
        square_sums(0, 1)
        for h in range(2):
            for t in range(NT):
                at.shifted(0, 0, h, t)
        body(0, 0)
        body(0, 1)
        with v.Fori(1, LAST) as i:
            body(i, 0)
            body(i, 1)
        body(LAST, 0, further=False)
        body(LAST, 1, further=False, following=False)
        add_output(nc, M, s, v)

    def pe():
        e.wait_ge(M.xl_done, KT * (n_norm + 1))
        for c in range(2):
            e.wait_ge(s.w_lo[c], MIX_LOADS + 1)
            for t in range(NT):
                for q in range(2):
                    for kk in range(KH):
                        k = KH * c + kk
                        for n, (x, w) in enumerate([(M.XL, M.HI), (M.XH, M.LO), (M.XH, M.HI)]):
                            m = e.matmul(PS[:, 2 * t + q, 0:half], x[:, k, 128 * t:128 * t + 128],
                                         down_chunk(w, c)[:, kk, half * q:half * q + half],
                                         start=(k == 0 and n == 0), stop=(k == KT - 1 and n == 2))
                if c == 1:
                    m.then_inc(s.c_full, 1)
        e.wait_ge(s.cn, 4)
        for b in range(3):
            if b == 2:
                e.wait_ge(s.ct_done, 2)
            for k in range(2 * b, min(2 * b + 2, 5)):
                for t in range(NT):
                    m = e.transpose(M.TRB[b % 2][:, T * (k % 2) + 128 * t:T * (k % 2) + 128 * t + 128],
                                    C[:, t, 128 * k:128 * k + 128], M.ID[:])
            m.then_inc(s.ct_full, 1)
        e.wait_ge(s.ct_done, 5)
        e.wait_ge(s.wq_in, 32)

        def scores(i, j, h, n_turned):
            if h == 0:
                e.wait_ge(s.fb_free, n_turned)
            for t in range(NT):
                at.scores(i, j, h, t)

        def body(i, j, further=True, following=True):
            ni, nj = after(i, j)
            if further:
                project(i + 1, j)
            if following:
                turn(ni, nj, last=not further)
            at.weighted(i, j, 0, 0)
            at.weighted(i, j, 0, 1)
            if following:
                scores(ni, nj, 0, turned(ni, nj, not further) + 2)
            at.weighted(i, j, 1, 0)
            at.weighted(i, j, 1, 1)
            if following:
                scores(ni, nj, 1, None)
        project(0, 0)
        project(0, 1)
        turn(0, 0)
        scores(0, 0, 0, turned(0, 0) + 2)
        scores(0, 0, 1, None)
        body(0, 0)
        body(0, 1)
        with e.Fori(1, LAST) as i:
            body(i, 0)
            body(i, 1)
        body(LAST, 0, further=False)
        body(LAST, 1, further=False, following=False)
        output_product(nc, M, s, 20, wo_at, 16 * KT)

    def first_high():
        a.wait_ge(M.ffn.dn_used[0], 3 * FF_TWICE + 1)
        high(0)

    return sync, act, pool, dve, pe, first_high, lambda: low(0)


def rope_tables(nc, M):
    v, a, s = nc.vector, nc.scalar, M.rope
    two_pi = 2 * np.pi
    c1 = 6.28125
    c2 = float(two_pi - c1)
    magic = 1.5 * 2 ** 23
    ANG, TURNS, CS = M.r_ANG, M.r_TURNS, M.r_CS
    NF = 48

    def dve():
        n = Chain(v, s.ch)
        v.wait_ge(M.small_in, M.n_small)
        n.add(v.tensor_copy(M.POSF[:], M.POS[:]))
        n.wait()
        for t in range(NT):
            n.add(v.tensor_scalar(ANG[:, t], M.FREQ[:], M.POSF[:, t:t + 1], None, ALU.mult))
        n.wait()
        for which, quarter in enumerate((0.0, 0.25)):
            tr, cs = TURNS[:, which], CS[:, which]
            n.add(v.tensor_scalar(tr, ANG[:], 1 / two_pi, quarter, ALU.mult, ALU.add))
            n.wait()
            n.add(v.tensor_scalar(tr, tr, magic, None, ALU.add))
            n.wait()
            n.add(v.tensor_scalar(tr, tr, magic, None, ALU.subtract))
            n.wait()
            n.add(v.scalar_tensor_tensor(cs, tr, -c1, ANG[:], ALU.mult, ALU.add))
            n.wait()
            n.add(v.scalar_tensor_tensor(cs, tr, -c2, cs, ALU.mult, ALU.add))
            n.wait()
            n.add(v.tensor_scalar(cs, cs, quarter * two_pi, 3.1415925, ALU.add, ALU.min))
            n.wait()
            n.add(v.tensor_scalar(cs, cs, -3.1415925, None, ALU.max))
            n.wait()
        v.sem_inc(s.reduced, 1)
        v.wait_ge(s.sines, 1)
        n = Chain(v, s.ch, n.n)
        for t in range(NT):
            for q in range(2):
                for sin_lo, sin_hi, fl, g0, w, tab_c, tab_s in (
                        (0, 1, 0, 0, 32, M.ROPE_A[:, t, 0, q], M.ROPE_A[:, t, 1, q]),
                        (0, 1, 32, 64, 16, M.ROPE_B[:, t, q, B_NOPE:B_QK], M.ROPE_B[:, t, q, B_QK:])):
                    gains = M.HG[:, 160 * q:160 * q + 160]
                    g1 = gains[:, 0:32] if w == 32 else gains[:, 128:144]
                    g2 = gains[:, 32:64] if w == 32 else gains[:, 144:160]
                    cos, sin = CS[:, 1, t, fl:fl + w], CS[:, 0, t, fl:fl + w]
                    n.add(v.tensor_tensor(tab_c[:, 0:w], g1, cos, ALU.mult))
                    n.add(v.tensor_tensor(tab_c[:, w:2 * w], g2, cos, ALU.mult))
                    n.add(v.scalar_tensor_tensor(tab_s[:, 0:w], g2, -1.0, sin, ALU.mult, ALU.mult))
                    n.add(v.tensor_tensor(tab_s[:, w:2 * w], g1, sin, ALU.mult))
                n.add(v.tensor_copy(M.ROPE_B[:, t, q, 0:B_NOPE], M.HG[:, 160 * q + 64:160 * q + 128]))
        n.wait()

    def act():
        a.wait_ge(s.reduced, 1)
        a.activation(CS[:], CS[:], ACT.Sin).then_inc(s.sines, 1)

    return act, dve


def conditioning(nc, M, w_ada, b_ada):
    e, a, v, sp, s = nc.tensor, nc.scalar, nc.vector, nc.sync, M.ada
    AB, MTB = M.PS[:, 0, :], M.PS[:, 1, :]

    def load(n):
        g, m = divmod(n, 9)
        slot, u = n % R_SLOTS, n // R_SLOTS
        at_least(sp, s.r_used[slot], u)
        dst = M.R[:, SR * slot:SR * slot + SR]
        if m == 0:
            sp.dma_start(dst[0:1], b_ada[:, SR * g:SR * g + SR]).then_inc(s.r_in[slot], 16)
        else:
            sp.dma_start(dst, w_ada[128 * (m - 1):128 * m, SR * g:SR * g + SR]).then_inc(s.r_in[slot], 16)

    def product(n):
        g, m = divmod(n, 9)
        slot, u = n % R_SLOTS, n // R_SLOTS
        if n == 0:
            e.wait_ge(s.cs, 1)
            e.wait_ge(M.ones_set, 3)
        e.wait_ge(s.r_in[slot], 16 * u + 16)
        if m == 0:
            at_least(e, s.mr, 4 * g)
        for q in range(4):
            rhs = M.R[:, SR * slot + 512 * q:SR * slot + 512 * q + 512]
            lhsT = M.ONES[0:1, 0:2] if m == 0 else M.CS[:, m - 1, :]
            mm = e.matmul(AB[32 * q:32 * q + 2, :], lhsT, rhs[0:1] if m == 0 else rhs, start=m == 0, stop=m == 8)
        mm.then_inc(s.r_used[slot], 1)

    def rows_out(g):
        a.wait_ge(M.ones_set, 3)
        a.wait_ge(s.r_used[(9 * g + 8) % R_SLOTS], (9 * g + 8) // R_SLOTS + 1)
        for q in range(4):
            a.activation(M.MR[32 * q:32 * q + 2, g, :], AB[32 * q:32 * q + 2, :], ACT.Copy).then_inc(s.mr, 1)

    def turn(g):
        e.wait_ge(s.mr, 4 * g + 4)
        at_least(e, s.mc, g)
        for b in range(4):
            mm = e.transpose(MTB[:, 128 * b:128 * b + 128], M.MR[:, g, 128 * b:128 * b + 128], M.ID[:])
        mm.then_inc(s.mt, 1)

    def columns_out(g):
        v.wait_ge(s.mt, g + 1)
        v.tensor_copy(M.MC[:, 32 * g:32 * g + 32].rearrange("p (q b w) -> p q b w", q=4, b=4),
                      MTB.rearrange("p (b q r) -> p q b r", b=4, q=4)[:, :, :, 0:2]).then_inc(s.mc, 1)

    return load, product, rows_out, turn, columns_out


def first_mixer(nc, M, A):
    e, a, v, sp, p, s = nc.tensor, nc.scalar, nc.vector, nc.sync, nc.gpsimd, M.mix
    PS, TRB = M.PS, M.TRB
    FB = [PS[:, 4, :], PS[:, 5, :]]
    load, product, rows_out, turn_rows, columns_out = conditioning(nc, M, A["w_ada"], A["b_ada"])
    w_in_v = A["w_in"].rearrange("(k p) n -> p k n", p=128)
    Q0, K0, V0, B0 = FH, 3 * FH, 5 * FH, 7 * FH
    CHUNKS = [(K0, "k", 0), (K0 + 256, "k", 1), (V0, "v", 0), (V0 + 256, "v", 1), (Q0, "q", 0), (Q0 + 256, "q", 1),
              (0, "f", 0), (B0, "b", 0), (B0 + 256, "c", 0), (B0 + 512, "h", 0)]
    CH_PART = lambda buf, c: buf[:, c % 2, 0:SR].rearrange("p (k n) -> p k n", k=KT)
    CXP = lambda buf, k: buf[:, k // 4, SR + T * (k % 4):SR + T * (k % 4) + T]
    SIDES = [(lambda k: M.XH[:, k], lambda k: M.XL[:, k]), (lambda k: CXP(M.HI, k), lambda k: CXP(M.LO, k))]

    def uses():
        n = 0
        for c, (_, kind, at) in enumerate(CHUNKS):
            for side in range(2 if kind in "kv" else 1):
                yield n, c, kind, at, side
                n += 1
    USES = list(uses())

    class L:
        depth, shared_bank = 4, False
        width = [512, 512]
        scores = [PS[:, b, :] for b in range(4)]
        fills = [[[(128 * kt, kt) for kt in range(4)]]] * 2
        SC, PT = M.n_SC, M.n_PT

        @staticmethod
        def products(i, j, h, t):
            return [(L.scores[2 * h + t], M.QT0[64 * h:64 * h + 64, 2 * i + j, 128 * t:128 * t + 128],
                     M.KT0[64 * h:64 * h + 64, 2 * i + j, :])]

        @staticmethod
        def shift(v, i, j, h, t):
            v.wait_ge(s.bias_in[2 * h + t], 16 * (2 * i + j) + 16)
            return v.tensor_tensor_reduce(out=L.SC[2 * h + t], in0=L.scores[2 * h + t], in1=M.BIAS[2 * h + t], scale=-1.0,
                                          scalar=3.0e38, op0=ALU.add, op1=ALU.min, accum_out=M.NM[2 * h + t])

        @staticmethod
        def value(i, j, key, h):
            return M.V0[:, key, 128 * (2 * i + j) + 64 * h:128 * (2 * i + j) + 64 * h + 64]

        @staticmethod
        def out(i, j):
            return M.mix_OT[:, 2 + 2 * i + j]

    NAP = 4
    at = Attention(nc, M, L)

    def softmax(n):
        return n // 8, n // 4 % 2, n // 2 % 2, n % 2

    def bias_load(pr, h, t):
        at_least(sp, M.att.sc_read, 4 * (pr - 1) + 2 * h + t + 1)
        sp.dma_start(M.BIAS[2 * h + t][:, 0:T], A["bias"][2 * pr + h, 128 * t:128 * t + 128, :]).then_inc(s.bias_in[2 * h + t], 16)

    def sync():
        sp.dma_start(M.CRAW[:], A["conditions"]).then_inc(s.c_in, 16)
        for n in range(9):
            load(n)
        for h in range(2):
            for t in range(NT):
                bias_load(0, h, t)
        for n in range(9, 27):
            load(n)
        for k in range(4):
            n = 27 + k
            slot, u = n % R_SLOTS, n // R_SLOTS
            sp.wait_ge(M.ada.r_used[slot], u)
            sp.dma_start(M.R[:, SR * slot:SR * slot + SR].rearrange("p (a n) -> p a n", a=2),
                         A["w_out"][256 * k:256 * k + 256, :].rearrange("(a p) n -> p a n", p=128)).then_inc(M.ada.r_in[slot], 16)
        for pr in range(1, NAP):
            for h in range(2):
                for t in range(NT):
                    bias_load(pr, h, t)

    def pool():
        p.memset(M.BIASZ, 0.0).then_inc(s.zeroed, 1)
        for c in range(2):
            p.dma_start(CH_PART(M.RAW, c), w_in_v[:, :, CHUNKS[c][0]:CHUNKS[c][0] + 256]).then_inc(s.w_in[c], 16)
        p.wait_ge(s.sq, 4)
        p.tensor_scalar(M.RS4[:], M.SS4[:], 1 / D, EPS, ALU.mult, ALU.add).then_inc(s.rs, 1)
        p.wait_ge(s.rs, 1)
        p.tensor_tensor(M.RS4[:], M.RS4[:], M.HF[:, 0:4], ALU.pow).then_inc(s.rs, 1)
        for c in range(2, len(CHUNKS)):
            p.wait_ge(s.w_lo[c % 2], c // 2)
            p.dma_start(CH_PART(M.RAW, c), w_in_v[:, :, CHUNKS[c][0]:CHUNKS[c][0] + 256]).then_inc(s.w_in[c % 2], 16)

    def act():
        a.wait_ge(s.c_in, 16)
        a.activation(M.CS[:], M.CRAW[:], ACT.Silu).then_inc(M.ada.cs, 1)
        a.wait_ge(s.x_in, 32)
        for n in range(4):
            at_least(a, s.sq, n)
            src = (M.X, M.CX)[n // 2][:, n % 2]
            a.activation(M.JUNK1, src, ACT.Square, accum_out=M.SS4[:, n:n + 1]).then_inc(s.sq, 1)
        rows_out(0)
        for side in range(2):
            for k in range(KT):
                a.wait_ge(s.tm, KT * side + k + 1)
                a.activation(SIDES[side][0](k), M.TM[k % 4], ACT.Copy).then_inc(s.xh, 1)

        def high(c):
            a.wait_ge(s.w_in[c % 2], 16 * (c // 2) + 16)
            a.activation(M.HI[:, c % 2, 0:SR], M.RAW[:, c % 2, 0:SR], ACT.Copy).then_inc(s.w_hi[c % 2], 1)
        high(0)
        high(1)
        for n, c, kind, at_, side in USES:
            a.wait_ge(s.fb_full, n + 1)
            src = FB[n % 2]
            two = src.rearrange("p (m n) -> p m n", m=2)
            if kind == "v":
                dst = M.V0[:, 2 * side:2 * side + 2, 256 * at_:256 * at_ + 256]
            elif kind == "k":
                dst = M.KT0[:, 2 * at_:2 * at_ + 2, T * side:T * side + T]
            elif kind == "q":
                dst = M.QT0[:, 2 * at_:2 * at_ + 2]
            else:
                dst = {"f": M.FT, "b": M.BT, "c": M.CT0, "h": M.HT0}[kind]
            a.activation(dst, two, ACT.Copy, scale=AD ** -0.5 if kind == "q" else 1.0).then_inc(s.fb_free, 1)
            if c + 2 < len(CHUNKS) and (n + 1 == len(USES) or USES[n + 1][1] != c):
                high(c + 2)
            if c == 4:
                rows_out(1)
            if c == 9:
                rows_out(2)
        for t in range(NT):
            a.wait_ge(s.fo_full, t + 1)
            a.activation(M.FA[:, t], FB[t], ACT.Copy).then_inc(s.fo_done, 1)
        a.wait_ge(s.fo_full, 3)
        a.activation(M.FOT, FB[0], ACT.Copy).then_inc(s.fo_done, 1)
        a.wait_ge(s.fo_full, 4)
        a.activation(M.mix_OT[:, 0:2].rearrange("p a n -> p (a n)"), FB[1], ACT.Copy).then_inc(s.fo_done, 1)
        for n in range(2):
            at.exponent(*softmax(n))
        for n in range(4 * NAP):
            if n + 2 < 4 * NAP:
                at.exponent(*softmax(n + 2))
            at.turned_out(*softmax(n))
            if n % 4 == 3:
                at.output(*softmax(n)[0:2])
        for g, q0, dst in ((1, 0, M.G1B), (2, 2, M.G2B)):
            for q in range(2):
                n = 2 * (g - 1) + q
                a.wait_ge(s.gb_full, n + 1)
                a.activation(dst[:, 512 * q:512 * q + 512], FB[n % 2], ACT.Copy).then_inc(s.gb_done, 1)

    def dve():
        columns_out(0)
        n = Chain(v, s.ch)
        v.wait_ge(M.ada.mc, 1)
        v.wait_ge(M.small_in, M.n_small)
        mc = M.MC[:].rearrange("p (f w) -> p f w", w=2)
        for who in range(2):
            n.add(v.scalar_tensor_tensor(M.MSC[:, who], mc[:, 8:16, who], 1.0, M.GC[:, GC_N1:GC_N1 + 8], ALU.add, ALU.mult))
        v.wait_ge(s.rs, 2)
        for side in range(2):
            src, dst = ((M.X, M.mix_XN), (M.CX, M.CX))[side]
            for t in range(NT):
                n.add(v.tensor_scalar(dst[:, t], src[:, t], M.RS4[:, 2 * side + t:2 * side + t + 1], None, ALU.mult))
        n.wait()
        for side in range(2):
            for k in range(KT):
                m = KT * side + k
                v.wait_ge(s.turned, m // 2 + 1)
                at_least(v, s.xl, m - 3)
                v.tensor_scalar(M.TM[k % 4], TRB[m // 2 % 2][:, T * (k % 2):T * (k % 2) + T],
                                M.MSC[:, side, k:k + 1], mc[:, k, side:side + 1], ALU.mult, ALU.add).then_inc(s.tm, 1)
                if k % 2:
                    for kk in (k - 1, k):
                        v.wait_ge(s.xh, KT * side + kk + 1)
                        v.tensor_tensor(SIDES[side][1](kk), M.TM[kk % 4], SIDES[side][0](kk).bitcast(f32),
                                        ALU.subtract).then_inc(s.xl, 1)
        for c in range(len(CHUNKS)):
            v.wait_ge(s.w_hi[c % 2], c // 2 + 1)
            v.tensor_tensor(M.LO[:, c % 2, 0:SR], M.RAW[:, c % 2, 0:SR], M.HI[:, c % 2, 0:SR].bitcast(f32),
                            ALU.subtract).then_inc(s.w_lo[c % 2], 1)
            if c == 7:
                columns_out(1)
        columns_out(2)
        n = Chain(v, s.ch, 6)
        v.wait_ge(s.fb_free, len(USES))
        v.wait_ge(s.zeroed, 1)
        for col in (0, T + 1):
            n.add(v.memset(M.CHP[:, :, col:col + 1], 0.0))
        n.add(v.tensor_tensor(M.CHP[:, :, 1:T + 1], M.CT0, M.HT0, ALU.mult))
        n.wait()
        for m in range(2):
            w = lambda tap: M.GC[:, GC_CONV + 2 * tap + m:GC_CONV + 2 * tap + m + 1]
            dst = M.mix_OT[:, 6 + m]
            n.add(v.tensor_scalar(dst, M.CHP[:, m, 0:T], w(0), None, ALU.mult))
            n.wait()
            for tap in (1, 2):
                n.add(v.scalar_tensor_tensor(dst, M.CHP[:, m, tap:tap + T], w(tap), dst, ALU.mult, ALU.add))
                n.wait()
            n.add(v.tensor_tensor(dst, dst, M.BT[:, m], ALU.mult))
        n.wait()
        for n in range(2):
            at.shifted(*softmax(n))
        for n in range(4 * NAP):
            if n + 2 < 4 * NAP:
                at.shifted(*softmax(n + 2))
            at.divided(*softmax(n))
        for n4 in range(4):
            v.wait_ge(s.y_done, n4 + 1)
            v.wait_ge(s.gb_done, n4 % 2 + 1)
            at_least(v, s.xu, 2 * (n4 - 1))
            q = n4 % 2
            v.tensor_tensor(M.TMPX[n4 % 2], PS[:, n4, :], M.G1B[:, 512 * q:512 * q + 512], ALU.mult).then_inc(s.xu, 1)
            v.wait_ge(s.xu, 2 * n4 + 1)
            xs = M.X[:, n4 // 2, 512 * q:512 * q + 512]
            v.tensor_tensor(xs, M.TMPX[n4 % 2], xs, ALU.add).then_inc(s.xu, 1)

    def pe():
        for n in range(9):
            product(n)
        turn_rows(0)
        e.wait_ge(s.ch, 6)
        for m in range(KT):
            side, b = divmod(m, 4)
            at_least(e, s.tm, 2 * (m - 1))
            src = (M.mix_XN, M.CX)[side]
            for kk in range(2):
                for t in range(NT):
                    k = 2 * b + kk
                    mm = e.transpose(TRB[m % 2][:, T * kk + 128 * t:T * kk + 128 * t + 128],
                                     src[:, t, 128 * k:128 * k + 128], M.ID[:])
            mm.then_inc(s.turned, 1)
        e.wait_ge(s.xl, 2 * KT)
        ada = 9
        for n, c, kind, at_, side in USES:
            e.wait_ge(s.w_lo[c % 2], c // 2 + 1)
            at_least(e, s.fb_free, n - 1)
            xh, xl = SIDES[side]
            hi, lo = CH_PART(M.HI, c), CH_PART(M.LO, c)
            for m in range(2):
                for k in range(KT):
                    for q, (w, x) in enumerate([(hi, xh), (hi, xl), (lo, xh)]):
                        if kind == "v":
                            l, r = x(k)[:, 128 * m:128 * m + 128], w[:, k, :]
                        else:
                            l, r = w[:, k, 128 * m:128 * m + 128], x(k)
                        mm = e.matmul(FB[n % 2][:, 256 * m:256 * m + 256], l, r,
                                      start=(k == 0 and q == 0), stop=(k == KT - 1 and q == 2))
            mm.then_inc(s.fb_full, 1)
            if n + 1 == len(USES) or USES[n + 1][1] != c:
                if c < 9:
                    for _ in range(2):
                        product(ada)
                        ada += 1
                if c in (5, 9):
                    turn_rows(1 if c == 5 else 2)
        e.wait_ge(M.small2, 64)
        e.wait_ge(s.fb_free, len(USES))
        for t in range(NT):
            for kc in range(2):
                mm = e.matmul(FB[t][:, 256 * kc:256 * kc + 256], M.FT[:, kc, 128 * t:128 * t + 128], M.DFT[:, 0:256],
                              start=True, stop=True)
            mm.then_inc(s.fo_full, 1)
        e.wait_ge(s.fo_done, 2)
        for kc in range(2):
            for n, (t, q) in enumerate([(0, 0), (0, 1), (1, 0), (1, 1)]):
                mm = e.matmul(FB[0][:, 256 * kc:256 * kc + 256], M.FA[:, t, 256 * kc + 128 * q:256 * kc + 128 * q + 128],
                              M.DFT[:, 256 + 512 * q + 256 * t:256 + 512 * q + 256 * t + 256], start=n == 0, stop=n == 3)
        mm.then_inc(s.fo_full, 1)
        e.wait_ge(s.fo_done, 3)
        for m in range(2):
            for kc in range(2):
                mm = e.matmul(FB[1][:, 256 * m:256 * m + 256], M.WF[:, kc, 128 * m:128 * m + 128], M.FOT[:, 256 * kc:256 * kc + 256],
                              start=kc == 0, stop=kc == 1)
        mm.then_inc(s.fo_full, 1)
        e.wait_ge(s.fo_done, 4)
        e.wait_ge(M.ada.mc, 3)
        e.wait_ge(s.ch, 17)
        for n in range(3):
            at.scores(*softmax(n))
        for n in range(4 * NAP):
            if n + 3 < 4 * NAP:
                at.scores(*softmax(n + 3))
            at.weighted(*softmax(n))
        e.wait_ge(M.att.o_free, NAP)
        for g, q0 in ((1, 0), (2, 2)):
            for q in range(2):
                n = 2 * (g - 1) + q
                at_least(e, s.gb_done, n - 1)
                r = 32 * (q0 + q)
                e.matmul(FB[n % 2], M.ONES[r:r + 1, :], M.MR[r:r + 1, g, :], start=True, stop=True).then_inc(s.gb_full, 1)
        for k in range(4):
            e.wait_ge(M.ada.r_in[(27 + k) % R_SLOTS], 16 * ((27 + k) // R_SLOTS) + 16)
        for n4 in range(4):
            t, q = divmod(n4, 2)
            for k in range(KT):
                slot = (27 + k // 2) % R_SLOTS
                w = M.R[:, SR * slot + D * (k % 2):SR * slot + D * (k % 2) + D]
                mm = e.matmul(PS[:, n4, :], M.mix_OT[:, k, 128 * t:128 * t + 128], w[:, 512 * q:512 * q + 512],
                              start=k == 0, stop=k == KT - 1)
            mm.then_inc(s.y_done, 1)

    return sync, act, pool, dve, pe


def experts(nc, M, A):
    e, a, v, sp, p, s = nc.tensor, nc.scalar, nc.vector, nc.sync, nc.gpsimd, M.moe
    PS, TRB, XN = M.PS, M.TRB, M.XN
    GB, UB = PS[:, 0, :], PS[:, 1, :]
    N_SLOTS = 6
    SLOTS = [M.R[:, SR * q:SR * q + SR] for q in range(R_SLOTS)] + [M.RAW[:, 0, 0:SR]]
    NL = N_GROUPS + EXPERTS
    lg = M.LG.rearrange("p (t n) -> p t n", t=NT)
    KEY, CW = M.KEY, M.CW
    gate, up = (w.rearrange("(g e) (c k p) n -> g c p e k n", e=2, k=2, p=128) for w in (A["w_gate"], A["w_up"]))
    down = A["w_down"].rearrange("(g e) (c p) n -> g c p e n", e=2, p=128)

    def passes(first, end):
        s = M.steps

        def load(g, m):
            slot = m % N_SLOTS
            for x in range(2):
                if m < 8:
                    dst = SLOTS[slot].rearrange("p (e k n) -> p e k n", e=2, k=2)[:, x]
                    src = (gate, up)[m // 4][bass.ds(g, 1), m % 4, :, x].rearrange("g p k n -> p (g k) n")
                else:
                    dst = SLOTS[slot].rearrange("p (e n) -> p e n", e=2)[:, x]
                    src = down[bass.ds(g, 1), m - 8, :, x].rearrange("g p n -> p (g n)")
                sp.dma_start(dst, src).then_inc(s.w_in[slot], 16)

        def step_loads(g, r):
            for m in range(12):
                sp.wait_ge(s.used[m % N_SLOTS], g * 2 + (2 * PAIR_STEPS * r + m // N_SLOTS))
                load(g, m)

        def sync():
            if first == 0:
                for m in range(12):
                    if m in (0, 2):
                        sp.wait_ge(M.mix.y_done, 4)
                    if m >= N_SLOTS:
                        sp.wait_ge(s.used[m % N_SLOTS], 1)
                    load(0, m)
                with sp.Fori(1, PAIR_STEPS) as g:
                    step_loads(g, 0)
            else:
                for r in range(1, ROUNDS):
                    with sp.Fori(0, PAIR_STEPS) as g:
                        step_loads(g, r)

        def gathered(it):
            for k in range(KT):
                if k % 4 == 0:
                    a.wait_ge(s.xg_full, it * 8 + (k + 4))
                a.activation(M.XG[:, k], PS[:, 4 + k // 4, 128 * (k % 4):128 * (k % 4) + 128], ACT.Identity,
                             scale=M.MSC[:, 2, k:k + 1], bias=M.SH2[:, k:k + 1]).then_inc(s.xg_done, 1)

        def silu(it):
            a.wait_ge(s.used[7 % N_SLOTS], it * 2 + 2)
            a.activation(M.SGM, GB, ACT.Silu).then_inc(s.silu, 1)

        def turned(it):
            a.wait_ge(s.ht_full, it + 1)
            a.activation(M.HT, PS[:, 6, :], ACT.Copy).then_inc(s.ht_done, 1)
            a.wait_ge(s.cm_full, it + 1)
            a.activation(M.CM, PS[:, 7, 0:T], ACT.Copy).then_inc(s.cm_done, 1)

        def y_out(it):
            a.wait_ge(s.used[11 % N_SLOTS], it * 2 + 2)
            a.activation(M.YS, PS[:, 2:4, :].rearrange("p a n -> p (a n)"), ACT.Copy).then_inc(s.y_done, 1)

        def act():
            gathered(first)
            silu(first)
            gathered(first + 1)
            turned(first)
            y_out(first)
            with a.Fori(first + 1, end - 1) as it:
                silu(it)
                gathered(it + 1)
                turned(it)
                y_out(it)
            silu(end - 1)
            turned(end - 1)
            y_out(end - 1)

        def hot(it, weighted):
            sem, dst = (s.ohc, M.OHC) if weighted else (s.oh, M.OH)
            for t in range(NT):
                for x in range(2):
                    col = bass.ds(it * 2 + x, 1)
                    out = dst[:, t, CAP * x:CAP * x + CAP]
                    if weighted:
                        m = v.tensor_scalar(out, M.IOTA, KEY[:, t, col], CW[:, t, col], ALU.is_equal, ALU.mult)
                    else:
                        m = v.tensor_scalar(out, M.IOTA, KEY[:, t, col], None, ALU.is_equal)
                    m.then_inc(sem, 1)

        def hidden(it):
            v.wait_ge(s.silu, it + 1)
            v.tensor_tensor(M.HM, M.SGM, UB, ALU.mult).then_inc(s.h_done, 1)

        def accumulate(it):
            for c in range(4):
                v.wait_ge(s.sc_full, it * 4 + (c + 1))
                ys = M.YACC[:, c // 2, 512 * (c % 2):512 * (c % 2) + 512]
                v.tensor_tensor(ys, PS[:, 6 + c % 2, :], ys, ALU.add).then_inc(s.acc, 1)

        def dve():
            hot(first, False)
            v.wait_ge(s.xg_full, 8 * first + 8)
            hot(first + 1, False)
            hot(first, True)
            hidden(first)
            with v.Fori(first + 1, end - 1) as it:
                v.wait_ge(s.xg_full, it * 8 + 8)
                hot(it + 1, False)
                v.wait_ge(s.cm_full, it)
                hot(it, True)
                accumulate(it - 1)
                hidden(it)
            it = end - 1
            v.wait_ge(s.cm_full, it)
            hot(it, True)
            accumulate(it - 1)
            hidden(it)
            accumulate(it)
            v.wait_ge(s.acc, 4 * end)

        def gather(it):
            e.wait_ge(s.oh, it * 4 + 4)
            at_least(e, s.xg_done, it * 8)
            for k in range(KT):
                for t in range(NT):
                    m = e.matmul(PS[:, 4 + k // 4, 128 * (k % 4):128 * (k % 4) + 128], XN[:, t, 128 * k:128 * k + 128],
                                 M.OH[:, t], start=t == 0, stop=t == 1)
                m.then_inc(s.xg_full, 1)

        def gate_up(it):
            e.wait_ge(s.xg_done, it * 8 + 8)
            at_least(e, s.h_done, it)
            for m in range(8):
                slot = m % N_SLOTS
                e.wait_ge(s.w_in[slot], it * 64 + (32 * (m // N_SLOTS) + 32))
                w = SLOTS[slot].rearrange("p (e k n) -> p e k n", e=2, k=2)
                for kk in range(2):
                    k = 2 * (m % 4) + kk
                    for x in range(2):
                        mm = e.matmul((GB, UB)[m // 4][CAP * x:CAP * x + CAP], M.XG[:, k, CAP * x:CAP * x + CAP],
                                      w[:, x, kk, :], start=k == 0, stop=k == KT - 1)
                mm.then_inc(s.used[slot], 1)

        def scatter(it):
            e.wait_ge(s.y_done, it + 1)
            e.wait_ge(s.cm_done, it + 1)
            for c in range(4):
                if c >= 2:
                    e.wait_ge(s.acc, it * 4 + (c - 1))
                e.matmul(PS[:, 6 + c % 2, :], M.CM[:, 128 * (c // 2):128 * (c // 2) + 128],
                         M.YS[:, 512 * (c % 2):512 * (c % 2) + 512], start=True, stop=True).then_inc(s.sc_full, 1)

        def turn(it):
            e.wait_ge(s.h_done, it + 1)
            at_least(e, s.acc, it * 4)
            for f in range(4):
                m = e.transpose(PS[:, 6, 128 * f:128 * f + 128], M.HM[:, 128 * f:128 * f + 128], M.ID[:])
            m.then_inc(s.ht_full, 1)
            e.wait_ge(s.ohc, it * 4 + 4)
            for t in range(NT):
                m = e.transpose(PS[:, 7, 128 * t:128 * t + 128], M.OHC[:, t], M.ID[:])
            m.then_inc(s.cm_full, 1)

        def down_product(it):
            e.wait_ge(s.ht_done, it + 1)
            at_least(e, s.y_done, it)
            for f in range(4):
                slot = (8 + f) % N_SLOTS
                e.wait_ge(s.w_in[slot], it * 64 + 64)
                w = SLOTS[slot].rearrange("p (e n) -> p e n", e=2)
                for q in range(2):
                    for x in range(2):
                        mm = e.matmul(PS[CAP * x:CAP * x + CAP, 2 + q, :],
                                      M.HT[:, 128 * f + CAP * x:128 * f + CAP * x + CAP],
                                      w[:, x, 512 * q:512 * q + 512], start=f == 0, stop=f == 3)
                mm.then_inc(s.used[slot], 1)

        def pe():
            gather(first)
            gate_up(first)
            gather(first + 1)
            turn(first)
            down_product(first)
            with e.Fori(first + 1, end - 1) as it:
                gate_up(it)
                scatter(it - 1)
                gather(it + 1)
                turn(it)
                down_product(it)
            it = end - 1
            gate_up(it)
            scatter(it - 1)
            turn(it)
            down_product(it)
            scatter(it)

        return sync, act, dve, pe

    sync1, act1, dve1, pe1 = passes(0, PAIR_STEPS)
    sync2, act2, dve2, pe2 = passes(PAIR_STEPS, ROUNDS * PAIR_STEPS)

    def other_rounds(eng, steps):
        eng.wait_ge(M.steps.acc, 4 * PAIR_STEPS)
        eng.wait_ge(s.counted, 1)
        left = eng.value_load(M.FLAG[0:1, 0:1], min_val=0, max_val=1)
        with eng.If(left > 0):
            steps()

    def sync():
        sync1()

        def steps():
            sync2()
            for q in range(N_SLOTS):
                sp.wait_ge(M.steps.used[q], 2 * ROUNDS * PAIR_STEPS)
        other_rounds(sp, steps)
        sp.dma_start(M.NFR, A["norm_final"]).then_inc(s.nf_in, 16)

    def act():
        a.wait_ge(M.mix.xu, 8)
        for t in range(NT):
            a.wait_ge(M.mix.sq, 4 + t)
            a.activation(M.m_JUNK, M.X[:, t], ACT.Square, accum_out=M.SS[:, t:t + 1]).then_inc(M.mix.sq, 1)
        a.wait_ge(s.ge, 1)
        a.activation(M.GE, M.GE, ACT.Exp).then_inc(s.ex, 1)
        a.wait_ge(s.ed, 1)
        a.activation(M.ED, M.ED, ACT.Exp).then_inc(s.ex, 1)
        act1()
        other_rounds(a, act2)
        a.wait_ge(s.fin, 4)
        for t in range(NT):
            a.wait_ge(M.mix.sq, 4 + NT + t)
            a.activation(M.m_JUNK, M.X[:, t], ACT.Square, accum_out=M.SS[:, t:t + 1]).then_inc(M.mix.sq, 1)

    def pool():
        for n in range(2):
            p.wait_ge(M.mix.sq, 4 + NT * (n + 1))
            p.tensor_scalar(M.RS[:], M.SS[:], 1 / D, EPS, ALU.mult, ALU.add).then_inc(M.mix.rs, 1)
            p.wait_ge(M.mix.rs, 2 * n + 3)
            p.tensor_tensor(M.RS[:], M.RS[:], M.HF[:, 0:NT], ALU.pow).then_inc(M.mix.rs, 1)

    def dve():
        n = Chain(v, s.rt)
        mc = M.MC[:].rearrange("p (f w) -> p f w", w=2)
        v.wait_ge(M.mix.xu, 8)
        v.wait_ge(M.ada.mc, 3)
        n.add(v.scalar_tensor_tensor(M.MSC[:, 2], mc[:, 32:40, 0], 1.0, M.GC[:, GC_N2:GC_N2 + 8], ALU.add, ALU.mult))
        n.add(v.tensor_copy(M.SH2[:], mc[:, 24:32, 0]))
        v.wait_ge(M.mix.rs, 4)
        for t in range(NT):
            n.add(v.tensor_scalar(XN[:, t], M.X[:, t], M.RS[:, t:t + 1], None, ALU.mult))
        n.wait()
        for k in range(KT):
            v.wait_ge(M.mix.turned, KT + k // 2 + 1)
            v.tensor_scalar(M.XT2[:, k], TRB[k // 2 % 2][:, T * (k % 2):T * (k % 2) + T], M.MSC[:, 2, k:k + 1],
                            M.SH2[:, k:k + 1], ALU.mult, ALU.add).then_inc(M.mix.tm, 1)
        v.wait_ge(s.lg_full, 1)
        n.add(v.tensor_copy(M.LG, PS[:, 0, 0:NT * NL]))
        n.wait()
        gl, el = lg[:, :, 0:N_GROUPS], lg[:, :, N_GROUPS:]
        MX = M.MX
        by_tile = lambda ap: ap.rearrange("p (t n) -> p t n", t=NT)
        GE, OHG, T4 = by_tile(M.GE), by_tile(M.OHG), by_tile(M.T4)
        EM, T32, OH1, OH2, ED = by_tile(M.EM), by_tile(M.T32), by_tile(M.OH1), by_tile(M.OH2), M.ED
        over = lambda col, w: col.unsqueeze(2).broadcast_to([128, NT, w])
        row = lambda r, w: r.unsqueeze(1).broadcast_to([128, NT, w])

        def step(ins):
            n.add(ins)
            n.wait()

        def first_largest(x, mx, hot, tmp, w):
            step(v.tensor_reduce(mx, x, axis=AX.X, op=ALU.max))
            step(v.tensor_tensor(tmp, x, over(mx, w), ALU.is_equal))
            step(v.tensor_tensor(tmp, tmp, row(M.DESC[:, EXPERTS - w:EXPERTS], w), ALU.mult))
            step(v.tensor_reduce(M.PK, tmp, axis=AX.X, op=ALU.max))
            step(v.tensor_tensor(hot, tmp, over(M.PK, w), ALU.is_equal))

        first_largest(gl, MX[:, 0:2], OHG, T4, N_GROUPS)
        v.tensor_tensor(GE, gl, over(MX[:, 0:2], N_GROUPS), ALU.subtract).then_inc(s.ge, 1)
        step(v.tensor_scalar(T4, OHG, -FAR, FAR, ALU.mult, ALU.add))
        for t in range(NT):
            group = lambda ap: ap[:, t].unsqueeze(2).broadcast_to([128, N_GROUPS, EPG])
            expert = lambda ap: ap[:, t].rearrange("p (g e) -> p g e", e=EPG)
            step(v.tensor_tensor(expert(EM), expert(el), group(OHG), ALU.mult))
            step(v.tensor_tensor(expert(EM), expert(EM), group(T4), ALU.add))
        first_largest(EM, MX[:, 2:4], OH1, T32, EXPERTS)
        step(v.scalar_tensor_tensor(EM, OH1, 2 * FAR, EM, ALU.mult, ALU.add))
        first_largest(EM, MX[:, 4:6], OH2, T32, EXPERTS)
        v.tensor_tensor(ED, MX[:, 4:6], MX[:, 2:4], ALU.subtract).then_inc(s.ed, 1)
        v.tensor_tensor(EM, OH1, OH2, ALU.add).then_inc(s.sel, 1)
        v.wait_ge(s.ex, 1)
        step(v.tensor_reduce(M.GW, GE, axis=AX.X, op=ALU.add))
        step(v.reciprocal(M.GW, M.GW))
        v.wait_ge(s.ex, 2)
        step(v.tensor_scalar(M.P1, ED, 1.0, None, ALU.add))
        step(v.reciprocal(M.P1, M.P1))
        step(v.tensor_tensor(M.P1, M.P1, M.GW, ALU.mult))
        step(v.tensor_tensor(M.P2, M.P1, ED, ALU.mult))
        n.add(v.tensor_tensor(OH1, OH1, over(M.P1, EXPERTS), ALU.mult))
        n.add(v.tensor_tensor(OH2, OH2, over(M.P2, EXPERTS), ALU.mult))
        n.wait()
        step(v.tensor_tensor(OH1, OH1, OH2, ALU.add))
        v.wait_ge(s.rk_full, 1)
        step(v.tensor_reduce(M.CNT, PS[0:1, 1, 64:96], axis=AX.X, op=ALU.max))
        v.tensor_scalar(M.FLAG[0:1, 0:1], M.CNT, float(CAP), None, ALU.is_gt).then_inc(s.counted, 1)
        v.wait_ge(s.sel, 1)
        step(v.tensor_scalar(T32, by_tile(PS[:, 1, 0:64]), 1.0, None, ALU.add))
        step(v.tensor_tensor(T32, T32, EM, ALU.mult))
        for r in range(ROUNDS):
            n.add(v.tensor_scalar(KEY[:, :, 32 * r:32 * r + 32], T32, -(1.0 + CAP * r), None, ALU.add))
            n.add(v.tensor_copy(CW[:, :, 32 * r:32 * r + 32], OH1))
        n.add(v.memset(M.YACC[:], 0.0))
        n.wait()
        dve1()
        other_rounds(v, dve2)
        v.wait_ge(M.mix.gb_done, 4)
        for t in range(NT):
            v.tensor_tensor(M.YACC[:, t], M.YACC[:, t], M.G2B, ALU.mult).then_inc(s.fin, 1)
        v.wait_ge(s.fin, 2)
        for t in range(NT):
            v.tensor_tensor(M.X[:, t], M.YACC[:, t], M.X[:, t], ALU.add).then_inc(s.fin, 1)
        v.wait_ge(M.mix.rs, 6)
        v.wait_ge(s.nf_in, 16)
        for t in range(NT):
            v.scalar_tensor_tensor(M.X[:, t], M.X[:, t], M.RS[:, t:t + 1], M.NFR, ALU.mult, ALU.mult).then_inc(M.x_ready, 2)

    def pe():
        e.wait_ge(s.rt, 4)
        for b in range(4):
            if b > 1:
                e.wait_ge(M.mix.tm, 2 * KT + 2 * (b - 1))
            for kk in range(2):
                for t in range(NT):
                    k = 2 * b + kk
                    m = e.transpose(TRB[b % 2][:, T * kk + 128 * t:T * kk + 128 * t + 128],
                                    XN[:, t, 128 * k:128 * k + 128], M.ID[:])
            m.then_inc(M.mix.turned, 1)
        e.wait_ge(M.mix.tm, 3 * KT)
        e.wait_ge(M.small2, 64)
        for t in range(NT):
            for k in range(KT):
                e.matmul(PS[:, 0, NL * t:NL * t + NL], M.XT2[:, k, 128 * t:128 * t + 128], M.WR[:, k, :],
                         start=k == 0, stop=False)
            m = e.matmul(PS[:, 0, NL * t:NL * t + NL], M.ONES[0:1, :], M.BR[0:1, :], start=False, stop=True)
        m.then_inc(s.lg_full, 1)
        e.wait_ge(s.sel, 1)
        EM = M.EM.rearrange("p (t n) -> p t n", t=NT)
        for t in range(NT):
            out = PS[:, 1, 32 * t:32 * t + 32]
            e.matmul(out, M.UPPER[:], EM[:, t], start=True, stop=t == 0)
            if t:
                e.matmul(out, M.ONES[:], EM[:, 0], start=False, stop=True)
        for t in range(NT):
            m = e.matmul(PS[0:1, 1, 64:96], M.ONES[:, 0:1], EM[:, t], start=t == 0, stop=t == 1)
        m.then_inc(s.rk_full, 1)
        e.wait_ge(M.mix.gb_done, 4)
        pe1()
        other_rounds(e, pe2)

    return sync, act, pool, dve, pe


def program(nc, A, out):
    with ExitStack() as c:
        M = Names()

        def sb(name, shape, dtype=f32):
            return c.enter_context(nc.sbuf_tensor(name, shape, dtype))

        def sem(name):
            return c.enter_context(nc.semaphore(name))

        def sems(prefix, names):
            return [sem(prefix + n) for n in names.split()]

        def for_each(n_buffers, prefix, names):
            return [[sem(f"{prefix}{n}{b}") for b in range(n_buffers)] for n in names.split()]

        M.X = sb("X", [128, NT, D])
        M.ID = sb("ID", [128, 128])
        M.GC = sb("GC", [128, N_GC])
        M.XH, M.XL = sb("XH", [128, KT, T], f32r), sb("XL", [128, KT, T], f32r)
        M.RAW = sb("RAW", [128, 2, SLOT])
        M.HI, M.LO = sb("HI", [128, 2, SLOT], f32r), sb("LO", [128, 2, SLOT], f32r)
        M.R = sb("R", [128, 11776])
        M.MASK = sb("MASK", [128, N_MASK])
        M.ROPE_A, M.ROPE_B = sb("ROPE_A", [128, NT, 2, 2, AD]), sb("ROPE_B", [128, NT, 2, B_QK + B_ROPE])
        M.SS, M.RS, M.HF = sb("SS", [128, NT]), sb("RS", [128, NT]), sb("HF", [128, 24])
        M.HG, M.FREQ = sb("HG", [128, 320]), sb("FREQ", [128, 48])
        M.POS, M.POSF = sb("POS", [128, NT], i32), sb("POSF", [128, NT])
        M.SSH, M.RSH, M.SSB, M.RSB = sb("SSH", [128, 24]), sb("RSH", [128, 24]), sb("SSB", [128, 4]), sb("RSB", [128, 4])
        M.SS4, M.RS4 = M.SSB, M.RSB
        stats = sb("STATS", [128, 12])
        M.NM, M.SM, M.RC = ([stats[:, 4 * n + b:4 * n + b + 1] for b in range(4)] for n in range(3))
        M.HH, M.HL = sb("HH", [128, 2, T], f32r), sb("HL", [128, 2, T], f32r)
        M.FLAG = sb("FLAG", [1, 1], i32)

        ARENA = 12544
        arena = sb("ARENA", [128, ARENA])
        end = [0]

        def carve(*shape, at=None):
            n = math.prod(shape)
            start = end[0] if at is None else at
            end[0] = start + n
            assert end[0] <= ARENA
            ap = arena[:, start:start + n]
            if len(shape) == 2:
                return ap.rearrange("p (a b) -> p a b", a=shape[0])
            if len(shape) == 3:
                return ap.rearrange("p (a b c) -> p a b c", a=shape[0], b=shape[1])
            if len(shape) == 4:
                return ap.rearrange("p (a b c d) -> p a b c d", a=shape[0], b=shape[1], c=shape[2])
            return ap

        M.WF = carve(2, FH, at=11268)
        M.MC, M.CRAW, M.CS = carve(96), carve(KT, 2), carve(KT, 2)
        M.MSC, M.SH2, M.ONES = carve(3, KT), carve(KT), carve(128)
        M.WR, M.BR = carve(KT, N_GROUPS + EXPERTS), carve(N_GROUPS + EXPERTS)
        M.DFT = M.MASK[:, 0:1280]
        M.UPPER, M.IOTA, M.DESC = M.MASK[:, 1280:1408], M.MASK[:, 1408:1472], M.MASK[:, 1472:1504]
        M.MR = M.R[:, R_SLOTS * SR:R_SLOTS * SR + 1536].rearrange("p (g n) -> p g n", g=3)
        tm = carve(4, T, at=0)
        M.TM = [tm[:, k] for k in range(4)]
        M.JUNK1 = carve(D)
        M.r_ANG, M.r_TURNS, M.r_CS = carve(NT, 48), carve(2, NT, 48), carve(2, NT, 48)
        M.QT0, M.KT0, M.V0 = carve(4, T, at=0), carve(4, 2 * T), carve(4, 512)
        M.FT, M.BT, M.CT0, M.HT0 = carve(2, T), carve(2, T), carve(2, T), carve(2, T)
        M.XN, M.CX = carve(NT, D), carve(NT, D)
        M.mix_XN = M.XN
        M.mix_OT = carve(KT, T, at=7168)
        M.n_SC = [carve(512), carve(512), carve(512, at=5120), carve(512)]
        end[0] = 10240
        M.n_PT = [carve(512), carve(512)]
        M.FA, M.FOT, M.CHP = carve(2, 512, at=9216), carve(512), carve(2, T + 2)
        M.G2B, M.G1B = carve(D, at=0), carve(D)
        M.TMPX = [carve(512), carve(512)]
        beside = [M.RAW[:, n // 2, SR + 512 * (n % 2):SR + 512 * (n % 2) + 512] for n in range(4)]
        M.BIAS = beside
        M.BIASZ = M.RAW[:, :, SR:].rearrange("p a (b n) -> p a b n", b=2)[:, :, :, T:]
        M.moe_XN = carve(NT, D, at=1024)
        M.XT2 = carve(KT, T)
        M.YACC = carve(NT, D, at=3072)
        M.XG, M.SGM, M.HM, M.HT, M.CM, M.YS = carve(KT, 128), carve(512), carve(512), carve(512), carve(T), carve(D)
        M.m_JUNK = M.YS
        M.OH, M.OHC = carve(NT, 128), carve(NT, 128)
        M.NFR = carve(D)
        M.KEY, M.CW = carve(NT, KEYS), carve(NT, KEYS)
        M.LG = carve(NT * (N_GROUPS + EXPERTS), at=5120)
        M.GE, M.OHG, M.T4 = carve(8), carve(8), carve(8)
        M.EM, M.T32, M.OH1, M.OH2 = carve(64), carve(64), carve(64), carve(64)
        M.MX, M.PK, M.ED, M.GW, M.P1, M.P2 = carve(6), carve(2), carve(2), carve(2), carve(2), carve(2)
        M.CNT = carve(1)[0:1]
        xn = carve(NT, D, at=0)
        ot = carve(KT, T, at=0)
        base = end[0]
        junk, M.SG, M.H = carve(D), carve(2, T), carve(2, T)
        M.SC, M.PT = [carve(384, at=base), carve(768)], [carve(384), carve(384)]
        M.b_SC = [carve(128, at=base), carve(T), carve(128), carve(T)]
        M.b_PT = [carve(T), carve(T)]
        base = base + 384 + 768 + 384 + 384
        end[0] = base
        M.a_QK, M.a_SQ, M.a_QR = carve(NT, 2, AW), carve(2, AW), carve(NT, 2, AW)
        M.a_QT, M.a_KT, M.a_V = carve(2, GROUPS, T), carve(2, GROUPS, T), carve(2, NT, AW)
        M.b_C, M.b_CT = carve(NT, B_IN, at=base), carve(5, T)
        b_QK, M.b_SQ, M.b_QR = carve(NT, 4, B_QK), carve(4, B_QK), carve(NT, 4, B_QK)
        M.b_QKT, M.b_V, M.b_WO = carve(2, 4, T)[0:B_QK], carve(2, NT, 2, B_V), carve(D)
        M.b_VN = carve(NT, 2, B_V)
        M.b_QK = [b_QK, M.b_C[:, :, 0:4 * B_QK].rearrange("p t (h d) -> p t h d", h=4)]
        M.PS = c.enter_context(nc.psum_tensor("PS", [128, 8, 512], f32))
        M.TRB = M.PTB = [M.PS[:, 6, :], M.PS[:, 7, :]]
        M.OB = M.PS[:, 5, 0:T]

        (M.x_ready, M.squared, M.turned, M.xh_done, M.xl_done, M.rstd, M.xn_done, M.small_in) = \
            sems("", "x_ready squared turned xh_done xl_done rstd xn_done small_in")
        M.small2, M.ones_set, M.mask_in, M.out_written = sems("", "small2 ones_set mask_in out_written")
        M.att = Names()
        (M.att.sc_full, M.att.sc_read, M.att.exp_done, M.att.recip, M.att.p_ready, M.att.pt_full, M.att.pt_done, M.att.pv_done) = \
            sems("t_", "sc_full sc_read exp_done recip p_ready pt_full pt_done pv_done")
        M.att.o_free, = sems("t_", "o_free")
        M.ffn = Names()
        M.ffn.y_done, = sems("f_", "y_done")
        (M.ffn.gu_in, M.ffn.dn_in, M.ffn.gu_hi, M.ffn.gu_lo, M.ffn.dn_hi, M.ffn.dn_lo, M.ffn.gu_used, M.ffn.dn_used) = \
            for_each(2, "f_", "gu_in dn_in gu_hi gu_lo dn_hi dn_lo gu_used dn_used")
        M.ffn.silu, M.ffn.h_done, M.ffn.hh_done, M.ffn.hl_done = for_each(2, "f_", "silu h_done hh_done hl_done")
        M.dil = Names()
        (M.dil.y_done, M.dil.wo_in, M.dil.fb_full, M.dil.fb_free, M.dil.nr, M.dil.rs) = \
            sems("a_", "y_done wo_in fb_full fb_free nr rs")
        M.dil.w_in, M.dil.w_hi, M.dil.w_lo = for_each(2, "a_", "w_in w_hi w_lo")
        M.lat = Names()
        (M.lat.y_done, M.lat.wo_in, M.lat.fb_full, M.lat.fb_free, M.lat.nr, M.lat.rs, M.lat.c_full, M.lat.c_out) = \
            sems("b_", "y_done wo_in fb_full fb_free nr rs c_full c_out")
        M.lat.ct_full, M.lat.ct_done, M.lat.c_rs, M.lat.cn, M.lat.wq_in, M.lat.v_moved = \
            sems("b_", "ct_full ct_done c_rs cn wq_in v_moved")
        M.rope = Names()
        M.rope.ch, M.rope.reduced, M.rope.sines = sems("r_", "ch reduced sines")
        M.ada = Names()
        M.ada.cs, M.ada.mr, M.ada.mt, M.ada.mc = sems("d_", "cs mr mt mc")
        M.ada.r_in, M.ada.r_used = for_each(R_SLOTS, "d_", "r_in r_used")
        M.mix = Names()
        (M.mix.c_in, M.mix.x_in, M.mix.sq, M.mix.rs, M.mix.ch, M.mix.turned, M.mix.tm, M.mix.xh) = \
            sems("m_", "c_in x_in sq rs ch turned tm xh")
        (M.mix.xl, M.mix.fb_full, M.mix.fb_free, M.mix.fo_full, M.mix.fo_done, M.mix.zeroed, M.mix.y_done, M.mix.xu) = \
            sems("m_", "xl fb_full fb_free fo_full fo_done zeroed y_done xu")
        M.mix.gb_full, M.mix.gb_done = sems("m_", "gb_full gb_done")
        M.mix.w_in, M.mix.w_hi, M.mix.w_lo = for_each(2, "m_", "w_in w_hi w_lo")
        M.lat.w_in, M.lat.w_hi, M.lat.w_lo = M.dil.w_in, M.mix.w_hi, M.mix.w_lo
        M.mix.bias_in, = for_each(4, "m_", "bias_in")
        M.moe = Names()
        (M.moe.ge, M.moe.ed, M.moe.ex, M.moe.sel, M.moe.counted, M.moe.rt, M.moe.lg_full, M.moe.rk_full) = \
            sems("e_", "ge ed ex sel counted rt lg_full rk_full")
        M.moe.nf_in, M.moe.fin = sems("e_", "nf_in fin")
        M.steps = Names()
        (M.steps.oh, M.steps.xg_full, M.steps.xg_done, M.steps.silu, M.steps.h_done, M.steps.ht_full, M.steps.ht_done, M.steps.cm_full) = \
            sems("s_", "oh xg_full xg_done silu h_done ht_full ht_done cm_full")
        (M.steps.cm_done, M.steps.ohc, M.steps.y_done, M.steps.sc_full, M.steps.acc) = \
            sems("s_", "cm_done ohc y_done sc_full acc")
        M.steps.w_in, M.steps.used = for_each(6, "s_", "w_in used")
        M.passed = sem("passed")
        M.n_small = 16 * 5

        def after_experts(sp, j):
            if j == 0:
                sp.wait_ge(M.steps.used[5], 2 * PAIR_STEPS)
            else:
                sp.wait_ge(M.mix.w_lo[1], 5)
                for n in range(2, 4):
                    sp.wait_ge(M.att.sc_read, 16)

        def after_ffn(f):
            def wait(sp, j):
                sp.wait_ge(M.ffn.gu_lo[j], 1 + FF_TWICE * (f + 1))
                sp.wait_ge(M.ffn.dn_lo[j], 1 + FF_TWICE * (f + 1))
            return wait

        def after_dilated(sp, j):
            sp.wait_ge(M.dil.w_lo[j], 12)

        def after_latent(sp, j):
            sp.wait_ge(M.lat.fb_full, 6 * PAIRS - 4)

        def nothing():
            pass

        M.XN, M.OT, M.JUNK = M.mix_XN, M.mix_OT, M.JUNK1
        mixer = first_mixer(nc, M, A)
        M.XN = M.moe_XN
        moe = experts(nc, M, A)
        M.XN, M.OT, M.JUNK = xn, ot, junk
        rope_act, rope_dve = rope_tables(nc, M)
        phases = []
        n_ffn = 0
        before = after_experts
        for n, kind in enumerate(("ffn", "dilated", "ffn", "ffn", "latent", "ffn")):
            if kind == "ffn":
                sync, act, dve, pe, high, low = ffn(nc, M, n, n_ffn, A["ffn_w_in"][n_ffn // 2, n_ffn % 2], A["ffn_w_out"][n_ffn // 2, n_ffn % 2],
                                         before)
                pool = nothing
                before = after_ffn(n_ffn)
                n_ffn += 1
            elif kind == "dilated":
                sync, act, pool, dve, pe, high, low = dilated(nc, M, n, A["a_w_in"], A["a_w_out"], before)
                before = after_dilated
            else:
                sync, act, pool, dve, pe, high, low = latent(nc, M, n, A["b_w_in"], A["b_w_q_up"], A["b_w_kv_up"], A["b_w_out"], before)
                before = after_latent
            n_act, n_pool, n_dve, n_pe = norm_and_transpose(nc, M, n, KT * n, high, low)
            phases.append((sync, n_act, act, n_pool, pool, n_dve, dve, n_pe, pe))

        block = c.enter_context(nc.Block())

        @block.sync
        def _(sp):
            mixer[0]()
            moe[0]()
            for n, (sync, *_) in enumerate(phases):
                sync()
                if n == 0:
                    sp.wait_ge(M.x_ready, 4)
                    sp.dma_start(M.MASK[:], A["mask"]).then_inc(M.mask_in, 16)
            sp.wait_ge(M.x_ready, 28)
            sp.dma_start(out.rearrange("(t p) n -> p t n", p=128), M.X[:]).then_inc(M.out_written, 16)
            sp.wait_ge(M.out_written, 16)

        @block.scalar
        def _(a):
            for to, what in ((M.POS, A["positions"]), (M.FREQ, A["freq"]), (M.HG, A["head_gains"]), (M.ID, A["identity"]), (M.GC, A["gains"])):
                a.dma_start(to[:], what).then_inc(M.small_in, 16)
            a.dma_start(M.X[:], A["x"].rearrange("(t p) n -> p t n", p=128)).then_inc(M.mix.x_in, 16)
            a.dma_start(M.CX, A["ctx"].rearrange("(t p) n -> p t n", p=128)).then_inc(M.mix.x_in, 16)
            a.dma_start(M.MASK[:, 0:1504], A["constants"]).then_inc(M.small2, 16)
            a.dma_start(M.WF, A["w_fourier"].rearrange("(k p) n -> p k n", p=128)).then_inc(M.small2, 16)
            a.dma_start(M.WR, A["w_router"].rearrange("(k p) n -> p k n", p=128)).then_inc(M.small2, 16)
            a.dma_start(M.BR[0:1], A["b_router"]).then_inc(M.small2, 16)
            rope_act()
            mixer[1]()
            moe[1]()
            for _, norm, act, *_ in phases:
                norm()
                act()

        @block.gpsimd
        def _(p):
            p.memset(M.HF[:], -0.5).then_inc(M.ones_set, 1)
            p.memset(M.ONES, 1.0).then_inc(M.ones_set, 1)
            p.memset(M.MR, 0.0).then_inc(M.ones_set, 1)
            p.wait_ge(M.ones_set, 3)
            mixer[2]()
            moe[2]()
            for _, _, _, norm, pool, *_ in phases:
                norm()
                pool()

        @block.vector
        def _(v):
            for j in range(2):
                v.sem_inc(M.ffn.h_done[j], 1)
                v.sem_inc(M.ffn.gu_lo[j], 1)
                v.sem_inc(M.ffn.dn_lo[j], 1)
            rope_dve()
            mixer[3]()
            moe[3]()
            for n, (_, _, _, _, _, norm, dve, _, _) in enumerate(phases):
                norm()
                if n == 1:
                    v.wait_ge(M.mask_in, 16)
                dve()

        @block.tensor
        def _(e):
            for j in range(2):
                e.sem_inc(M.ffn.gu_used[j], 1)
                e.sem_inc(M.ffn.dn_used[j], 1)
            e.wait_ge(M.small_in, M.n_small)
            mixer[4]()
            moe[4]()
            for *_, norm, pe in phases:
                norm()
                pe()


def kernel(**inputs):
    import concourse.bacc as bacc
    from concourse.bass_utils import run_bass_kernel_spmd

    given = {name: np.asarray(value) for name, value in inputs.items()}

    def columns(vector):
        return vector.reshape(-1, 128).T

    def on_all(row):
        return np.broadcast_to(row, (128, row.shape[-1]))

    def two(name):
        return given[name].reshape(given[name].shape[1:])

    zero_or_far = lambda ok: np.where(ok, 0.0, FAR).astype(np.float32)
    q, k = np.arange(T)[:, None], np.arange(T)[None, :]
    gap = q - k
    bands = [zero_or_far((gap >= 0) & (gap % dilation == 0) & (gap <= window)) for window, dilation in ((128, 1), (512, 4), (2048, 16))]
    causal = zero_or_far(gap >= 0)
    mask = np.concatenate([b[:128, :128] for b in bands] + [b[128:] for b in bands] + [causal[:128, :128], causal[128:]], axis=1)
    freq = np.concatenate([10000.0 ** (-np.arange(32) * 2.0 / 64), 10000.0 ** (-np.arange(16) * 2.0 / 32)])
    n64, n256 = np.arange(64), np.arange(T)
    angle64 = 2 * np.pi * ((n64[:, None] * n64[None, :]) % 64) / 64
    angle256 = 2 * np.pi * ((n256[:, None] * n256[None, :]) % T) / T
    both = lambda m: np.kron(np.eye(2), m)
    tiles = lambda m: m.reshape(NT, 128, T).transpose(1, 0, 2).reshape(128, NT * T)
    norm = 1 / math.sqrt(64 * T)
    constants = np.concatenate([both(np.cos(angle64)), both(np.sin(angle64)), tiles(np.cos(angle256) * norm),
                                tiles(-np.sin(angle256) * norm), np.triu(np.ones((128, 128)), 1),
                                on_all(np.arange(64.0)[None]), on_all(np.arange(32.0, 0.0, -1.0)[None])], axis=1)
    row, col = n256 // 64, n256 % 64
    start = np.clip(col - 8, 0, 64 - 16)[:, None]
    inside = (col[None, :] >= start) & (col[None, :] < start + 16)
    bias = two("rpb")[:, row[None, :] - row[:, None] + 7, np.clip(col[None, :] - col[:, None] + 15, 0, 30)]
    bias = np.where(inside[None], bias, np.float32(FAR))

    A = dict(
        x=given["x"][0], ctx=given["ctx"][0],
        conditions=np.stack([given["c"][0], given["c_ctx"]], axis=-1).reshape(KT, 128, 2).transpose(1, 0, 2),
        w_ada=two("w_ada"), b_ada=given["b_ada"], w_in=two("w_in"), w_fourier=two("w_fourier"), w_out=two("w_out"),
        w_router=np.concatenate([two("w_rg"), two("w_re")], axis=1),
        b_router=np.concatenate([given["b_rg"], given["b_re"]], axis=1),
        w_gate=two("w_gate"), w_up=two("w_up"), w_down=two("w_down"), norm_final=on_all(given["norm_final"][None]),
        bias=bias, positions=given["positions_2"].reshape(NT, 128).T, freq=on_all(freq.astype(np.float32)[None]),
        head_gains=on_all(np.concatenate([given[n][0] for n in ("a_q_gain_2", "b_q_gain_2", "a_k_gain_2", "b_k_gain_2")])[None]),
        gains=np.concatenate([columns(given[n]) for n in ("norm_gains_2", "norm1", "norm2", "b_q_a_gain_2", "b_kv_a_gain_2",
                                                          "w_conv")], axis=1),
        identity=np.eye(128, dtype=np.float32), constants=constants.astype(np.float32), mask=mask,
        ffn_w_in=given["ffn_w_in_2"], ffn_w_out=given["ffn_w_out_2"], a_w_in=two("a_w_in_2"), a_w_out=two("a_w_out_2"),
        b_w_in=two("b_w_in_2"), b_w_q_up=two("b_w_q_up_2"), b_w_kv_up=two("b_w_kv_up_2"), b_w_out=two("b_w_out_2"),
    )
    nc = bacc.Bacc("TRN2", target_bir_lowering=False, num_devices=1)
    arrays = {name: np.ascontiguousarray(value) for name, value in A.items()}
    handles = {name: nc.dram_tensor(name, value.shape, mybir.dt.from_np(value.dtype), kind="ExternalInput").ap()
               for name, value in arrays.items()}
    out = nc.dram_tensor("out_0_dram", (T, D), f32, kind="ExternalOutput").ap()
    program(nc, handles, out)
    result = run_bass_kernel_spmd(nc, [arrays], core_ids=[0])
    return result.results[0]["out_0_dram"].reshape(1, T, D)
```
